# Optimizing a Trainium2 kernel written in Bass

```python
import jax, jax.numpy as jnp
from jax import lax
import numpy as np
import math

D_MODEL = 1024
BATCH = 1
SEQ = 512
DEPTH = 1

N_Q_HEADS = 16
N_KV_HEADS = 4
HEAD_DIM = 64
WINDOW = 128
ATTN_BLOCK = 128
ROPE_THETA = 500000.0
ROPE_DIM = HEAD_DIM // 4
HGRN_HEADS = 8
HGRN_DK = 128
HGRN_DV = 128
HGRN_CHUNK = 64
D_FF = 2816
ATTN_WIDTH = N_Q_HEADS * HEAD_DIM
KV_WIDTH = N_KV_HEADS * HEAD_DIM
HGRN_KWIDTH = HGRN_HEADS * HGRN_DK
HGRN_VWIDTH = HGRN_HEADS * HGRN_DV
IN_WIDTHS = (ATTN_WIDTH, KV_WIDTH, KV_WIDTH, HGRN_KWIDTH, HGRN_KWIDTH, HGRN_VWIDTH, HGRN_VWIDTH, D_MODEL, D_MODEL)
D_IN = sum(IN_WIDTHS)
DEEPNORM_ALPHA = (2 * DEPTH) ** 0.25
DEEPNORM_BETA = (8 * DEPTH) ** -0.25
LN_EPS = 1e-5
RMS_EPS = 1e-6
NEG_INF = -1e30


def layer_norm(x, g, b):
    xf = x.astype(jnp.float32)
    mu = jnp.mean(xf, axis=-1, keepdims=True)
    var = jnp.mean(jnp.square(xf - mu), axis=-1, keepdims=True)
    y = (xf - mu) * lax.rsqrt(var + LN_EPS) * g.astype(jnp.float32) + b.astype(jnp.float32)
    return y.astype(x.dtype)

def swiglu(x, w1, w3, w2):
    return (jax.nn.silu(x @ w1) * (x @ w3)) @ w2

def rope_tables(seq_len):
    pos = jnp.arange(seq_len, dtype=jnp.float32)
    inv_freq = ROPE_THETA ** (-jnp.arange(0, ROPE_DIM, 2, dtype=jnp.float32) / ROPE_DIM)
    ang = pos[:, None] * inv_freq[None, :]
    return jnp.cos(ang)[None, :, None, :], jnp.sin(ang)[None, :, None, :]

def partial_rope(t, cos, sin):
    tf = t.astype(jnp.float32)
    half = ROPE_DIM // 2
    t1, t2, rest = tf[..., :half], tf[..., half:ROPE_DIM], tf[..., ROPE_DIM:]
    rot = jnp.concatenate([t1 * cos - t2 * sin, t2 * cos + t1 * sin, rest], axis=-1)
    return rot.astype(t.dtype)

def sliding_window_attention(q, k, v, sinks):
    B, S = q.shape[0], q.shape[1]
    nb = S // ATTN_BLOCK
    grp = N_Q_HEADS // N_KV_HEADS
    qb = q.reshape(B, nb, ATTN_BLOCK, N_KV_HEADS, grp, HEAD_DIM)

    def band(t):
        tp = jnp.pad(t, ((0, 0), (ATTN_BLOCK, 0), (0, 0), (0, 0)))
        tp = tp.reshape(B, nb + 1, ATTN_BLOCK, N_KV_HEADS, HEAD_DIM)
        return jnp.concatenate([tp[:, :-1], tp[:, 1:]], axis=2)

    kb, vb = band(k), band(v)
    scores = jnp.einsum('bnqkgd,bnskd->bnkgqs', qb, kb).astype(jnp.float32) * (HEAD_DIM ** -0.5)
    qi = jnp.arange(ATTN_BLOCK)[:, None]
    kj = jnp.arange(2 * ATTN_BLOCK)[None, :]
    blk = jnp.arange(nb)[:, None, None]
    dist = qi + ATTN_BLOCK - kj
    mask = (dist >= 0) & (dist < WINDOW) & (blk * ATTN_BLOCK + kj - ATTN_BLOCK >= 0)
    scores = jnp.where(mask[None, :, None, None], scores, NEG_INF)
    sink = sinks.astype(jnp.float32).reshape(1, 1, N_KV_HEADS, grp, 1, 1)
    m = jnp.maximum(jnp.max(scores, axis=-1, keepdims=True), sink)
    p = jnp.exp(scores - m)
    denom = jnp.sum(p, axis=-1, keepdims=True) + jnp.exp(sink - m)
    probs = (p / denom).astype(v.dtype)
    out = jnp.einsum('bnkgqs,bnskd->bnqkgd', probs, vb)
    return out.reshape(B, S, ATTN_WIDTH)

def hgrn2_recurrence(q, f_logit, v, lb):
    B, S = q.shape[0], q.shape[1]
    nc = S // HGRN_CHUNK
    lb = lb.reshape(HGRN_HEADS, HGRN_DK)
    f = lb + (1.0 - lb) * jax.nn.sigmoid(f_logit.astype(jnp.float32))
    k = 1.0 - f

    def chunks(t):
        return t.reshape(B, nc, HGRN_CHUNK, HGRN_HEADS, t.shape[-1]).transpose(0, 3, 1, 2, 4)

    qc, kc, vc = chunks(q.astype(jnp.float32)), chunks(k), chunks(v.astype(jnp.float32))
    gc = jnp.cumsum(chunks(jnp.log(f)), axis=3)
    g_last = gc[:, :, :, -1:, :]
    q_dec = qc * jnp.exp(gc)
    k_inv = kc * jnp.exp(-gc)
    k_end = kc * jnp.exp(g_last - gc)
    causal = jnp.tril(jnp.ones((HGRN_CHUNK, HGRN_CHUNK), dtype=bool))
    scores = jnp.where(causal, jnp.einsum('bhntd,bhnsd->bhnts', q_dec, k_inv), 0.0)
    o_intra = jnp.einsum('bhnts,bhnse->bhnte', scores, vc)
    upd = jnp.einsum('bhnsd,bhnse->bhnde', k_end, vc)
    decay = jnp.exp(g_last[:, :, :, 0, :])

    def step(state, inp):
        a_n, u_n = inp
        return state * a_n[..., None] + u_n, state

    s0 = jnp.zeros((B, HGRN_HEADS, HGRN_DK, HGRN_DV), jnp.float32)
    _, s_start = lax.scan(step, s0, (jnp.moveaxis(decay, 2, 0), jnp.moveaxis(upd, 2, 0)))
    s_start = jnp.moveaxis(s_start, 0, 2)
    o = o_intra + jnp.einsum('bhntd,bhnde->bhnte', q_dec, s_start)
    return o.transpose(0, 2, 3, 1, 4).reshape(B, S, HGRN_HEADS, HGRN_DV)

def token_mixer(h, w_in, b_in, sinks, lb, norm_g, w_pa, w_ph, w_out, cos, sin):
    B, S = h.shape[0], h.shape[1]
    proj = h @ w_in + b_in
    splits = np.cumsum(IN_WIDTHS)[:-1].tolist()
    q_a, k_a, v_a, f_h, q_h, i_h, og_h, gate_a, gate_h = jnp.split(proj, splits, axis=-1)
    q_a = partial_rope(q_a.reshape(B, S, N_Q_HEADS, HEAD_DIM), cos, sin)
    k_a = partial_rope(k_a.reshape(B, S, N_KV_HEADS, HEAD_DIM), cos, sin)
    v_a = v_a.reshape(B, S, N_KV_HEADS, HEAD_DIM)
    y_attn = sliding_window_attention(q_a, k_a, v_a, sinks)
    q_h = jax.nn.silu(q_h).reshape(B, S, HGRN_HEADS, HGRN_DK)
    o_h = hgrn2_recurrence(q_h, f_h.reshape(B, S, HGRN_HEADS, HGRN_DK),
                           i_h.reshape(B, S, HGRN_HEADS, HGRN_DV), lb)
    o_h = o_h * lax.rsqrt(jnp.mean(jnp.square(o_h), axis=-1, keepdims=True) + RMS_EPS) * norm_g.astype(jnp.float32)
    y_hgrn = o_h.reshape(B, S, HGRN_VWIDTH).astype(h.dtype) * jax.nn.silu(og_h)
    merged = jax.nn.sigmoid(gate_a) * (y_attn @ w_pa) + jax.nn.sigmoid(gate_h) * (y_hgrn @ w_ph)
    return merged @ w_out

def first_inputs(seed: int = 0) -> dict:
    key = jax.random.key(seed)
    ks = jax.random.split(key, 24)

    def nrm(k, shape, scale):
        return jax.random.normal(k, shape, jnp.float32) * scale

    D = D_MODEL
    return {
        'x': nrm(ks[0], (BATCH, SEQ, D), 1.0),
        'ln1_g': 1.0 + nrm(ks[1], (DEPTH, D), 0.02),
        'ln1_b': nrm(ks[2], (DEPTH, D), 0.02),
        'ffn1_w1': nrm(ks[3], (DEPTH, D, D_FF), D ** -0.5),
        'ffn1_w3': nrm(ks[4], (DEPTH, D, D_FF), D ** -0.5),
        'ffn1_w2': nrm(ks[5], (DEPTH, D_FF, D), D_FF ** -0.5 * DEEPNORM_BETA),
        'ln2_g': 1.0 + nrm(ks[6], (DEPTH, D), 0.02),
        'ln2_b': nrm(ks[7], (DEPTH, D), 0.02),
        'w_in': nrm(ks[8], (DEPTH, D, D_IN), D ** -0.5),
        'b_in': nrm(ks[9], (DEPTH, D_IN), 0.02),
        'attn_sinks': nrm(ks[10], (DEPTH, N_Q_HEADS), 0.5),
        'hgrn_lb_logits': nrm(ks[11], (DEPTH + 1, HGRN_KWIDTH), 0.1),
        'hgrn_norm_g': 1.0 + nrm(ks[12], (DEPTH, HGRN_DV), 0.02),
        'w_proj_attn': nrm(ks[13], (DEPTH, ATTN_WIDTH, D), ATTN_WIDTH ** -0.5 * DEEPNORM_BETA),
        'w_proj_hgrn': nrm(ks[14], (DEPTH, HGRN_VWIDTH, D), HGRN_VWIDTH ** -0.5 * DEEPNORM_BETA),
        'w_out': nrm(ks[15], (DEPTH, D, D), D ** -0.5 * DEEPNORM_BETA),
        'ln3_g': 1.0 + nrm(ks[16], (DEPTH, D), 0.02),
        'ln3_b': nrm(ks[17], (DEPTH, D), 0.02),
        'ffn2_w1': nrm(ks[18], (DEPTH, D, D_FF), D ** -0.5),
        'ffn2_w3': nrm(ks[19], (DEPTH, D, D_FF), D ** -0.5),
        'ffn2_w2': nrm(ks[20], (DEPTH, D_FF, D), D_FF ** -0.5 * DEEPNORM_BETA),
    }

def first_block(x, ln1_g, ln1_b, ffn1_w1, ffn1_w3, ffn1_w2, ln2_g, ln2_b, w_in, b_in,
              attn_sinks, hgrn_lb_logits, hgrn_norm_g, w_proj_attn, w_proj_hgrn, w_out,
              ln3_g, ln3_b, ffn2_w1, ffn2_w3, ffn2_w2):
    cos, sin = rope_tables(x.shape[1])
    lb_all = jnp.cumsum(jax.nn.softmax(hgrn_lb_logits.astype(jnp.float32), axis=0), axis=0)
    for l in range(DEPTH):
        x = layer_norm(DEEPNORM_ALPHA * x + 0.5 * swiglu(x, ffn1_w1[l], ffn1_w3[l], ffn1_w2[l]),
                       ln1_g[l], ln1_b[l])
        mix = token_mixer(x, w_in[l], b_in[l], attn_sinks[l], lb_all[l], hgrn_norm_g[l],
                          w_proj_attn[l], w_proj_hgrn[l], w_out[l], cos, sin)
        x = layer_norm(DEEPNORM_ALPHA * x + mix, ln2_g[l], ln2_b[l])
        x = layer_norm(DEEPNORM_ALPHA * x + 0.5 * swiglu(x, ffn2_w1[l], ffn2_w3[l], ffn2_w2[l]),
                       ln3_g[l], ln3_b[l])
    return x


_first_inputs = first_inputs


def first_inputs(seed=0):
    import zlib

    import numpy as np

    out = dict(_first_inputs(seed))
    spreads = {}
    factors = {'ln2_g': 2.712,
     'ln2_b': 2.84,
     'b_in': 8.0,
     'attn_sinks': 8.0,
     'hgrn_lb_logits': 8.0,
     'hgrn_norm_g': 8.0,
     'ln3_g': 2.858,
     'ln3_b': 2.874}
    for name, (base, spread) in spreads.items():
        noise = np.random.default_rng([zlib.crc32(name.encode()), seed]).standard_normal(out[name].shape)
        drawn = base * np.exp(spread * noise) if base else spread * noise
        out[name] = __import__('jax').numpy.asarray(drawn.astype(out[name].dtype))
    for name, factor in factors.items():
        out[name] = (out[name] * factor).astype(out[name].dtype)
    return out


_narrow_inputs = first_inputs


def first_inputs(seed=0):

    out = dict(_narrow_inputs(seed))
    wider = {'attn_sinks': 5.34, 'hgrn_norm_g': 5.25, 'ln3_g': 3.22, 'ln3_b': 3.22}
    for name, times in wider.items():
        mean = out[name].mean()
        out[name] = (mean + times * (out[name] - mean)).astype(out[name].dtype)
    return out


MIX_WIDTH = D_MODEL // 2
N_BRANCH = 4
EPS = 1e-6

RWKV_HEAD_DIM = 64
RWKV_HEADS = MIX_WIDTH // RWKV_HEAD_DIM
RWKV_DECAY_LORA = 64
RWKV_A_LORA = 64
RWKV_G_LORA = 128
RWKV_DECAY_SCALE = 0.6065306597
RWKV_GN_EPS = 64e-5
GLA_HEADS = 4
GLA_DK = MIX_WIDTH // 2
GLA_DV = MIX_WIDTH
GLA_GATE_LORA = 16
GLA_TAU = 16.0
GLA_CHUNK = 16
MLSTM_HEADS = 4
MLSTM_DQK = MIX_WIDTH // 2
MLSTM_DV = MIX_WIDTH
MLSTM_CONV = 4
MLSTM_CHUNK = 64
SSD_HEADS = 8
SSD_HEAD_DIM = MIX_WIDTH // SSD_HEADS
SSD_GROUPS = 2
SSD_HPG = SSD_HEADS // SSD_GROUPS
SSD_STATE = 128
SSD_CONV = 4
SSD_CHUNK = 128
SSD_CONV_DIM = MIX_WIDTH + 2 * SSD_GROUPS * SSD_STATE
FFN_CONV = 3

RWKV_IN = 3 * MIX_WIDTH + RWKV_DECAY_LORA + RWKV_A_LORA + RWKV_G_LORA
GLA_IN = 2 * GLA_DK + 2 * GLA_DV + GLA_GATE_LORA
MLSTM_IN = 2 * MLSTM_DQK + 2 * MLSTM_DV + 2 * MLSTM_HEADS
SSD_IN = MIX_WIDTH + SSD_CONV_DIM + SSD_HEADS
GATE_IN = N_BRANCH * D_MODEL
MIXER_IN_SIZES = (RWKV_IN, GLA_IN, MLSTM_IN, SSD_IN, GATE_IN)
D_IN_2 = RWKV_IN + GLA_IN + MLSTM_IN + SSD_IN + GATE_IN


def _split(a, sizes):
    idx = np.cumsum(np.array(sizes))[:-1].tolist()
    return jnp.split(a, idx, axis=-1)

def rms_norm(x, g):
    xf = x.astype(jnp.float32)
    return xf * lax.rsqrt(jnp.mean(xf * xf, axis=-1, keepdims=True) + EPS) * g

def head_rms_norm(y, g):
    y = y.astype(jnp.float32)
    return y * lax.rsqrt(jnp.mean(y * y, axis=-1, keepdims=True) + EPS) * g

def head_group_norm(y, g, b, eps):
    y = y.astype(jnp.float32)
    yc = y - jnp.mean(y, axis=-1, keepdims=True)
    return yc * lax.rsqrt(jnp.mean(yc * yc, axis=-1, keepdims=True) + eps) * g + b

def causal_dwconv(x, w, b):
    k, c = w.shape
    y = lax.conv_general_dilated(x, w[:, None, :].astype(x.dtype), window_strides=(1,),
                                 padding=((k - 1, 0),), dimension_numbers=('NWC', 'WIO', 'NWC'),
                                 feature_group_count=c)
    return y + b

def token_shift(f, mu):
    prev = jnp.pad(f, ((0, 0), (1, 0), (0, 0)))[:, :-1]
    return f + mu * (prev - f)

def to_chunks(a, size):
    bsz, t = a.shape[:2]
    return jnp.moveaxis(a.reshape((bsz, t // size, size) + a.shape[2:]), 1, 0)

def from_chunks(a):
    nc, bsz, size = a.shape[:3]
    return jnp.moveaxis(a, 0, 1).reshape((bsz, nc * size) + a.shape[3:])

def causal_mask(size):
    return jnp.tril(jnp.ones((size, size), dtype=bool))

def rwkv7_mix(fa, mu, w0, w_up, a0, a_up, g_up, k_k, k_a, r_k, gn_g, gn_b):
    bsz, t, _ = fa.shape
    fa = token_shift(fa.astype(jnp.float32), mu)
    r, k, v, w_lo, a_lo, g_lo = _split(fa, (MIX_WIDTH, MIX_WIDTH, MIX_WIDTH, RWKV_DECAY_LORA, RWKV_A_LORA, RWKV_G_LORA))
    heads = lambda z: z.reshape(bsz, t, RWKV_HEADS, RWKV_HEAD_DIM)
    log_decay = -RWKV_DECAY_SCALE * jax.nn.sigmoid(w0 + jnp.tanh(w_lo) @ w_up)
    a = jax.nn.sigmoid(a0 + a_lo @ a_up)
    g = jax.nn.sigmoid(g_lo) @ g_up
    kk = heads(k * k_k)
    kk = kk / jnp.maximum(jnp.sqrt(jnp.sum(kk * kk, axis=-1, keepdims=True)), 1e-12)
    k = k * (1.0 + (a - 1.0) * k_a)
    r, k, v, a, decay = heads(r), heads(k), heads(v), heads(a), jnp.exp(heads(log_decay))

    def step(s, inp):
        r_t, w_t, k_t, v_t, kk_t, a_t = inp
        sa = jnp.einsum('bhvk,bhk->bhv', s, -kk_t)
        s = (s * w_t[:, :, None, :] + sa[..., None] * (kk_t * a_t)[:, :, None, :]
             + v_t[..., None] * k_t[:, :, None, :])
        return s, jnp.einsum('bhvk,bhk->bhv', s, r_t)

    time_major = lambda z: jnp.moveaxis(z, 1, 0)
    s0 = jnp.zeros((bsz, RWKV_HEADS, RWKV_HEAD_DIM, RWKV_HEAD_DIM), jnp.float32)
    _, y = lax.scan(step, s0, tuple(time_major(z) for z in (r, decay, k, v, kk, a)))
    y = jnp.moveaxis(y, 0, 1)
    y = head_group_norm(y, gn_g.reshape(RWKV_HEADS, RWKV_HEAD_DIM), gn_b.reshape(RWKV_HEADS, RWKV_HEAD_DIM), RWKV_GN_EPS)
    y = y + jnp.sum(r * k * r_k, axis=-1, keepdims=True) * v
    return y.reshape(bsz, t, MIX_WIDTH) * g

def gla_mix(fb, f_up, f_bias, norm_g):
    bsz, t, _ = fb.shape
    dk, dv = GLA_DK // GLA_HEADS, GLA_DV // GLA_HEADS
    q, k, v, f_lo, og = _split(fb.astype(jnp.float32), (GLA_DK, GLA_DK, GLA_DV, GLA_GATE_LORA, GLA_DV))
    hk = lambda z: z.reshape(bsz, t, GLA_HEADS, dk)
    log_alpha = hk(jax.nn.log_sigmoid(f_lo @ f_up + f_bias) / GLA_TAU)
    q = hk(q) * dk ** -0.5
    k = hk(k)
    v = v.reshape(bsz, t, GLA_HEADS, dv)
    mask = causal_mask(GLA_CHUNK)

    def step(s, inp):
        q_c, k_c, v_c, la_c = inp
        b = jnp.cumsum(la_c, axis=1)
        b_last = b[:, -1]
        qd = q_c * jnp.exp(b)
        kd = k_c * jnp.exp(-b)
        att = jnp.where(mask, jnp.einsum('blhd,bshd->bhls', qd, kd), 0.0)
        o = jnp.einsum('bhls,bshe->blhe', att, v_c) + jnp.einsum('blhd,bhde->blhe', qd, s)
        s = jnp.exp(b_last)[..., None] * s + jnp.einsum('bshd,bshe->bhde', k_c * jnp.exp(b_last[:, None] - b), v_c)
        return s, o

    s0 = jnp.zeros((bsz, GLA_HEADS, dk, dv), jnp.float32)
    _, o = lax.scan(step, s0, tuple(to_chunks(z, GLA_CHUNK) for z in (q, k, v, log_alpha)))
    o = head_rms_norm(from_chunks(o), norm_g)
    return o.reshape(bsz, t, GLA_DV) * jax.nn.silu(og)

def mlstm_mix(fc, conv_w, conv_b, i_bias, f_bias, norm_g):
    bsz, t, _ = fc.shape
    dqk, dv = MLSTM_DQK // MLSTM_HEADS, MLSTM_DV // MLSTM_HEADS
    qk, v, i_pre, f_pre, og = _split(fc.astype(jnp.float32), (2 * MLSTM_DQK, MLSTM_DV, MLSTM_HEADS, MLSTM_HEADS, MLSTM_DV))
    q, k = _split(jax.nn.silu(causal_dwconv(qk, conv_w, conv_b)), (MLSTM_DQK, MLSTM_DQK))
    q = q.reshape(bsz, t, MLSTM_HEADS, dqk)
    k = k.reshape(bsz, t, MLSTM_HEADS, dqk) * dqk ** -0.5
    v = v.reshape(bsz, t, MLSTM_HEADS, dv)
    log_i = i_pre + i_bias
    log_f = jax.nn.log_sigmoid(f_pre + f_bias)
    mask = causal_mask(MLSTM_CHUNK)

    def step(carry, inp):
        c, n, m = carry
        q_c, k_c, v_c, li_c, lf_c = inp
        b = jnp.swapaxes(jnp.cumsum(lf_c, axis=1), 1, 2)
        li_c = jnp.swapaxes(li_c, 1, 2)
        log_d = jnp.where(mask, b[..., :, None] - b[..., None, :] + li_c[..., None, :], -jnp.inf)
        m_t = jnp.maximum(b + m[..., None], jnp.max(log_d, axis=-1))
        d = jnp.exp(log_d - m_t[..., None])
        inter = jnp.exp(b + m[..., None] - m_t)
        sc = jnp.einsum('blhd,bshd->bhls', q_c, k_c) * d
        num = (jnp.einsum('bhls,bshe->blhe', sc, v_c)
               + jnp.einsum('blhd,bhde->blhe', q_c, c) * jnp.swapaxes(inter, 1, 2)[..., None])
        den = jnp.sum(sc, axis=-1) + inter * jnp.einsum('blhd,bhd->bhl', q_c, n)
        h = num / jnp.swapaxes(jnp.maximum(jnp.abs(den), jnp.exp(-m_t)), 1, 2)[..., None]
        w_last, f_last = d[..., -1, :], inter[..., -1]
        c = f_last[..., None, None] * c + jnp.einsum('bhs,bshd,bshe->bhde', w_last, k_c, v_c)
        n = f_last[..., None] * n + jnp.einsum('bhs,bshd->bhd', w_last, k_c)
        return (c, n, m_t[..., -1]), h

    carry0 = (jnp.zeros((bsz, MLSTM_HEADS, dqk, dv), jnp.float32),
              jnp.zeros((bsz, MLSTM_HEADS, dqk), jnp.float32),
              jnp.zeros((bsz, MLSTM_HEADS), jnp.float32))
    _, h = lax.scan(step, carry0, tuple(to_chunks(z, MLSTM_CHUNK) for z in (q, k, v, log_i, log_f)))
    h = head_rms_norm(from_chunks(h), norm_g.reshape(MLSTM_HEADS, dv))
    return h.reshape(bsz, t, MLSTM_DV) * jax.nn.sigmoid(og)

def ssd_mix(fd, conv_w, conv_b, dt_bias, a_log, d_skip, norm_g):
    bsz, t, _ = fd.shape
    z, xbc, dt = _split(fd.astype(jnp.float32), (MIX_WIDTH, SSD_CONV_DIM, SSD_HEADS))
    x, bm, cm = _split(jax.nn.silu(causal_dwconv(xbc, conv_w, conv_b)),
                       (MIX_WIDTH, SSD_GROUPS * SSD_STATE, SSD_GROUPS * SSD_STATE))
    x = x.reshape(bsz, t, SSD_GROUPS, SSD_HPG, SSD_HEAD_DIM)
    bm = bm.reshape(bsz, t, SSD_GROUPS, SSD_STATE)
    cm = cm.reshape(bsz, t, SSD_GROUPS, SSD_STATE)
    dt = jax.nn.softplus(dt + dt_bias).reshape(bsz, t, SSD_GROUPS, SSD_HPG)
    a = -jnp.exp(a_log).reshape(SSD_GROUPS, SSD_HPG)
    mask = causal_mask(SSD_CHUNK)

    def step(s, inp):
        x_c, dt_c, b_c, c_c = inp
        acum = jnp.cumsum(dt_c * a, axis=1)
        ah = jnp.moveaxis(acum, 1, -1)
        seg = jnp.exp(jnp.where(mask, ah[..., :, None] - ah[..., None, :], -jnp.inf))
        xdt = x_c * dt_c[..., None]
        cb = jnp.einsum('blgn,bsgn->bgls', c_c, b_c)
        y = (jnp.einsum('bgls,bgrls,bsgrp->blgrp', cb, seg, xdt)
             + jnp.einsum('blgn,bgrpn,blgr->blgrp', c_c, s, jnp.exp(acum)))
        last = acum[:, -1]
        s = (jnp.exp(last)[..., None, None] * s
             + jnp.einsum('bsgn,bsgr,bsgrp->bgrpn', b_c, jnp.exp(last[:, None] - acum), xdt))
        return s, y

    s0 = jnp.zeros((bsz, SSD_GROUPS, SSD_HPG, SSD_HEAD_DIM, SSD_STATE), jnp.float32)
    _, y = lax.scan(step, s0, tuple(to_chunks(zz, SSD_CHUNK) for zz in (x, dt, bm, cm)))
    y = from_chunks(y) + x * d_skip.reshape(SSD_GROUPS, SSD_HPG)[..., None]
    return rms_norm(y.reshape(bsz, t, MIX_WIDTH) * jax.nn.silu(z), norm_g)

def second_inputs(seed: int = 0) -> dict:
    key = jax.random.key(seed)
    ks = iter(jax.random.split(key, 48))

    def nrm(shape, scale):
        return scale * jax.random.normal(next(ks), shape, jnp.float32)

    def gain(shape):
        return 1.0 + nrm(shape, 0.02)

    L = DEPTH
    dt0 = jnp.exp(jax.random.uniform(next(ks), (L, SSD_HEADS), jnp.float32, math.log(1e-3), math.log(1e-1)))
    return {
        'x': nrm((BATCH, SEQ, D_MODEL), 1.0),
        'mix_norm_g': gain((L, D_MODEL)),
        'w_in': nrm((L, D_MODEL, D_IN_2), D_MODEL ** -0.5),
        'rwkv_mu': jax.random.uniform(next(ks), (L, RWKV_IN), jnp.float32),
        'rwkv_w0': nrm((L, MIX_WIDTH), 1.0),
        'rwkv_w_up': nrm((L, RWKV_DECAY_LORA, MIX_WIDTH), RWKV_DECAY_LORA ** -0.5),
        'rwkv_a0': nrm((L, MIX_WIDTH), 0.5),
        'rwkv_a_up': nrm((L, RWKV_A_LORA, MIX_WIDTH), 0.5 * RWKV_A_LORA ** -0.5),
        'rwkv_g_up': nrm((L, RWKV_G_LORA, MIX_WIDTH), RWKV_G_LORA ** -0.5),
        'rwkv_k_k': 0.85 + nrm((L, MIX_WIDTH), 0.02),
        'rwkv_k_a': 1.0 + nrm((L, MIX_WIDTH), 0.02),
        'rwkv_r_k': nrm((L, RWKV_HEADS, RWKV_HEAD_DIM), 0.1),
        'rwkv_gn_g': gain((L, MIX_WIDTH)),
        'rwkv_gn_b': nrm((L, MIX_WIDTH), 0.02),
        'gla_f_up': nrm((L, GLA_GATE_LORA, GLA_DK), GLA_GATE_LORA ** -0.5),
        'gla_f_bias': nrm((L, GLA_DK), 0.5),
        'gla_norm_g': gain((L, GLA_DV // GLA_HEADS)),
        'mlstm_conv_w': nrm((L, MLSTM_CONV, 2 * MLSTM_DQK), MLSTM_CONV ** -0.5),
        'mlstm_conv_b': nrm((L, 2 * MLSTM_DQK), 0.02),
        'mlstm_i_bias': nrm((L, MLSTM_HEADS), 0.1),
        'mlstm_f_bias': jnp.linspace(3.0, 6.0, MLSTM_HEADS) + nrm((L, MLSTM_HEADS), 0.1),
        'mlstm_norm_g': gain((L, MLSTM_DV)),
        'ssd_conv_w': nrm((L, SSD_CONV, SSD_CONV_DIM), SSD_CONV ** -0.5),
        'ssd_conv_b': nrm((L, SSD_CONV_DIM), 0.02),
        'ssd_dt_bias': dt0 + jnp.log(-jnp.expm1(-dt0)),
        'ssd_a_log': jnp.log(jax.random.uniform(next(ks), (L, SSD_HEADS), jnp.float32, 1.0, 16.0)),
        'ssd_d': gain((L, SSD_HEADS)),
        'ssd_norm_g': gain((L, MIX_WIDTH)),
        'branch_proj': nrm((L, N_BRANCH, MIX_WIDTH, D_MODEL), MIX_WIDTH ** -0.5),
        'w_out': nrm((L, D_MODEL, D_MODEL), D_MODEL ** -0.5),
        'ffn_norm_g': gain((L, D_MODEL)),
        'ffn_up': nrm((L, D_MODEL, 2 * D_FF), D_MODEL ** -0.5),
        'ffn_conv_w': nrm((L, FFN_CONV, 2 * D_FF), FFN_CONV ** -0.5),
        'ffn_conv_b': nrm((L, 2 * D_FF), 0.02),
        'ffn_down': nrm((L, D_FF, D_MODEL), D_FF ** -0.5),
        'final_norm_g': gain((D_MODEL,)),
    }

def second_block(x, mix_norm_g, w_in, rwkv_mu, rwkv_w0, rwkv_w_up, rwkv_a0, rwkv_a_up, rwkv_g_up,
              rwkv_k_k, rwkv_k_a, rwkv_r_k, rwkv_gn_g, rwkv_gn_b, gla_f_up, gla_f_bias, gla_norm_g,
              mlstm_conv_w, mlstm_conv_b, mlstm_i_bias, mlstm_f_bias, mlstm_norm_g,
              ssd_conv_w, ssd_conv_b, ssd_dt_bias, ssd_a_log, ssd_d, ssd_norm_g,
              branch_proj, w_out, ffn_norm_g, ffn_up, ffn_conv_w, ffn_conv_b, ffn_down, final_norm_g):
    bsz, t, _ = x.shape
    h = x
    for l in range(DEPTH):
        u = rms_norm(h, mix_norm_g[l])
        fa, fb, fc, fd, fg = _split(u @ w_in[l], MIXER_IN_SIZES)
        branches = (
            rwkv7_mix(fa, rwkv_mu[l], rwkv_w0[l], rwkv_w_up[l], rwkv_a0[l], rwkv_a_up[l], rwkv_g_up[l],
                      rwkv_k_k[l], rwkv_k_a[l], rwkv_r_k[l], rwkv_gn_g[l], rwkv_gn_b[l]),
            gla_mix(fb, gla_f_up[l], gla_f_bias[l], gla_norm_g[l]),
            mlstm_mix(fc, mlstm_conv_w[l], mlstm_conv_b[l], mlstm_i_bias[l], mlstm_f_bias[l], mlstm_norm_g[l]),
            ssd_mix(fd, ssd_conv_w[l], ssd_conv_b[l], ssd_dt_bias[l], ssd_a_log[l], ssd_d[l], ssd_norm_g[l]),
        )
        gates = jax.nn.sigmoid(fg.astype(jnp.float32)).reshape(bsz, t, N_BRANCH, D_MODEL)
        merged = gates[:, :, 0] * (branches[0] @ branch_proj[l, 0])
        for i in range(1, N_BRANCH):
            merged = merged + gates[:, :, i] * (branches[i] @ branch_proj[l, i])
        h = h + merged @ w_out[l]
        u = rms_norm(h, ffn_norm_g[l])
        gate, val = _split(causal_dwconv(u @ ffn_up[l], ffn_conv_w[l], ffn_conv_b[l]), (D_FF, D_FF))
        h = h + (jax.nn.silu(gate) * val) @ ffn_down[l]
    return rms_norm(h, final_norm_g).astype(x.dtype)


_first_inputs_2 = second_inputs


def second_inputs(seed=0):
    import zlib

    import numpy as np

    out = dict(_first_inputs_2(seed))
    spreads = {}
    factors = {'rwkv_k_k': 8.0,
     'rwkv_k_a': 8.0,
     'rwkv_gn_g': 8.0,
     'rwkv_gn_b': 8.0,
     'gla_norm_g': 8.0,
     'mlstm_conv_b': 6.683,
     'mlstm_i_bias': 8.0,
     'mlstm_norm_g': 8.0,
     'ssd_conv_b': 4.012,
     'ssd_d': 8.0,
     'ssd_norm_g': 6.486,
     'ffn_norm_g': 4.31,
     'ffn_conv_b': 4.56,
     'final_norm_g': 2.944}
    for name, (base, spread) in spreads.items():
        noise = np.random.default_rng([zlib.crc32(name.encode()), seed]).standard_normal(out[name].shape)
        drawn = base * np.exp(spread * noise) if base else spread * noise
        out[name] = __import__('jax').numpy.asarray(drawn.astype(out[name].dtype))
    for name, factor in factors.items():
        out[name] = (out[name] * factor).astype(out[name].dtype)
    return out


_narrow_inputs_2 = second_inputs


def second_inputs(seed=0):

    out = dict(_narrow_inputs_2(seed))
    wider = {'rwkv_k_k': 12.0,
     'rwkv_k_a': 3.76,
     'rwkv_gn_g': 5.55,
     'rwkv_gn_b': 5.65,
     'gla_norm_g': 5.11,
     'mlstm_i_bias': 12.0,
     'mlstm_norm_g': 5.35,
     'ssd_d': 6.09,
     'ssd_norm_g': 4.06,
     'final_norm_g': 3.32}
    for name, times in wider.items():
        mean = out[name].mean()
        out[name] = (mean + times * (out[name] - mean)).astype(out[name].dtype)
    return out


DEPTH_3 = 2

N_MIXERS = 2
N_A_LAYERS = (DEPTH_3 + 1) // 2
N_B_LAYERS = DEPTH_3 // 2
CHUNK = 128
GM_WIDTH = 2 * D_MODEL
GM_GROUPS = 8
GM_GROUP_DIM = GM_WIDTH // GM_GROUPS
N_HEADS = 16
HEAD_DIM_3 = D_MODEL // N_HEADS
Q_BLOCK = 128
FFN_DIM = 2 * D_MODEL
CONV_WIDTH = 3
FORGET_BIAS_INIT = 4.0


def rmsnorm(x, g):
    xf = x.astype(jnp.float32)
    y = xf * lax.rsqrt(jnp.mean(xf * xf, axis=-1, keepdims=True) + RMS_EPS)
    return (y * g.astype(jnp.float32)).astype(x.dtype)

def layernorm(x, g, b):
    xf = x.astype(jnp.float32)
    mu = jnp.mean(xf, axis=-1, keepdims=True)
    xc = xf - mu
    y = xc * lax.rsqrt(jnp.mean(xc * xc, axis=-1, keepdims=True) + LN_EPS)
    return (y * g.astype(jnp.float32) + b.astype(jnp.float32)).astype(x.dtype)

def chunked_spatial_gating_mixer(h, w_in, ln_g, ln_b, w_s, b_s, w_out):
    bsz, seq, _ = h.shape
    z = jax.nn.gelu(h @ w_in)
    u, v = jnp.split(z, 2, axis=-1)
    v = layernorm(v, ln_g, ln_b)
    n_chunks = seq // CHUNK
    v = v.reshape(bsz, n_chunks, CHUNK, GM_GROUPS, GM_GROUP_DIM)
    causal = jnp.tril(jnp.ones((CHUNK, CHUNK), dtype=bool))
    w_causal = jnp.where(causal[None], w_s, jnp.zeros((), w_s.dtype))
    s = jnp.einsum("gts,bnsgc->bntgc", w_causal, v)
    s = s + b_s.T[None, None, :, :, None]
    s = s.reshape(bsz, seq, GM_WIDTH)
    return (u * s) @ w_out

def forgetting_attention_mixer(h, w_qkvf, b_f, w_o):
    bsz, seq, _ = h.shape
    proj = h @ w_qkvf
    q, k, v, f_logit = jnp.split(proj, [D_MODEL, 2 * D_MODEL, 3 * D_MODEL], axis=-1)
    q = q.reshape(bsz, seq, N_HEADS, HEAD_DIM_3)
    k = k.reshape(bsz, seq, N_HEADS, HEAD_DIM_3)
    v = v.reshape(bsz, seq, N_HEADS, HEAD_DIM_3)
    log_f = jax.nn.log_sigmoid((f_logit + b_f).astype(jnp.float32))
    cum = jnp.cumsum(log_f, axis=1).transpose(0, 2, 1)
    scale = HEAD_DIM_3 ** -0.5
    neg = jnp.finfo(jnp.float32).min
    outs = []
    for blk in range(seq // Q_BLOCK):
        q0 = blk * Q_BLOCK
        q1 = q0 + Q_BLOCK
        qb = q[:, q0:q1]
        kb = k[:, :q1]
        vb = v[:, :q1]
        logits = jnp.einsum("bqhd,bkhd->bhqk", qb, kb,
                            preferred_element_type=jnp.float32) * scale
        logits = logits + cum[:, :, q0:q1, None] - cum[:, :, None, :q1]
        mask = jnp.arange(q0, q1)[:, None] >= jnp.arange(q1)[None, :]
        logits = jnp.where(mask, logits, neg)
        p = jax.nn.softmax(logits, axis=-1)
        outs.append(jnp.einsum("bhqk,bkhd->bqhd", p.astype(vb.dtype), vb))
    o = jnp.concatenate(outs, axis=1).reshape(bsz, seq, D_MODEL)
    return o @ w_o

def conv_gated_ffn(h, w_gate, w_up, conv_w, conv_b, w_down):
    seq = h.shape[1]
    a = h @ w_gate
    a_pad = jnp.pad(a, ((0, 0), (CONV_WIDTH - 1, 0), (0, 0)))
    a = conv_b + a_pad[:, 0:seq] * conv_w[0]
    for i in range(1, CONV_WIDTH):
        a = a + a_pad[:, i:i + seq] * conv_w[i]
    return (jax.nn.silu(a) * (h @ w_up)) @ w_down

def third_inputs(seed: int = 0) -> dict:
    key = jax.random.key(seed)
    ks = jax.random.split(key, 20)

    def normal(k, shape, scale):
        return jax.random.normal(k, shape, jnp.float32) * scale

    D, E, G, C, H, F = D_MODEL, GM_WIDTH, GM_GROUPS, CHUNK, N_HEADS, FFN_DIM
    return {
        "x": normal(ks[0], (BATCH, SEQ, D), 1.0),
        "mix_norm_g": 1.0 + normal(ks[1], (DEPTH_3, D), 0.02),
        "ffn_norm_g": 1.0 + normal(ks[2], (DEPTH_3, D), 0.02),
        "gm_w_in": normal(ks[3], (N_A_LAYERS, D, 2 * E), D ** -0.5),
        "gm_ln_g": 1.0 + normal(ks[4], (N_A_LAYERS, E), 0.02),
        "gm_ln_b": normal(ks[5], (N_A_LAYERS, E), 0.02),
        "gm_w_s": normal(ks[6], (N_A_LAYERS, G, C, C), C ** -0.5),
        "gm_b_s": 1.0 + normal(ks[7], (N_A_LAYERS, G, C), 0.02),
        "gm_w_out": normal(ks[8], (N_A_LAYERS, E, D), E ** -0.5),
        "fox_w_qkvf": normal(ks[9], (N_B_LAYERS, D, 3 * D + H), D ** -0.5),
        "fox_b_f": FORGET_BIAS_INIT + normal(ks[10], (N_B_LAYERS, H), 0.5),
        "fox_w_o": normal(ks[11], (N_B_LAYERS, D, D), D ** -0.5),
        "ffn_w_gate": normal(ks[12], (DEPTH_3, D, F), D ** -0.5),
        "ffn_w_up": normal(ks[13], (DEPTH_3, D, F), D ** -0.5),
        "ffn_conv_w": normal(ks[14], (DEPTH_3, CONV_WIDTH, F), CONV_WIDTH ** -0.5),
        "ffn_conv_b": normal(ks[15], (DEPTH_3, F), 0.01),
        "ffn_w_down": normal(ks[16], (DEPTH_3, F, D), F ** -0.5),
        "final_norm_g": 1.0 + normal(ks[17], (D,), 0.02),
    }

def third_block(x, mix_norm_g, ffn_norm_g, gm_w_in, gm_ln_g, gm_ln_b, gm_w_s, gm_b_s,
              gm_w_out, fox_w_qkvf, fox_b_f, fox_w_o, ffn_w_gate, ffn_w_up,
              ffn_conv_w, ffn_conv_b, ffn_w_down, final_norm_g):
    h = x
    for i in range(DEPTH_3):
        hn = rmsnorm(h, mix_norm_g[i])
        j = i // N_MIXERS
        if i % N_MIXERS == 0:
            mix = chunked_spatial_gating_mixer(hn, gm_w_in[j], gm_ln_g[j], gm_ln_b[j],
                                               gm_w_s[j], gm_b_s[j], gm_w_out[j])
        else:
            mix = forgetting_attention_mixer(hn, fox_w_qkvf[j], fox_b_f[j], fox_w_o[j])
        h = h + mix
        hn = rmsnorm(h, ffn_norm_g[i])
        h = h + conv_gated_ffn(hn, ffn_w_gate[i], ffn_w_up[i], ffn_conv_w[i],
                               ffn_conv_b[i], ffn_w_down[i])
    return rmsnorm(h, final_norm_g)


_first_inputs_3 = third_inputs


def third_inputs(seed=0):
    import zlib

    import numpy as np

    out = dict(_first_inputs_3(seed))
    spreads = {}
    factors = {'mix_norm_g': 2.914,
     'ffn_norm_g': 8.691,
     'gm_ln_g': 21.818,
     'gm_ln_b': 20.445,
     'gm_b_s': 13.925,
     'ffn_conv_b': 25.598,
     'final_norm_g': 8.237}
    for name, (base, spread) in spreads.items():
        noise = np.random.default_rng([zlib.crc32(name.encode()), seed]).standard_normal(out[name].shape)
        drawn = base * np.exp(spread * noise) if base else spread * noise
        out[name] = __import__('jax').numpy.asarray(drawn.astype(out[name].dtype))
    for name, factor in factors.items():
        out[name] = (out[name] * factor).astype(out[name].dtype)
    return out


def setup_inputs(seed=0):
    out = dict(first_inputs(seed))
    for name, value in second_inputs(seed + 1).items():
        if name != "x":
            out[name + "_2"] = value
    for name, value in third_inputs(seed + 2).items():
        if name != "x":
            out[name + "_3"] = value
    return out


def reference(
    x, ln1_g, ln1_b, ffn1_w1, ffn1_w3, ffn1_w2, ln2_g, ln2_b, w_in, b_in, attn_sinks,
    hgrn_lb_logits, hgrn_norm_g, w_proj_attn, w_proj_hgrn, w_out, ln3_g, ln3_b, ffn2_w1,
    ffn2_w3, ffn2_w2, mix_norm_g_2, w_in_2, rwkv_mu_2, rwkv_w0_2, rwkv_w_up_2, rwkv_a0_2,
    rwkv_a_up_2, rwkv_g_up_2, rwkv_k_k_2, rwkv_k_a_2, rwkv_r_k_2, rwkv_gn_g_2, rwkv_gn_b_2,
    gla_f_up_2, gla_f_bias_2, gla_norm_g_2, mlstm_conv_w_2, mlstm_conv_b_2, mlstm_i_bias_2,
    mlstm_f_bias_2, mlstm_norm_g_2, ssd_conv_w_2, ssd_conv_b_2, ssd_dt_bias_2, ssd_a_log_2,
    ssd_d_2, ssd_norm_g_2, branch_proj_2, w_out_2, ffn_norm_g_2, ffn_up_2, ffn_conv_w_2,
    ffn_conv_b_2, ffn_down_2, final_norm_g_2, mix_norm_g_3, ffn_norm_g_3, gm_w_in_3, gm_ln_g_3,
    gm_ln_b_3, gm_w_s_3, gm_b_s_3, gm_w_out_3, fox_w_qkvf_3, fox_b_f_3, fox_w_o_3, ffn_w_gate_3,
    ffn_w_up_3, ffn_conv_w_3, ffn_conv_b_3, ffn_w_down_3, final_norm_g_3,
):
    x = first_block(
        x, ln1_g, ln1_b, ffn1_w1, ffn1_w3, ffn1_w2, ln2_g, ln2_b, w_in, b_in, attn_sinks,
        hgrn_lb_logits, hgrn_norm_g, w_proj_attn, w_proj_hgrn, w_out, ln3_g, ln3_b, ffn2_w1,
        ffn2_w3, ffn2_w2,
    )
    x = second_block(
        x, mix_norm_g_2, w_in_2, rwkv_mu_2, rwkv_w0_2, rwkv_w_up_2, rwkv_a0_2, rwkv_a_up_2,
        rwkv_g_up_2, rwkv_k_k_2, rwkv_k_a_2, rwkv_r_k_2, rwkv_gn_g_2, rwkv_gn_b_2, gla_f_up_2,
        gla_f_bias_2, gla_norm_g_2, mlstm_conv_w_2, mlstm_conv_b_2, mlstm_i_bias_2,
        mlstm_f_bias_2, mlstm_norm_g_2, ssd_conv_w_2, ssd_conv_b_2, ssd_dt_bias_2, ssd_a_log_2,
        ssd_d_2, ssd_norm_g_2, branch_proj_2, w_out_2, ffn_norm_g_2, ffn_up_2, ffn_conv_w_2,
        ffn_conv_b_2, ffn_down_2, final_norm_g_2,
    )
    return third_block(
        x, mix_norm_g_3, ffn_norm_g_3, gm_w_in_3, gm_ln_g_3, gm_ln_b_3, gm_w_s_3, gm_b_s_3,
        gm_w_out_3, fox_w_qkvf_3, fox_b_f_3, fox_w_o_3, ffn_w_gate_3, ffn_w_up_3, ffn_conv_w_3,
        ffn_conv_b_3, ffn_w_down_3, final_norm_g_3,
    )


_drawn_inputs = setup_inputs


def setup_inputs(seed=0):
    import zlib

    import numpy as np

    out = dict(_drawn_inputs(seed))
    spreads = {}
    factors = {'mlstm_i_bias_2': 200.0,
     'gm_ln_g_3': 25.336,
     'gm_ln_b_3': 27.659,
     'gm_b_s_3': 25.994,
     'fox_b_f_3': 46.544,
     'final_norm_g_3': 21.509,
     'ffn_norm_g_3': 3.215,
     'ffn_conv_b_3': 3.1,
     'fox_w_qkvf_3': 8.0,
     'fox_w_o_3': 8.0}
    for name, (base, spread) in spreads.items():
        noise = np.random.default_rng([zlib.crc32(name.encode()), seed]).standard_normal(out[name].shape)
        drawn = base * np.exp(spread * noise) if base else spread * noise
        out[name] = __import__('jax').numpy.asarray(drawn.astype(out[name].dtype))
    for name, factor in factors.items():
        out[name] = (out[name] * factor).astype(out[name].dtype)
    return out
```

```python
from contextlib import ExitStack

import numpy as np

import concourse.bass as bass
from concourse import mybir

F32 = mybir.dt.float32
ACT = mybir.ActivationFunctionType
ALU = mybir.AluOpType
AX_X = mybir.AxisListType.X

P = 128
S = 512
TT = S // P
D = 1024
DT = D // P
D_FF = 2816
FT = D_FF // P
CHUNK = 64
NC = S // CHUNK
ALPHA = 2.0 ** 0.25
DECAY_SCALE = 0.6065306597
LEVELS = 6
NEG = -1e30


def tables():
    s = np.arange(P)[:, None]
    t = np.arange(P)[None, :]
    same = (s // CHUNK) == (t // CHUNK)
    out = {
        "ident": (s == t),
        "ones": np.ones((P, P)),
        "head_ones": (s // 64) == (t // 64),
        "causal_chunk": (s <= t) & same,
        "strict_chunk": (s < t) & same,
        "mask_diag": np.where(t <= s, 0.0, NEG),
        "mask_prev": np.where(t > s, 0.0, NEG),
        "causal": (s <= t),
    }
    rot = np.zeros((P, P))
    for base in (0, 64):
        for j in range(8):
            rot[base + 8 + j, base + j] = -1.0
            rot[base + j, base + 8 + j] = 1.0
    out["rot"] = rot
    for n in range(LEVELS):
        half = 1 << n
        block = (s // (2 * half)) == (t // (2 * half))
        out[f"level{n}"] = block & (s % (2 * half) < half) & (t % (2 * half) >= half)
    out["mask_after"] = np.concatenate([np.where(s <= t, 0.0, NEG), np.zeros((P, S - P))], 1)
    out["restart"] = np.broadcast_to((np.arange(S) % CHUNK != 0), (P, S))
    pos = np.arange(S, dtype=np.float32)
    inv = np.float32(500000.0) ** (-np.arange(0, 16, 2, dtype=np.float32) / np.float32(16))
    ang = (pos[:, None] * inv[None, :]).astype(np.float32)
    c, sn = np.ones((P, S), np.float32), np.zeros((P, S), np.float32)
    for base in (0, 8, 64, 72):
        c[base:base + 8] = np.cos(ang).T
        sn[base:base + 8] = np.sin(ang).T
    out["cos"], out["sin"] = c, sn
    pick = np.zeros((P, 16, P))
    for h in range(16):
        pick[h, h, :] = 1.0
    out["pick"] = pick.reshape(P, 16 * P)
    return {k: np.ascontiguousarray(v, dtype=np.float32) for k, v in out.items()}


TABLES = tables()
TABLE_AT, _at = {}, 0
for _name, _v in TABLES.items():
    TABLE_AT[_name] = (_at, _v.shape[1])
    _at += _v.shape[1]
TABLE_WIDTH = _at

COLUMNS = [
    ("ln1_g", 8), ("ln1_b", 8), ("ln2_g", 8), ("ln2_b", 8), ("ln3_g", 8), ("ln3_b", 8),
    ("att_qb", 8), ("att_kb", 8), ("sinks", 16),
    ("hg_qb", 8), ("hg_fb", 8), ("hg_ogb", 8), ("hg_lb", 16), ("hg_ng", 1), ("gate_b", 16),
    ("mix2_g", 8), ("lora_mu", 2), ("r_mu", 4), ("k_mu", 4), ("v_mu", 4), ("w0", 4), ("a0", 4),
    ("k_k", 4), ("k_a", 4), ("r_k", 4), ("gn_g", 4), ("gn_b", 4),
    ("gla_fb", 4), ("gla_ng", 1),
    ("ml_cw", 32), ("ml_cb", 8), ("ml_ib", 4), ("ml_fb", 4), ("ml_ng", 4),
    ("sd_cwx", 16), ("sd_cbx", 4), ("sd_cwbc", 32), ("sd_cbbc", 8), ("sd_dtb", 8), ("sd_alog", 8), ("sd_d", 4),
    ("sd_ng", 4), ("ffn2_g", 8), ("ffn2_cw", 132), ("ffn2_cb", 44), ("fin2_g", 8),
    ("mix3_g", 16), ("ffn3_g", 16), ("ffn3_cw", 96), ("ffn3_cb", 32), ("fox_fb", 1), ("fin3_g", 8),
]
COLUMN_AT, _at = {}, 0
for _name, _n in COLUMNS:
    COLUMN_AT[_name] = _at
    _at += _n
COLUMN_WIDTH = _at


class Stage:

    def __init__(self, nc, name):
        self.nc, self.name, self.stack, self.sems = nc, name, ExitStack(), []

    def __enter__(self):
        return self

    def __exit__(self, *e):
        if e[0] is None:
            for sem in self.sems:
                self.nc.gpsimd.sem_clear(sem)
        return self.stack.__exit__(*e)

    def sb(self, name, shape):
        return self.stack.enter_context(self.nc.sbuf_tensor(f"{self.name}_{name}", shape, F32))

    def ps(self, name, shape):
        return self.stack.enter_context(self.nc.psum_tensor(f"{self.name}_{name}", shape, F32))

    def sem(self, name):
        self.sems.append(self.stack.enter_context(self.nc.semaphore(f"{self.name}_{name}")))
        return self.sems[-1]


class InOrder:

    def __init__(self, eng, sem):
        self.eng, self.sem, self.base, self.n = eng, sem, 0, 0

    def __call__(self, ins):
        ins.then_inc(self.sem, 1)
        self.n += 1
        self.eng.wait_ge(self.sem, self.base + self.n)


class Steps:

    def __init__(self, sem, names):
        self.sem, self.names = sem, names.split()
        assert len(set(self.names)) == len(self.names)

    def wait(self, eng, name, r=0):
        eng.wait_ge(self.sem, r * len(self.names) + self.names.index(name) + 1)

    def wait_round(self, eng, r):
        eng.wait_ge(self.sem, r * len(self.names))

    def done(self, ins, name):
        assert name in self.names
        ins.then_inc(self.sem, 1)


def rounds(eng, n, body, chain=None):
    start = chain.base + chain.n if chain else 0
    if chain:
        chain.base, chain.n = start, 0
    body(0, True)
    per = chain.n if chain else 0
    if n > 1:
        with eng.Fori(1, n) as r:
            if chain:
                chain.base, chain.n = r * per + start, 0
            body(r, False)
    if chain:
        chain.base, chain.n = start + n * per, 0


def tile_cols(k):
    return slice(k * P, (k + 1) * P)


class Ctx:

    def __init__(self, nc, table, column):
        self.nc, self.table, self.column = nc, table, column

    def tab(self, name, part=P):
        at, width = TABLE_AT[name]
        return self.table[0:part, at:at + width]

    def col(self, name, i=0, n=1):
        at = COLUMN_AT[name] + i
        return self.column[:, bass.ds(at, n)]


def load_constants(c, table_d, column_d, x_d, x):
    nc = c.nc
    with Stage(nc, "const") as st:
        landed = st.sem("landed")
        with nc.Block() as block:
            @block.sync
            def _(sp):
                sp.dma_start(c.table[:, :], table_d).then_inc(landed, 16)
                sp.dma_start(c.column[:, :], column_d).then_inc(landed, 16)
                sp.dma_start(x[:, :, :], x_d).then_inc(landed, 16)
                sp.wait_ge(landed, 48)


def stream(sp, n, w_d, w, landed, used):
    def body(r, first):
        for j in range(2):
            if not first:
                sp.wait_ge(used, 2 * r + j - 1)
            sp.dma_start(w[j][:], w_d[2 * r + j]).then_inc(landed[j], 16)
    rounds(sp, n // 2, body)


def norm(c, name, x, out, kt, centre, eps, g, b=None, sink_d=None):
    nc = c.nc
    width = kt * P
    with Stage(nc, name) as st:
        mean_p, var_p = st.ps("mean", [P, S]), st.ps("var", [P, S])
        sq = st.sb("sq", [P, 2, S])
        xc = st.sb("xc", [P, kt, S]) if centre else x
        rstd, std, negmean = st.sb("rstd", [P, S]), st.sb("std", [P, S]), st.sb("mean_s", [P, S])
        mean_ready, mean_here, centred, squared, summed = (
            st.sem(n) for n in ("mean_ready", "mean_here", "centred", "squared", "summed"))
        var_ready, std_ready, rstd_ready, scaled, normed, stored = (
            st.sem(n) for n in ("var_ready", "std_ready", "rstd_ready", "scaled", "normed", "stored"))
        with nc.Block() as block:
            @block.tensor
            def _(pe):
                if centre:
                    for k in range(kt):
                        last = pe.matmul(mean_p[:, :], c.tab("ones"), x[:, k, :], start=k == 0, stop=k == kt - 1)
                    last.then_inc(mean_ready, 1)
                for k in range(kt):
                    pe.wait_ge(squared, k + 1)
                    pe.matmul(var_p[:, :], c.tab("ones"), sq[:, k % 2, :], start=k == 0,
                              stop=k == kt - 1).then_inc(summed, 1)

            @block.scalar
            def _(act):
                for k in range(kt):
                    if centre:
                        act.wait_ge(centred, k + 1)
                    if k >= 2:
                        act.wait_ge(summed, k - 1)
                    act.activation(sq[:, k % 2, :], xc[:, k, :], ACT.Square).then_inc(squared, 1)
                act.wait_ge(var_ready, 1)
                act.activation(std[:, :], std[:, :], ACT.Sqrt).then_inc(std_ready, 1)
                for k in range(kt):
                    act.wait_ge(scaled, k + 1)
                    act.activation(out[:, k, :], (xc if centre else out)[:, k, :], ACT.Identity, scale=g(k),
                                   bias=b(k) if b else 0.0).then_inc(normed, 1)

            @block.vector
            def _(dve):
                if centre:
                    dve.wait_ge(mean_ready, 1)
                    dve.tensor_scalar(negmean[:, :], mean_p[:, :], 1.0 / width, None, ALU.mult).then_inc(mean_here, 1)
                    dve.wait_ge(mean_here, 1)
                    for k in range(kt):
                        dve.tensor_tensor(xc[:, k, :], x[:, k, :], negmean[:, :], ALU.subtract).then_inc(centred, 1)
                dve.wait_ge(summed, kt)
                dve.tensor_scalar(std[:, :], var_p[:, :], 1.0 / width, eps, ALU.mult, ALU.add).then_inc(var_ready, 1)
                dve.wait_ge(std_ready, 1)
                dve.reciprocal(rstd[:, :], std[:, :]).then_inc(rstd_ready, 1)
                dve.wait_ge(rstd_ready, 1)
                for k in range(kt):
                    o = xc if centre else out
                    dve.tensor_tensor(o[:, k, :], xc[:, k, :], rstd[:, :], ALU.mult).then_inc(scaled, 1)

            if sink_d is not None:
                @block.sync
                def _(sp):
                    sp.wait_ge(normed, kt)
                    sp.dma_start(sink_d, out[:, :, :]).then_inc(stored, 16)
                    sp.wait_ge(stored, 16)


def swiglu_up(c, name, w_d, x, hidden, n):
    nc = c.nc
    with Stage(nc, name) as st:
        w = [st.sb(f"w{j}", [P, 2, D]) for j in range(2)]
        acc = st.ps("acc", [P, 2, 2, S])
        gate = st.sb("gate", [P, 2, S])
        landed = [st.sem(f"landed{j}") for j in range(2)]
        made, gated, done = st.sem("made"), st.sem("gated"), st.sem("done")
        with nc.Block() as block:
            @block.sync
            def _(sp):
                stream(sp, n, w_d, w, landed, made)

            @block.tensor
            def _(pe):
                def body(r, first):
                    for j in range(2):
                        pe.wait_ge(landed[j], 16 * (r + 1))
                        if not first:
                            pe.wait_ge(done, 2 * r + j - 1)
                        for part in range(2):
                            for k in range(DT):
                                last = pe.matmul(acc[:, j, part, :], w[j][:, part, tile_cols(k)], x[:, k, :],
                                                 start=k == 0, stop=k == DT - 1)
                        last.then_inc(made, 1)
                rounds(pe, n // 2, body)

            @block.scalar
            def _(act):
                def body(r, first):
                    for j in range(2):
                        act.wait_ge(made, 2 * r + j + 1)
                        if not first:
                            act.wait_ge(done, 2 * r + j - 1)
                        act.activation(gate[:, j, :], acc[:, j, 0, :], ACT.Silu).then_inc(gated, 1)
                rounds(act, n // 2, body)

            @block.vector
            def _(dve):
                def body(r, first):
                    for j in range(2):
                        dve.wait_ge(gated, 2 * r + j + 1)
                        dve.tensor_tensor(hidden[:, 2 * r + j, :], gate[:, j, :], acc[:, j, 1, :],
                                          ALU.mult).then_inc(done, 1)
                rounds(dve, n // 2, body)


def project(c, name, w_d, src, kt, n, out, residual=None, res_scale=1.0, scale=1.0,
            func=ACT.Copy):
    nc = c.nc
    with Stage(nc, name) as st:
        w = [st.sb(f"w{j}", [P, kt * P]) for j in range(2)]
        acc = st.ps("acc", [P, 2, S])
        tmp = st.sb("tmp", [P, 2, S])
        landed = [st.sem(f"landed{j}") for j in range(2)]
        made, scaled, done = st.sem("made"), st.sem("scaled"), st.sem("done")
        read = scaled if residual is not None else done
        with nc.Block() as block:
            @block.sync
            def _(sp):
                stream(sp, n, w_d, w, landed, made)

            @block.tensor
            def _(pe):
                def body(r, first):
                    for j in range(2):
                        pe.wait_ge(landed[j], 16 * (r + 1))
                        if not first:
                            pe.wait_ge(read, 2 * r + j - 1)
                        for k in range(kt):
                            last = pe.matmul(acc[:, j, :], w[j][:, tile_cols(k)], src[:, k, :],
                                             start=k == 0, stop=k == kt - 1)
                        last.then_inc(made, 1)
                rounds(pe, n // 2, body)

            @block.scalar
            def _(act):
                def body(r, first):
                    for j in range(2):
                        act.wait_ge(made, 2 * r + j + 1)
                        if residual is None:
                            act.activation(out[:, 2 * r + j, :], acc[:, j, :], func, scale=scale).then_inc(done, 1)
                        else:
                            if not first:
                                act.wait_ge(done, 2 * r + j - 1)
                            act.activation(tmp[:, j, :], acc[:, j, :], ACT.Copy, scale=scale).then_inc(scaled, 1)
                rounds(act, n // 2, body)

            if residual is not None:
                @block.vector
                def _(dve):
                    def body(r, first):
                        for j in range(2):
                            dve.wait_ge(scaled, 2 * r + j + 1)
                            dve.scalar_tensor_tensor(out[:, 2 * r + j, :], residual[:, 2 * r + j, :], res_scale,
                                                     tmp[:, j, :], ALU.mult, ALU.add).then_inc(done, 1)
                    rounds(dve, n // 2, body)


def conv_glu_up(c, name, w_d, x, hidden, n, gate_w, gate_b, val_w=None, val_b=None):
    nc = c.nc
    sides = 2 if val_w is not None else 1
    with Stage(nc, name) as st:
        w = [st.sb(f"w{j}", [P, 2, D]) for j in range(2)]
        acc = st.ps("acc", [P, 2, 2, S])
        pad = st.sb("pad", [P, 2, 2, S + 2])
        conv = st.sb("conv", [P, 2, 2, S])
        gate = st.sb("gate", [P, 2, S])
        landed = [st.sem(f"landed{j}") for j in range(2)]
        made, zeroed, padded, chain, convolved, gated, done = (
            st.sem(n) for n in ("made", "zeroed", "padded", "chain", "convolved", "gated", "done"))
        with nc.Block() as block:
            @block.sync
            def _(sp):
                stream(sp, n, w_d, w, landed, made)

            @block.tensor
            def _(pe):
                def body(r, first):
                    for j in range(2):
                        pe.wait_ge(landed[j], 16 * (r + 1))
                        if not first:
                            pe.wait_ge(done, 2 * r + j - 1)
                        for part in range(2):
                            for k in range(DT):
                                last = pe.matmul(acc[:, j, part, :], w[j][:, part, tile_cols(k)], x[:, k, :],
                                                 start=k == 0, stop=k == DT - 1)
                        last.then_inc(made, 1)
                rounds(pe, n // 2, body)

            @block.scalar
            def _(act):
                act.wait_ge(zeroed, 1)

                def body(r, first):
                    for j in range(2):
                        act.wait_ge(made, 2 * r + j + 1)
                        if not first:
                            act.wait_ge(done, 2 * r + j - 1)
                        for q in range(sides):
                            act.activation(pad[:, j, q, 2:], acc[:, j, q, :], ACT.Copy).then_inc(padded, 1)
                        act.wait_ge(convolved, 2 * r + j + 1)
                        act.activation(gate[:, j, :], conv[:, j, 0, :], ACT.Silu).then_inc(gated, 1)
                rounds(act, n // 2, body)

            @block.vector
            def _(dve):
                dve.memset(pad[:, :, :, 0:2], 0.0).then_inc(zeroed, 1)
                q = InOrder(dve, chain)

                def body(r, first):
                    for j in range(2):
                        t = 2 * r + j
                        for side in reversed(range(sides)):
                            cw, cb = (gate_w, gate_b) if side == 0 else (val_w, val_b)
                            dve.wait_ge(padded, sides * t + side + 1)
                            a = conv[:, j, side, :]
                            q(dve.tensor_scalar(a, pad[:, j, side, 0:S], cw(0, t), cb(t), ALU.mult, ALU.add))
                            q(dve.scalar_tensor_tensor(a, pad[:, j, side, 1:S + 1], cw(1, t), a, ALU.mult, ALU.add))
                            last = dve.scalar_tensor_tensor(a, pad[:, j, side, 2:S + 2], cw(2, t), a, ALU.mult, ALU.add)
                            if side:
                                q(last)
                            else:
                                last.then_inc(convolved, 1)
                        dve.wait_ge(gated, t + 1)
                        value = conv[:, j, 1, :] if sides == 2 else acc[:, j, 1, :]
                        dve.tensor_tensor(hidden[:, t, :], gate[:, j, :], value, ALU.mult).then_inc(done, 1)
                rounds(dve, n // 2, body, q)


def merge(c, name, x, w_d, branches, kts, out, gate_b=None):
    nc = c.nc
    nb = len(branches)
    wide = D + max(kts) * P
    with Stage(nc, name) as st:
        w = [st.sb(f"w{j}", [P, wide]) for j in range(2)]
        acc = st.ps("acc", [P, 2, 2, S])
        gate, part = st.sb("gate", [P, 2, S]), st.sb("part", [P, 2, S])
        landed = [st.sem(f"landed{j}") for j in range(2)]
        made, gated, chain, done = st.sem("made"), st.sem("gated"), st.sem("chain"), st.sem("done")
        with nc.Block() as block:
            @block.sync
            def _(sp):
                def body(m, first):
                    for b in range(nb):
                        j = b % 2
                        if not first or b >= 2:
                            sp.wait_ge(made, m * nb + b - 1)
                        sp.dma_start(w[j][:], w_d[m, b]).then_inc(landed[j], 16)
                rounds(sp, DT, body)

            @block.tensor
            def _(pe):
                def body(m, first):
                    for b in range(nb):
                        j = b % 2
                        pe.wait_ge(landed[j], (m * (nb // 2) + b // 2 + 1) * 16)
                        if not first or b >= 2:
                            pe.wait_ge(done, m * nb + b - 1)
                        for k in range(DT):
                            pe.matmul(acc[:, j, 0, :], w[j][:, tile_cols(k)], x[:, k, :], start=k == 0, stop=k == DT - 1)
                        for k in range(kts[b]):
                            last = pe.matmul(acc[:, j, 1, :], w[j][:, D + k * P:D + (k + 1) * P], branches[b][:, k, :],
                                             start=k == 0, stop=k == kts[b] - 1)
                        last.then_inc(made, 1)
                rounds(pe, DT, body)

            @block.scalar
            def _(act):
                def body(m, first):
                    for b in range(nb):
                        j = b % 2
                        act.wait_ge(made, m * nb + b + 1)
                        if not first or b >= 2:
                            act.wait_ge(done, m * nb + b - 1)
                        act.activation(gate[:, j, :], acc[:, j, 0, :], ACT.Sigmoid,
                                       bias=gate_b(b, m) if gate_b else 0.0).then_inc(gated, 1)
                rounds(act, DT, body)

            @block.vector
            def _(dve):
                q = InOrder(dve, chain)

                def body(m, first):
                    for b in range(nb):
                        j = b % 2
                        dve.wait_ge(gated, m * nb + b + 1)
                        if b == 0:
                            dve.tensor_tensor(out[:, m, :], gate[:, j, :], acc[:, j, 1, :], ALU.mult).then_inc(done, 1)
                        else:
                            q(dve.tensor_tensor(part[:, j, :], gate[:, j, :], acc[:, j, 1, :], ALU.mult))
                            dve.wait_ge(done, m * nb + b)
                            dve.tensor_tensor(out[:, m, :], out[:, m, :], part[:, j, :], ALU.add).then_inc(done, 1)
                rounds(dve, DT, body, q)


def attention(c, name, x, w_d, y, spans, qb=None, kb=None, vb_d=None, sinks=None, forget=None, rope=False):
    nc = c.nc
    scale = 0.125
    pairs = DT
    with Stage(nc, name) as st:
        w = st.sb("w", [P, 3, D])
        qz, vz = st.sb("qz", [P, 2, S]), st.sb("vz", [P, 2, TT, P])
        kk = st.sb("kk", [P, S])
        qr, kr, rq = st.sb("qr", [P, S]), st.sb("kr", [P, S]), st.sb("rq", [P, S])
        vrow = st.sb("vrow", [P, P])
        prob, probT = st.sb("prob", [P, 2, S]), st.sb("probT", [P, 4, S])
        pick, sink = st.sb("pick", [P, 2, P]), st.sb("sink", [P, 2])
        top, nmax, rsum, esink, rinv = (st.sb(n, [P, 8]) for n in ("top", "nmax", "rsum", "esink", "rinv"))
        sc, tr, o = st.ps("sc", [P, 4, S]), st.ps("tr", [P, 2, S]), st.ps("o", [P, S])
        landed, zeroed, projected, biased, turned, roped, q_ready, k_ready, v_ready = (
            st.sem(n) for n in ("landed", "zeroed", "projected", "biased", "turned", "roped", "q_ready", "k_ready", "v_ready"))
        scored, maxed, exped, normed, transposed, copied, weighed, stored, chain, achain, picked = (
            st.sem(n) for n in ("scored", "maxed", "exped", "normed", "transposed", "copied", "weighed", "stored",
                                "chain", "achain", "picked"))
        loads = 2 if vb_d is not None else 1
        nqk = 2 if rope else 3

        with nc.Block() as block:
            @block.sync
            def _(sp):
                if vb_d is not None:
                    sp.wait_ge(zeroed, 3)

                def body(p, first):
                    if not first:
                        sp.wait_ge(projected, 3 * p)
                    sp.dma_start(w[:, :, :], w_d[p]).then_inc(landed, 16)
                    if vb_d is not None:
                        sp.dma_start(vrow[0:1, :], vb_d[p]).then_inc(landed, 16)
                rounds(sp, pairs, body)

            @block.tensor
            def _(pe):
                def body(p, first):
                    pe.wait_ge(landed, 16 * loads * (p + 1))
                    if not first:
                        pe.wait_ge(exped, 8 * p)
                    for part in range(2):
                        for k in range(DT):
                            last = pe.matmul(sc[:, part, :], w[:, part, tile_cols(k)], x[:, k, :], start=k == 0, stop=k == DT - 1)
                        last.then_inc(projected, 1)
                    for t in range(TT):
                        for k in range(DT):
                            last = pe.matmul(sc[:, 2, tile_cols(t)], x[:, k, tile_cols(t)], w[:, 2, tile_cols(k)],
                                             start=k == 0, stop=k == DT - 1 and vb_d is None)
                        if vb_d is not None:
                            last = pe.matmul(sc[:, 2, tile_cols(t)], c.tab("ones"), vrow[:, :], start=False, stop=True)
                    last.then_inc(projected, 1)
                    if rope:
                        pe.wait_ge(biased, 2 * p + 1)
                        pe.matmul(sc[:, 3, :], c.tab("rot"), qr[:, :], start=True, stop=True).then_inc(turned, 1)
                        pe.wait_ge(biased, 2 * p + 2)
                        pe.matmul(sc[:, 0, :], c.tab("rot"), kr[:, :], start=True, stop=True).then_inc(turned, 1)
                    pe.wait_ge(q_ready, 2 * (p + 1))
                    pe.wait_ge(k_ready, p + 1)
                    pe.wait_ge(v_ready, 2 * (p + 1))
                    if forget is not None:
                        pe.wait_ge(picked, 2 * (p + 1))

                    def scores(u):
                        i, h = u // 2, u % 2
                        if u >= 4:
                            pe.wait_ge(exped, 8 * p + u - 3)
                        k0, n = spans[i][0] * P, len(spans[i]) * P
                        pe.matmul(sc[:, u % 4, 0:n], qz[:, h, tile_cols(i)], kk[:, k0:k0 + n], start=True, stop=False)
                        if forget is not None:
                            pe.matmul(sc[:, u % 4, 0:n], pick[:, h, :], forget[:, k0:k0 + n], start=False, stop=False)
                        if rope and i:
                            pe.matmul(sc[:, u % 4, 0:P], c.tab("ident"), c.tab("mask_prev"), start=False, stop=False)
                        pe.matmul(sc[:, u % 4, n - P:n], c.tab("ident"), c.tab("mask_diag"), start=False,
                                  stop=True).then_inc(scored, 1)

                    for u in range(4):
                        scores(u)
                    for u in range(8):
                        i, h = u // 2, u % 2
                        pe.wait_ge(normed, 8 * p + u + 1)
                        if not first or u >= 2:
                            pe.wait_ge(copied, 8 * p + u - 1)
                        for b in range(len(spans[i])):
                            last = pe.transpose(tr[:, u % 2, tile_cols(b)], prob[:, u % 2, tile_cols(b)], c.tab("ident"))
                        last.then_inc(transposed, 1)
                        if u + 4 < 8:
                            scores(u + 4)
                        if h:
                            pe.wait_ge(copied, 8 * p + u + 1)
                            if i == 0 and not first:
                                pe.wait_ge(stored, p)
                            n = len(spans[i])
                            for g in range(2):
                                for b in range(n):
                                    last = pe.matmul(o[:, tile_cols(i)], vz[:, g, spans[i][b], :],
                                                     probT[:, (u - 1 + g) % 4, tile_cols(b)],
                                                     start=g == 0 and b == 0, stop=g == 1 and b == n - 1)
                            last.then_inc(weighed, 1)
                rounds(pe, pairs, body)

            @block.scalar
            def _(act):
                act.wait_ge(zeroed, 3)
                q = InOrder(act, achain)

                def body(p, first):
                    if not first:
                        act.wait_ge(scored, 8 * p)
                        act.wait_ge(weighed, 4 * p)
                    act.wait_ge(projected, 3 * p + 1)
                    if rope:
                        act.activation(qr[:, :], sc[:, 0, :], ACT.Identity, bias=qb(p)).then_inc(biased, 1)
                        act.wait_ge(projected, 3 * p + 2)
                        act.activation(kr[:, :], sc[:, 1, :], ACT.Identity, bias=kb(p)).then_inc(biased, 1)
                    else:
                        for h in range(2):
                            half = slice(64 * h, 64 * h + 64)
                            act.activation(qz[half, h, :], sc[half, 0, :], ACT.Copy).then_inc(q_ready, 1)
                        act.wait_ge(projected, 3 * p + 2)
                        act.activation(kk[:, :], sc[:, 1, :], ACT.Copy).then_inc(k_ready, 1)
                    act.wait_ge(projected, 3 * p + 3)
                    for h in range(2):
                        half = slice(64 * h, 64 * h + 64)
                        act.activation(vz[:, h, :, half], sc[:, 2, :].rearrange("p (t f) -> p t f", t=TT)[:, :, half],
                                       ACT.Copy).then_inc(v_ready, 1)

                    if sinks is not None:
                        q(act.activation(sink[:, :], sinks(2 * p, 2), ACT.Copy))

                    def exps(u):
                        i = u // 2
                        n = len(spans[i]) * P
                        act.wait_ge(maxed, 8 * p + u + 1)
                        if sinks is not None:
                            q(act.activation(esink[:, u:u + 1], sink[:, u % 2:u % 2 + 1], ACT.Exp, bias=nmax[:, u:u + 1]))
                        if not first or u >= 2:
                            act.wait_ge(transposed, 8 * p + u - 1)
                        act.activation(prob[:, u % 2, 0:n], sc[:, u % 4, 0:n], ACT.Exp, scale=scale,
                                       bias=nmax[:, u:u + 1], accum_out=rsum[:, u:u + 1]).then_inc(exped, 1)

                    def copies(u):
                        i = u // 2
                        n = len(spans[i]) * P
                        act.wait_ge(transposed, 8 * p + u + 1)
                        if not first or u >= 4:
                            act.wait_ge(weighed, 4 * p + i - 1)
                        act.activation(probT[:, u % 4, 0:n], tr[:, u % 2, 0:n], ACT.Copy).then_inc(copied, 1)

                    exps(0)
                    exps(1)
                    for u in range(8):
                        copies(u)
                        if u + 2 < 8:
                            exps(u + 2)
                    act.wait_ge(weighed, 4 * (p + 1))
                    act.activation(y[:, p, :], o[:, :], ACT.Copy).then_inc(stored, 1)
                rounds(act, pairs, body, q)

            @block.vector
            def _(dve):
                dve.memset(qz[:, :, :], 0.0).then_inc(zeroed, 1)
                dve.memset(vz[:, :, :, :], 0.0).then_inc(zeroed, 1)
                dve.memset(vrow[:, :], 0.0).then_inc(zeroed, 1)
                dve.wait_ge(zeroed, 3)
                q = InOrder(dve, chain)

                def body(p, first):
                    if forget is not None:
                        if not first:
                            dve.wait_ge(scored, 8 * p)
                        for h in range(2):
                            at = TABLE_AT["pick"][0]
                            dve.tensor_copy(pick[:, h, :], c.table[:, bass.ds(at + (2 * p + h) * P, P)]).then_inc(picked, 1)
                    if rope:
                        if not first:
                            dve.wait_ge(scored, 8 * p)
                        for part, (raw, src) in enumerate(((qr, 3), (kr, 0))):
                            dve.wait_ge(turned, 2 * p + part + 1)
                            q(dve.tensor_tensor(rq[:, :], sc[:, src, :], c.tab("sin"), ALU.mult))
                            q(dve.tensor_tensor(raw[:, :], raw[:, :], c.tab("cos"), ALU.mult))
                            if part == 0:
                                for h in range(2):
                                    half = slice(64 * h, 64 * h + 64)
                                    dve.tensor_tensor(qz[half, h, :], raw[half, :], rq[half, :], ALU.add).then_inc(q_ready, 1)
                                dve.wait_ge(q_ready, 2 * (p + 1))
                            else:
                                dve.tensor_tensor(kk[:, :], raw[:, :], rq[:, :], ALU.add).then_inc(k_ready, 1)

                    def maxima(u):
                        n = len(spans[u // 2]) * P
                        dve.wait_ge(scored, 8 * p + u + 1)
                        q(dve.tensor_reduce(top[:, u:u + 1], sc[:, u % 4, 0:n], AX_X, ALU.max))
                        if sinks is None:
                            dve.tensor_scalar(nmax[:, u:u + 1], top[:, u:u + 1], -scale, None, ALU.mult).then_inc(maxed, 1)
                        else:
                            q(dve.tensor_scalar(top[:, u:u + 1], top[:, u:u + 1], scale, sinks(2 * p + u % 2), ALU.mult, ALU.max))
                            dve.tensor_scalar(nmax[:, u:u + 1], top[:, u:u + 1], -1.0, None, ALU.mult).then_inc(maxed, 1)

                    def normalise(u):
                        n = len(spans[u // 2]) * P
                        dve.wait_ge(exped, 8 * p + u + 1)
                        if sinks is not None:
                            q(dve.tensor_tensor(rsum[:, u:u + 1], rsum[:, u:u + 1], esink[:, u:u + 1], ALU.add))
                        q(dve.reciprocal(rinv[:, u:u + 1], rsum[:, u:u + 1]))
                        dve.tensor_scalar(prob[:, u % 2, 0:n], prob[:, u % 2, 0:n], rinv[:, u:u + 1], None,
                                          ALU.mult).then_inc(normed, 1)

                    maxima(0)
                    maxima(1)
                    for u in range(8):
                        normalise(u)
                        if u + 2 < 8:
                            maxima(u + 2)
                rounds(dve, pairs, body, q)


def forget_rows(c, name, x, w_d, out, bias):
    nc = c.nc
    with Stage(nc, name) as st:
        w, row, neg = st.sb("w", [P, D]), st.sb("row", [P, S]), st.sb("neg", [P, S])
        acc = st.ps("acc", [P, S])
        landed, achain, chain = st.sem("landed"), st.sem("achain"), st.sem("chain")
        steps = Steps(st.sem("steps"), "made biased least soft done")
        with nc.Block() as block:
            @block.sync
            def _(sp):
                sp.dma_start(w[:, :], w_d).then_inc(landed, 16)

            @block.tensor
            def _(pe):
                pe.wait_ge(landed, 16)
                for k in range(DT):
                    last = pe.matmul(acc[:, :], w[:, tile_cols(k)], x[:, k, :], start=k == 0, stop=k == DT - 1)
                steps.done(last, "made")

            @block.scalar
            def _(act):
                q = InOrder(act, achain)
                steps.wait(act, "made")
                steps.done(act.activation(row[:, :], acc[:, :], ACT.Identity, bias=bias), "biased")
                steps.wait(act, "least")
                q(act.activation(row[:, :], row[:, :], ACT.Abs))
                q(act.activation(row[:, :], row[:, :], ACT.Exp, scale=-1.0))
                steps.done(act.activation(row[:, :], row[:, :], ACT.Ln, bias=1.0), "soft")

            @block.vector
            def _(dve):
                q = InOrder(dve, chain)
                steps.wait(dve, "biased")
                steps.done(dve.tensor_scalar(neg[:, :], row[:, :], 0.0, None, ALU.min), "least")
                steps.wait(dve, "soft")
                q(dve.tensor_tensor(neg[:, :], neg[:, :], row[:, :], ALU.subtract))
                q(dve.tensor_scalar(neg[:, :], neg[:, :], -8.0, None, ALU.mult))
                q(dve.memset(row[:, :], 1.0))
                q(dve.memset(out[:, :], 0.0))
                steps.done(dve.tensor_tensor_scan(out[0:16, :], row[0:16, :], neg[0:16, :], 0.0, ALU.mult, ALU.add), "done")


def log_sigmoid_act(act, q, u, v):
    q(act.activation(u, v, ACT.Abs))
    q(act.activation(u, u, ACT.Exp, scale=-1.0))
    return act.activation(u, u, ACT.Ln, bias=1.0)


def linear_recurrence(c, name, x, w_d, heads, y, kind, norm_g, qb=None, fb=None, vb_d=None, ogb=None, lb=None,
                      small=None, fup_d=None):
    nc = c.nc
    gla = kind == "gla"
    with Stage(nc, name) as st:
        lower = st.sem("lower")
        w = st.sb("w", [P, 4, D])
        fup = st.sb("fup", [P, P])
        vrow = st.sb("vrow", [P, P])
        q_, f_, og, g, u, qd, kinv, kend, eg = (st.sb(n, [P, S]) for n in ("q", "f", "og", "g", "u", "qd", "kinv", "kend", "eg"))
        v = st.sb("v", [P, TT, P])
        a = st.sb("a", [P, TT, P])
        kt = st.sb("kt", [P, 2, TT, P])
        state = st.sb("state", [P, NC, P])
        lbc, olb = st.sb("lbc", [P, 8]), st.sb("olb", [P, 8])
        b = [st.ps(f"b{i}", [P, S]) for i in range(8)]
        landed, zeroed, achain, chain = st.sem("landed"), st.sem("zeroed"), st.sem("achain"), st.sem("chain")
        steps = Steps(st.sem("steps"),
                      "projected activated gated logged summed decays folded scored masked kcopied updated "
                      "states mixed squared meaned rooted stored")
        loads = 2
        with nc.Block() as block:
            @block.sync
            def _(sp):
                if not gla:
                    sp.wait_ge(zeroed, 2)

                def body(h, first):
                    if not first:
                        steps.wait(sp, "projected", h - 1)
                    sp.dma_start(w[:, :, :], w_d[h]).then_inc(landed, 16)
                    if gla:
                        sp.dma_start(fup[:, :], fup_d[h]).then_inc(landed, 16)
                    else:
                        sp.dma_start(vrow[0:1, :], vb_d[h]).then_inc(landed, 16)
                rounds(sp, heads, body)

            @block.tensor
            def _(pe):
                def body(h, first):
                    pe.wait_ge(landed, 16 * loads * (h + 1))
                    if not first:
                        steps.wait_round(pe, h)
                    for part in (0, 1, 3):
                        for k in range(DT):
                            pe.matmul(b[part][:, :], w[:, part, tile_cols(k)], x[:, k, :], start=k == 0, stop=k == DT - 1)
                    if gla:
                        pe.matmul(b[4][:, :], fup[:, :], small[:, :], start=True, stop=True)
                    for t in range(TT):
                        for k in range(DT):
                            last = pe.matmul(b[2][:, tile_cols(t)], x[:, k, tile_cols(t)], w[:, 2, tile_cols(k)],
                                             start=k == 0, stop=k == DT - 1 and gla)
                        if not gla:
                            last = pe.matmul(b[2][:, tile_cols(t)], c.tab("ones"), vrow[:, :], start=False, stop=True)
                    steps.done(last, "projected")
                    steps.wait(pe, "folded", h)
                    for t in range(TT):
                        pe.matmul(b[5][:, tile_cols(t)], kinv[:, tile_cols(t)], qd[:, tile_cols(t)], start=True, stop=True)
                    for t in range(TT):
                        last = pe.transpose(b[6][:, tile_cols(t)], kend[:, tile_cols(t)], c.tab("ident"))
                    steps.done(last, "scored")
                    steps.wait(pe, "kcopied", h)
                    for n in range(NC - 1):
                        last = pe.matmul(b[n // 4][:, tile_cols(n % 4)], kt[:, n % 2, n // 2, :], v[:, n // 2, :],
                                         start=True, stop=True)
                    steps.done(last, "updated")
                    steps.wait(pe, "states", h)
                    for t in range(TT):
                        pe.matmul(b[3][:, tile_cols(t)], v[:, t, :], a[:, t, :], start=True, stop=False)
                        for n in (2 * t, 2 * t + 1):
                            if n:
                                last = pe.matmul(b[3][:, n * CHUNK:(n + 1) * CHUNK], state[:, n, :],
                                                 qd[:, n * CHUNK:(n + 1) * CHUNK], start=False, stop=n % 2 == 1)
                    steps.done(last, "mixed")
                    steps.wait(pe, "squared", h)
                    steps.done(pe.matmul(b[7][:, :], c.tab("ones"), u[:, :], start=True, stop=True), "meaned")
                rounds(pe, heads, body)

            @block.scalar
            def _(act):
                act.wait_ge(zeroed, 2)
                q = InOrder(act, achain)
                if not gla:
                    act.wait_ge(lower, 1)
                    act.activation(lbc[:, :], olb[:, :], ACT.Sigmoid).then_inc(lower, 1)

                def body(h, first):
                    steps.wait(act, "projected", h)
                    q(act.activation(v[:, :, :], b[2][:, :].rearrange("p (t f) -> p t f", t=TT), ACT.Copy))
                    if gla:
                        q(act.activation(og[:, :], b[3][:, :], ACT.Silu))
                        q(act.activation(q_[:, :], b[0][:, :], ACT.Copy, scale=0.125))
                        q(act.activation(kinv[:, :], b[1][:, :], ACT.Copy))
                        q(act.activation(f_[:, :], b[4][:, :], ACT.Identity, bias=fb(h)))
                        steps.done(log_sigmoid_act(act, q, u[:, :], f_[:, :]), "activated")
                    else:
                        q(act.activation(og[:, :], b[3][:, :], ACT.Silu, bias=ogb(h)))
                        q(act.activation(q_[:, :], b[0][:, :], ACT.Silu, bias=qb(h)))
                        steps.done(act.activation(f_[:, :], b[1][:, :], ACT.Sigmoid, bias=fb(h)), "activated")
                    steps.wait(act, "gated", h)
                    if gla:
                        steps.done(act.activation(g[:, :], f_[:, :], ACT.Copy, scale=1.0 / 16), "logged")
                    else:
                        steps.done(act.activation(g[:, :], f_[:, :], ACT.Ln), "logged")
                    steps.wait(act, "summed", h)
                    q(act.activation(u[:, :], g[:, :], ACT.Exp, scale=-1.0))
                    steps.done(act.activation(eg[:, :], g[:, :], ACT.Exp), "decays")
                    steps.wait(act, "masked", h)
                    for half in range(2):
                        rows = slice(64 * half, 64 * half + 64)
                        last = act.activation(kt[rows, half, :, :], b[6][rows, :].rearrange("p (t f) -> p t f", t=TT), ACT.Copy)
                        if half == 0:
                            q(last)
                    steps.done(last, "kcopied")
                    steps.wait(act, "mixed", h)
                    steps.done(act.activation(u[:, :], b[3][:, :], ACT.Square), "squared")
                    steps.wait(act, "meaned", h)
                    q(act.activation(g[:, :], b[7][:, :], ACT.Copy, scale=1.0 / P, bias=1e-6))
                    steps.done(act.activation(g[:, :], g[:, :], ACT.Sqrt), "rooted")
                rounds(act, heads, body, q)

            @block.vector
            def _(dve):
                dve.memset(kt[:, :, :, :], 0.0).then_inc(zeroed, 1)
                dve.memset(vrow[:, :], 0.0).then_inc(zeroed, 1)
                q = InOrder(dve, chain)

                def body(h, first):
                    steps.wait(dve, "activated", h)
                    if gla:
                        q(dve.tensor_scalar(f_[:, :], f_[:, :], 0.0, None, ALU.min))
                        steps.done(dve.tensor_tensor(f_[:, :], f_[:, :], u[:, :], ALU.subtract), "gated")
                    else:
                        q(dve.tensor_scalar(f_[:, :], f_[:, :], olb_at(h), lbc_at(h), ALU.mult, ALU.add))
                        steps.done(dve.tensor_scalar(kinv[:, :], f_[:, :], -1.0, 1.0, ALU.mult, ALU.add), "gated")
                    steps.wait(dve, "logged", h)
                    steps.done(dve.tensor_tensor_scan(g[:, :], c.tab("restart"), g[:, :], 0.0, ALU.mult, ALU.add), "summed")
                    steps.wait(dve, "decays", h)
                    q(dve.tensor_tensor(qd[:, :], q_[:, :], eg[:, :], ALU.mult))
                    q(dve.tensor_tensor(kinv[:, :], kinv[:, :], u[:, :], ALU.mult))
                    chunked = "p (n t) -> p n t"
                    ends = eg[:, :].rearrange(chunked, n=NC)[:, :, CHUNK - 1:CHUNK].broadcast_to([P, NC, CHUNK])
                    steps.done(dve.tensor_tensor(kend[:, :].rearrange(chunked, n=NC), kinv[:, :].rearrange(chunked, n=NC),
                                                 ends, ALU.mult), "folded")
                    steps.wait(dve, "scored", h)
                    mask = c.tab("causal_chunk").rearrange("p (o t) -> p o t", o=1).broadcast_to([P, TT, P])
                    steps.done(dve.tensor_tensor(a[:, :, :], b[5][:, :].rearrange("p (t f) -> p t f", t=TT), mask, ALU.mult), "masked")
                    steps.wait(dve, "updated", h)
                    q(dve.tensor_copy(state[:, 1, :], b[0][:, 0:P]))
                    for n in range(1, NC - 1):
                        last = dve.scalar_tensor_tensor(state[:, n + 1, :], state[:, n, :], eg[:, (n + 1) * CHUNK - 1:(n + 1) * CHUNK],
                                                        b[n // 4][:, tile_cols(n % 4)], ALU.mult, ALU.add)
                        if n < NC - 2:
                            q(last)
                    steps.done(last, "states")
                    steps.wait(dve, "rooted", h)
                    q(dve.reciprocal(g[:, :], g[:, :]))
                    q(dve.scalar_tensor_tensor(g[:, :], g[:, :], norm_g, og[:, :], ALU.mult, ALU.mult))
                    steps.done(dve.tensor_tensor(y[:, h, :], g[:, :], b[3][:, :], ALU.mult), "stored")

                def lbc_at(h):
                    return lbc[:, bass.ds(h, 1)]

                def olb_at(h):
                    return olb[:, bass.ds(h, 1)]

                if not gla:
                    dve.tensor_tensor(olb[:, :], lb[:, 0:8], lb[:, 8:16], ALU.subtract).then_inc(lower, 1)
                    dve.wait_ge(lower, 2)
                    q(dve.tensor_scalar(olb[:, :], lbc[:, :], -1.0, 1.0, ALU.mult, ALU.add))
                rounds(dve, heads, body, q)


def causal_conv(dve, q, out, pad, taps, weight, bias):
    q(dve.tensor_scalar(out, pad[:, 0:S], weight(0), bias, ALU.mult, ALU.add))
    for i in range(1, taps):
        q(dve.scalar_tensor_tensor(out, pad[:, i:i + S], weight(i), out, ALU.mult, ALU.add))


def mlstm(c, name, x, w_d, heads, y, small):
    nc = c.nc
    with Stage(nc, name) as st:
        w = st.sb("w", [P, 4, D])
        pick = st.sb("pick", [P, 2, P])
        pad, qk = st.sb("pad", [P, 2, S + 3]), st.sb("qk", [P, 2, S])
        v, og = st.sb("v", [P, TT, P]), st.sb("og", [P, S])
        li, lf, u, bsum, a, top, em, hh, one = (st.sb(n, [P, S]) for n in ("li", "lf", "u", "bsum", "a", "top", "em", "hh", "one"))
        diag, acol = st.sb("diag", [P, P]), st.sb("acol", [P, TT])
        e = st.sb("e", [P, TT, S])
        b = [st.ps(f"b{i}", [P, S]) for i in range(7)]
        landed, zeroed, achain, chain = st.sem("landed"), st.sem("zeroed"), st.sem("achain"), st.sem("chain")
        steps = Steps(st.sem("steps"), "picked projected taken gates exps scored weighted mixed absden divided "
                                       "squared meaned rooted stored")
        with nc.Block() as block:
            @block.sync
            def _(sp):
                def body(h, first):
                    if not first:
                        steps.wait(sp, "projected", h - 1)
                    sp.dma_start(w[:, :, :], w_d[h]).then_inc(landed, 16)
                rounds(sp, heads, body)

            @block.tensor
            def _(pe):
                def body(h, first):
                    pe.wait_ge(landed, 16 * (h + 1))
                    steps.wait(pe, "picked", h)
                    for part in (0, 1, 3):
                        for k in range(DT):
                            pe.matmul(b[part][:, :], w[:, part, tile_cols(k)], x[:, k, :], start=k == 0, stop=k == DT - 1)
                    for n in range(2):
                        pe.matmul(b[4 + n][:, :], pick[:, n, :], small[:, :], start=True, stop=True)
                    for t in range(TT):
                        for k in range(DT):
                            last = pe.matmul(b[2][:, tile_cols(t)], x[:, k, tile_cols(t)], w[:, 2, tile_cols(k)],
                                             start=k == 0, stop=k == DT - 1)
                    steps.done(last, "projected")
                    steps.wait(pe, "exps", h)
                    for j in range(TT):
                        last = pe.matmul(b[j][:, 0:S - j * P], qk[:, 1, tile_cols(j)], qk[:, 0, j * P:S], start=True, stop=True)
                    steps.done(last, "scored")
                    steps.wait(pe, "weighted", h)
                    for out, lhs in ((b[4], v), (b[5], None)):
                        for j in range(TT):
                            last = pe.matmul(out[:, j * P:S], c.tab("ones") if lhs is None else lhs[:, j, :],
                                             e[:, j, 0:S - j * P], start=j == 0, stop=j == TT - 1)
                    steps.done(last, "mixed")
                    steps.wait(pe, "squared", h)
                    steps.done(pe.matmul(b[6][:, :], c.tab("ones"), u[:, :], start=True, stop=True), "meaned")
                rounds(pe, heads, body)

            @block.scalar
            def _(act):
                act.wait_ge(zeroed, 2)
                q = InOrder(act, achain)

                def body(h, first):
                    steps.wait(act, "projected", h)
                    for n in range(2):
                        q(act.activation(pad[:, n, 3:], b[n][:, :], ACT.Copy))
                    q(act.activation(v[:, :, :], b[2][:, :].rearrange("p (t f) -> p t f", t=TT), ACT.Copy))
                    q(act.activation(og[:, :], b[3][:, :], ACT.Sigmoid))
                    q(act.activation(li[:, :], b[4][:, :], ACT.Identity, bias=c.col("ml_ib", h)))
                    q(act.activation(lf[:, :], b[5][:, :], ACT.Identity, bias=c.col("ml_fb", h)))
                    steps.done(log_sigmoid_act(act, q, u[:, :], lf[:, :]), "taken")
                    steps.wait(act, "gates", h)
                    for n in range(2):
                        q(act.activation(qk[:, n, :], qk[:, n, :], ACT.Silu))
                    q(act.activation(em[:, :], em[:, :], ACT.Exp, scale=-1.0))
                    for j in range(TT):
                        last = act.activation(e[:, j, 0:S - j * P], e[:, j, 0:S - j * P], ACT.Exp, bias=acol[:, j:j + 1])
                        if j < TT - 1:
                            q(last)
                    steps.done(last, "exps")
                    steps.wait(act, "mixed", h)
                    steps.done(act.activation(u[:, :], b[5][:, :], ACT.Abs), "absden")
                    steps.wait(act, "divided", h)
                    steps.done(act.activation(u[:, :], hh[:, :], ACT.Square), "squared")
                    steps.wait(act, "meaned", h)
                    q(act.activation(u[:, :], b[6][:, :], ACT.Copy, scale=1.0 / P, bias=1e-6))
                    steps.done(act.activation(u[:, :], u[:, :], ACT.Sqrt), "rooted")
                rounds(act, heads, body, q)

            @block.vector
            def _(dve):
                dve.memset(pad[:, :, 0:3], 0.0).then_inc(zeroed, 1)
                dve.memset(one[:, :], 1.0).then_inc(zeroed, 1)
                dve.wait_ge(zeroed, 2)
                q = InOrder(dve, chain)

                def body(h, first):
                    at = TABLE_AT["pick"][0]
                    if not first:
                        steps.wait_round(dve, h)
                    q(dve.tensor_copy(pick[:, 0, :], c.table[:, bass.ds(at + h * P, P)]))
                    steps.done(dve.tensor_copy(pick[:, 1, :], c.table[:, bass.ds(at + (4 + h) * P, P)]), "picked")
                    steps.wait(dve, "taken", h)
                    for n in range(2):
                        causal_conv(dve, q, qk[:, n, :], pad[:, n, :], 4, lambda i: c.col("ml_cw", h * 8 + n * 4 + i),
                                    c.col("ml_cb", h * 2 + n))
                    q(dve.tensor_scalar(lf[:, :], lf[:, :], 0.0, None, ALU.min))
                    q(dve.tensor_tensor(lf[:, :], lf[:, :], u[:, :], ALU.subtract))
                    q(dve.tensor_tensor_scan(bsum[:, :], one[:, :], lf[:, :], 0.0, ALU.mult, ALU.add))
                    q(dve.tensor_tensor(a[:, :], li[:, :], bsum[:, :], ALU.subtract))
                    q(dve.tensor_tensor_scan(top[:, :], one[:, :], a[:, :], 0.0, ALU.mult, ALU.max))
                    for j in range(TT):
                        q(dve.tensor_tensor_reduce(diag[:, :], a[:, tile_cols(j)], c.tab("ident"), 1.0, 0.0, ALU.mult,
                                                   ALU.add, acol[:, j:j + 1]))
                        q(dve.tensor_tensor(e[:, j, 0:S - j * P], c.tab("mask_after")[:, 0:S - j * P], top[:, j * P:S], ALU.subtract))
                    steps.done(dve.tensor_tensor(em[:, :], bsum[:, :], top[:, :], ALU.add), "gates")
                    steps.wait(dve, "scored", h)
                    for j in range(TT):
                        ej = e[:, j, 0:S - j * P]
                        last = dve.scalar_tensor_tensor(ej, b[j][:, 0:S - j * P], 0.125, ej, ALU.mult, ALU.mult)
                        if j < TT - 1:
                            q(last)
                    steps.done(last, "weighted")
                    steps.wait(dve, "absden", h)
                    q(dve.tensor_tensor(hh[:, :], u[:, :], em[:, :], ALU.max))
                    q(dve.reciprocal(hh[:, :], hh[:, :]))
                    steps.done(dve.tensor_tensor(hh[:, :], hh[:, :], b[4][:, :], ALU.mult), "divided")
                    steps.wait(dve, "rooted", h)
                    q(dve.reciprocal(u[:, :], u[:, :]))
                    q(dve.scalar_tensor_tensor(u[:, :], u[:, :], c.col("ml_ng", h), og[:, :], ALU.mult, ALU.mult))
                    steps.done(dve.tensor_tensor(y[:, h, :], u[:, :], hh[:, :], ALU.mult), "stored")
                rounds(dve, heads, body, q)


def ssd(c, name, x, w_d, y, small):
    nc = c.nc
    with Stage(nc, name) as st:
        w = st.sb("w", [P, 4, D])
        pick = st.sb("pick", [P, 2, P])
        pad, conv = st.sb("pad", [P, 3, S + 3]), st.sb("conv", [P, 3, S])
        z, one, la = st.sb("z", [P, S]), st.sb("one", [P, S]), st.sb("la", [P, 2, S])
        dt, u = st.sb("dt", [P, 2, S]), st.sb("u", [P, 2, S])
        rate, acol, dcol = st.sb("rate", [P, 2]), st.sb("acol", [P, 2, TT]), st.sb("dcol", [P, 2, TT])
        diag = st.sb("diag", [P, P])
        e = st.sb("e", [P, 2, TT, S])
        xz = st.sb("xz", [P, 2, TT, P])
        b = [st.ps(f"b{i}", [P, S]) for i in range(6)]
        landed, zeroed, achain, chain = st.sem("landed"), st.sem("zeroed"), st.sem("achain"), st.sem("chain")
        steps = Steps(st.sem("steps"), "picked projected taken convolved activated turned scans exps weighted mixed stored")
        with nc.Block() as block:
            @block.sync
            def _(sp):
                def body(i, first):
                    if not first:
                        steps.wait(sp, "projected", i - 1)
                    sp.dma_start(w[:, :, :], w_d[i]).then_inc(landed, 16)
                rounds(sp, 4, body)

            @block.tensor
            def _(pe):
                def body(i, first):
                    pe.wait_ge(landed, 16 * (i + 1))
                    steps.wait(pe, "picked", i)
                    for part in range(4):
                        for k in range(DT):
                            pe.matmul(b[part][:, :], w[:, part, tile_cols(k)], x[:, k, :], start=k == 0, stop=k == DT - 1)
                    for h in range(2):
                        last = pe.matmul(b[4 + h][:, :], pick[:, h, :], small[:, :], start=True, stop=True)
                    steps.done(last, "projected")
                    steps.wait(pe, "activated", i)
                    for t in range(TT):
                        pe.transpose(b[0][:, tile_cols(t)], conv[:, 0, tile_cols(t)], c.tab("ident"))
                    for j in range(TT):
                        last = pe.matmul(b[1 + j][:, 0:S - j * P], conv[:, 1, tile_cols(j)], conv[:, 2, j * P:S], start=True, stop=True)
                    steps.done(last, "turned")
                    steps.wait(pe, "weighted", i)
                    for h in range(2):
                        for j in range(TT):
                            last = pe.matmul(b[5][:, j * P:S], xz[:, h, j, :], e[:, h, j, 0:S - j * P],
                                             start=h == 0 and j == 0, stop=h == 1 and j == TT - 1)
                    steps.done(last, "mixed")
                rounds(pe, 4, body)

            @block.scalar
            def _(act):
                act.wait_ge(zeroed, 3)
                q = InOrder(act, achain)

                def body(i, first):
                    steps.wait(act, "projected", i)
                    for n, part in enumerate((0, 2, 3)):
                        q(act.activation(pad[:, n, 3:], b[part][:, :], ACT.Copy))
                    q(act.activation(z[:, :], b[1][:, :], ACT.Silu))
                    for h in range(2):
                        q(act.activation(dt[:, h, :], b[4 + h][:, :], ACT.Identity, bias=c.col("sd_dtb", 2 * i + h)))
                        last = log_sigmoid_act(act, q, u[:, h, :], dt[:, h, :])
                        if h == 0:
                            q(last)
                    steps.done(last, "taken")
                    steps.wait(act, "convolved", i)
                    q(act.activation(rate[:, 0:1], c.col("sd_alog", 2 * i), ACT.Exp))
                    q(act.activation(rate[:, 1:2], c.col("sd_alog", 2 * i + 1), ACT.Exp))
                    steps.done(act.activation(conv[:, :, :], conv[:, :, :], ACT.Silu), "activated")
                    steps.wait(act, "scans", i)
                    for h in range(2):
                        for j in range(TT):
                            last = act.activation(e[:, h, j, 0:S - j * P], e[:, h, j, 0:S - j * P], ACT.Exp, bias=acol[:, h, j:j + 1])
                            if (h, j) != (1, TT - 1):
                                q(last)
                    steps.done(last, "exps")
                rounds(act, 4, body, q)

            @block.vector
            def _(dve):
                dve.memset(pad[:, :, 0:3], 0.0).then_inc(zeroed, 1)
                dve.memset(one[:, :], 1.0).then_inc(zeroed, 1)
                dve.memset(xz[:, :, :, :], 0.0).then_inc(zeroed, 1)
                dve.wait_ge(zeroed, 3)
                q = InOrder(dve, chain)

                def body(i, first):
                    at = TABLE_AT["pick"][0]
                    if not first:
                        steps.wait_round(dve, i)
                    q(dve.tensor_copy(pick[:, 0, :], c.table[:, bass.ds(at + (8 + 2 * i) * P, P)]))
                    steps.done(dve.tensor_copy(pick[:, 1, :], c.table[:, bass.ds(at + (9 + 2 * i) * P, P)]), "picked")
                    steps.wait(dve, "taken", i)
                    causal_conv(dve, q, conv[:, 0, :], pad[:, 0, :], 4, lambda k: c.col("sd_cwx", i * 4 + k), c.col("sd_cbx", i))
                    for n in range(2):
                        causal_conv(dve, q, conv[:, 1 + n, :], pad[:, 1 + n, :], 4,
                                    lambda k: c.col("sd_cwbc", i * 8 + n * 4 + k), c.col("sd_cbbc", i * 2 + n))
                    q(dve.tensor_scalar(dt[:, :, :], dt[:, :, :], 0.0, None, ALU.max))
                    steps.done(dve.tensor_tensor(dt[:, :, :], dt[:, :, :], u[:, :, :], ALU.add), "convolved")
                    steps.wait(dve, "turned", i)
                    for h in range(2):
                        q(dve.tensor_scalar(la[:, h, :], dt[:, h, :], rate[:, h:h + 1], -1.0, ALU.mult, ALU.mult))
                        for j in range(TT):
                            ej = e[:, h, j, 0:S - j * P]
                            q(dve.tensor_tensor_scan(ej, one[:, 0:S - j * P], la[:, h, j * P:S], 0.0, ALU.mult, ALU.add))
                            q(dve.tensor_tensor_reduce(diag[:, :], ej[:, 0:P], c.tab("ident"), -1.0, 0.0, ALU.mult, ALU.add,
                                                       acol[:, h, j:j + 1]))
                            q(dve.tensor_tensor_reduce(diag[:, :], dt[:, h, tile_cols(j)], c.tab("ident"), 1.0, 0.0, ALU.mult,
                                                       ALU.add, dcol[:, h, j:j + 1]))
                            last = dve.tensor_tensor(ej[:, 0:P], ej[:, 0:P], c.tab("mask_after")[:, 0:P], ALU.add)
                            if (h, j) != (1, TT - 1):
                                q(last)
                    steps.done(last, "scans")
                    steps.wait(dve, "exps", i)
                    for h in range(2):
                        for j in range(TT):
                            ej = e[:, h, j, 0:S - j * P]
                            q(dve.tensor_tensor(ej, ej, b[1 + j][:, 0:S - j * P], ALU.mult))
                            last = dve.tensor_scalar(xz[:, h, j, 64 * h:64 * h + 64], b[0][:, j * P + 64 * h:j * P + 64 * h + 64],
                                                     dcol[:, h, j:j + 1], None, ALU.mult)
                            if (h, j) != (1, TT - 1):
                                q(last)
                    steps.done(last, "weighted")
                    steps.wait(dve, "mixed", i)
                    q(dve.scalar_tensor_tensor(conv[:, 0, :], conv[:, 0, :], c.col("sd_d", i), b[5][:, :], ALU.mult, ALU.add))
                    steps.done(dve.tensor_tensor(y[:, i, :], conv[:, 0, :], z[:, :], ALU.mult), "stored")
                rounds(dve, 4, body, q)


def rwkv(c, name, x, w_d, up_d, y, lora):
    nc = c.nc
    with Stage(nc, name) as st:
        w, up = st.sb("w", [P, 3, D]), st.sb("up", [P, 3, P])
        pad = st.sb("pad", [P, 3, S + 1])
        rkv = st.sb("rkv", [P, 3, S])
        ld, g, gp, aa, kn, tmp, gg, rhat, ahat, winv, wfull = (
            st.sb(n, [P, S]) for n in ("ld", "g", "gp", "aa", "kn", "tmp", "gg", "rhat", "ahat", "winv", "wfull"))
        bhat, khat = st.sb("bhat", [P, 3, S]), st.sb("khat", [P, 3, S])
        bt, kt = st.sb("bt", [P, 2, TT, P]), st.sb("kt", [P, 2, TT, P])
        vz, saz = st.sb("vz", [P, 2, TT, P]), st.sb("saz", [P, 2, TT, P])
        mt, nt, rb, rk = (st.sb(n, [P, 2, TT, P]) for n in ("mt", "nt", "rb", "rk"))
        tri, inv, part, level = (st.sb(n, [P, TT, P]) for n in ("tri", "inv", "part", "level"))
        invs = st.sb("invs", [P, 2, TT, P])
        xs = st.sb("xs", [P, P])
        state = st.sb("state", [P, NC + 1, P])
        upd = st.sb("upd", [P, P])
        b = [st.ps(f"b{i}", [P, S]) for i in range(8)]
        landed, zeroed, achain, chain, pre = (st.sem(n) for n in ("landed", "zeroed", "achain", "chain", "pre"))
        names = "projected taken shifted lora_up squared normed rooted decays hats0 hats turned tcopied "
        for h in range(2):
            names += f"pair{h} pmasked{h} "
            for n in range(LEVELS):
                names += f"lev{h}_{n} part{h}_{n} lpart{h}_{n} tp{h}_{n} tri{h}_{n} "
        for n in range(NC):
            names += f"x{n} xcopied{n} sa{n} sacopied{n} up{n} state{n} "
        names += "mixed bonus meaned centred csquared varied croot scaled affine stored"
        steps = Steps(st.sem("steps"), names)
        by_tile = "p (t f) -> p t f"
        with nc.Block() as block:
            @block.sync
            def _(sp):
                def body(p, first):
                    if not first:
                        steps.wait(sp, "lora_up", p - 1)
                    sp.dma_start(w[:, :, :], w_d[p]).then_inc(landed, 16)
                    sp.dma_start(up[:, :, :], up_d[p]).then_inc(landed, 16)
                rounds(sp, 4, body)

            @block.tensor
            def _(pe):
                def body(p, first):
                    pe.wait_ge(landed, 32 * (p + 1))
                    if first:
                        pe.wait_ge(pre, 3)
                    else:
                        steps.wait_round(pe, p)
                    for n in range(3):
                        for k in range(DT):
                            last = pe.matmul(b[n][:, :], w[:, n, tile_cols(k)], x[:, k, :], start=k == 0, stop=k == DT - 1)
                    steps.done(last, "projected")
                    steps.wait(pe, "shifted", p)
                    for n in range(3):
                        last = pe.matmul(b[3 + n][:, :], up[:, n, :], lora[:, 1 if n < 2 else 2, :], start=True, stop=True)
                    steps.done(last, "lora_up")
                    steps.wait(pe, "squared", p)
                    steps.done(pe.matmul(b[6][:, :], c.tab("head_ones"), tmp[:, :], start=True, stop=True), "normed")
                    steps.wait(pe, "hats", p)
                    for n, src in enumerate((bhat[:, 0, :], khat[:, 0, :], rkv[:, 2, :])):
                        for t in range(TT):
                            last = pe.transpose(b[n][:, tile_cols(t)], src[:, tile_cols(t)], c.tab("ident"))
                    steps.done(last, "turned")
                    steps.wait(pe, "tcopied", p)
                    for h in range(2):
                        if h:
                            steps.wait(pe, f"tri0_{LEVELS - 1}", p)
                        for n, (l, r_) in enumerate(((bhat, ahat), (khat, ahat), (bhat, rhat), (khat, rhat))):
                            for t in range(TT):
                                last = pe.matmul(b[n][:, tile_cols(t)], l[:, 1 + h, tile_cols(t)], r_[:, tile_cols(t)], start=True, stop=True)
                        steps.done(last, f"pair{h}")
                        for n in range(LEVELS):
                            steps.wait(pe, f"lev{h}_{n}", p)
                            for t in range(TT):
                                last = pe.matmul(b[4][:, tile_cols(t)], level[:, t, :], tri[:, t, :], start=True, stop=True)
                            steps.done(last, f"part{h}_{n}")
                            steps.wait(pe, f"lpart{h}_{n}", p)
                            for t in range(TT):
                                pe.matmul(b[5][:, tile_cols(t)], inv[:, t, :], part[:, t, :], start=True, stop=True)
                            for t in range(TT):
                                last = pe.matmul(b[6][:, tile_cols(t)], part[:, t, :], inv[:, t, :], start=True, stop=True)
                            steps.done(last, f"tp{h}_{n}")
                    for n in range(NC):
                        t = n // 2
                        steps.wait(pe, f"state{n - 1}" if n else f"tri1_{LEVELS - 1}", p)
                        pe.matmul(b[4][:, 0:P], ahat[:, tile_cols(t)], state[:, n, :], start=True, stop=False)
                        pe.matmul(b[4][:, 0:P], nt[:, 0, t, :], vz[:, 0, t, :], start=False, stop=False)
                        steps.done(pe.matmul(b[4][:, 0:P], nt[:, 1, t, :], vz[:, 1, t, :], start=False, stop=True), f"x{n}")
                        steps.wait(pe, f"xcopied{n}", p)
                        for h in range(2):
                            last = pe.matmul(b[5][:, 64 * h:64 * h + 64], invs[:, h, t, :], xs[:, 64 * h:64 * h + 64], start=True, stop=True)
                        steps.done(last, f"sa{n}")
                        steps.wait(pe, f"sacopied{n}", p)
                        ops = [(bt, saz, 0), (bt, saz, 1), (kt, vz, 0), (kt, vz, 1)]
                        for m, (l, r_, h) in enumerate(ops):
                            last = pe.matmul(b[6][:, 0:P], l[:, n % 2, t, :], r_[:, h, t, :], start=m == 0, stop=m == 3)
                        steps.done(last, f"up{n}")
                    steps.wait(pe, f"state{NC - 1}", p)
                    for t in range(TT):
                        first_mm = True
                        for h in range(2):
                            for l, r_ in ((saz, rb), (vz, rk)):
                                pe.matmul(b[7][:, tile_cols(t)], l[:, h, t, :], r_[:, h, t, :], start=first_mm, stop=False)
                                first_mm = False
                        for n in (2 * t, 2 * t + 1):
                            cols = slice(n * CHUNK, (n + 1) * CHUNK)
                            pe.matmul(b[7][:, cols], state[:, n, :], rhat[:, cols], start=False, stop=n % 2 == 1)
                    last = pe.matmul(b[0][:, :], c.tab("head_ones"), tmp[:, :], start=True, stop=True)
                    steps.done(last, "mixed")
                    steps.wait(pe, "bonus", p)
                    steps.done(pe.matmul(b[1][:, :], c.tab("head_ones"), kn[:, :], start=True, stop=True), "meaned")
                    steps.wait(pe, "csquared", p)
                    steps.done(pe.matmul(b[2][:, :], c.tab("head_ones"), tmp[:, :], start=True, stop=True), "varied")
                rounds(pe, 4, body)

            @block.scalar
            def _(act):
                q = InOrder(act, achain)
                act.wait_ge(pre, 1)
                act.activation(lora[0:64, 1, :], lora[0:64, 1, :], ACT.Tanh).then_inc(pre, 1)
                act.activation(lora[:, 2, :], lora[:, 2, :], ACT.Sigmoid).then_inc(pre, 1)

                def body(p, first):
                    steps.wait(act, "projected", p)
                    for n in range(3):
                        last = act.activation(pad[:, n, 1:], b[n][:, :], ACT.Copy)
                        if n < 2:
                            q(last)
                    steps.done(last, "taken")
                    steps.wait(act, "lora_up", p)
                    q(act.activation(ld[:, :], b[3][:, :], ACT.Sigmoid, bias=c.col("w0", p)))
                    q(act.activation(aa[:, :], b[4][:, :], ACT.Sigmoid, bias=c.col("a0", p)))
                    q(act.activation(gg[:, :], b[5][:, :], ACT.Copy))
                    q(act.activation(kn[:, :], rkv[:, 1, :], ACT.Copy, scale=c.col("k_k", p)))
                    steps.done(act.activation(tmp[:, :], kn[:, :], ACT.Square), "squared")
                    steps.wait(act, "normed", p)
                    steps.done(act.activation(tmp[:, :], b[6][:, :], ACT.Sqrt), "rooted")
                    steps.wait(act, "decays", p)
                    q(act.activation(winv[:, :], g[:, :], ACT.Exp, scale=-1.0))
                    q(act.activation(wfull[:, :], g[:, :], ACT.Exp))
                    steps.done(act.activation(gp[:, :], gp[:, :], ACT.Exp), "hats0")
                    steps.wait(act, "turned", p)
                    for dst, n in ((bt, 0), (kt, 1)):
                        for half in range(2):
                            rows = slice(64 * half, 64 * half + 64)
                            q(act.activation(dst[rows, half, :, :], b[n][rows, :].rearrange(by_tile, t=TT), ACT.Copy))
                    for h in range(2):
                        cols = slice(64 * h, 64 * h + 64)
                        last = act.activation(vz[:, h, :, cols], b[2][:, :].rearrange(by_tile, t=TT)[:, :, cols], ACT.Copy)
                        if h == 0:
                            q(last)
                    steps.done(last, "tcopied")
                    for h in range(2):
                        for n in range(LEVELS):
                            steps.wait(act, f"part{h}_{n}", p)
                            steps.done(act.activation(part[:, :, :], b[4][:, :].rearrange(by_tile, t=TT), ACT.Copy), f"lpart{h}_{n}")
                    for n in range(NC):
                        rows = slice(64 * (n % 2), 64 * (n % 2) + 64)
                        steps.wait(act, f"x{n}", p)
                        steps.done(act.activation(xs[rows, :], b[4][rows, 0:P], ACT.Copy, scale=-1.0), f"xcopied{n}")
                        steps.wait(act, f"sa{n}", p)
                        q(act.activation(saz[:, 0, n // 2, 0:64], b[5][:, 0:64], ACT.Copy))
                        steps.done(act.activation(saz[:, 1, n // 2, 64:128], b[5][:, 64:128], ACT.Copy), f"sacopied{n}")
                    steps.wait(act, "centred", p)
                    steps.done(act.activation(tmp[:, :], kn[:, :], ACT.Square), "csquared")
                    steps.wait(act, "varied", p)
                    q(act.activation(g[:, :], b[2][:, :], ACT.Copy, scale=1.0 / 64, bias=64e-5))
                    steps.done(act.activation(g[:, :], g[:, :], ACT.Sqrt), "croot")
                    steps.wait(act, "scaled", p)
                    steps.done(act.activation(kn[:, :], kn[:, :], ACT.Identity, scale=c.col("gn_g", p), bias=c.col("gn_b", p)), "affine")
                rounds(act, 4, body, q)

            @block.vector
            def _(dve):
                q = InOrder(dve, chain)
                q(dve.memset(pad[:, :, 0:1], 0.0))
                for n in (1, 2):
                    q(dve.tensor_tensor(tmp[:, 1:S], lora[:, n, 0:S - 1], lora[:, n, 1:S], ALU.subtract))
                    q(dve.tensor_scalar(tmp[:, 0:1], lora[:, n, 0:1], -1.0, None, ALU.mult))
                    q(dve.scalar_tensor_tensor(lora[:, n, :], tmp[:, :], c.col("lora_mu", n - 1), lora[:, n, :], ALU.mult, ALU.add))
                for buf in (bhat, khat):
                    q(dve.memset(buf[:, :, :], 0.0))
                for buf in (bt, kt, vz, saz):
                    q(dve.memset(buf[:, :, :, :], 0.0))
                q(dve.memset(state[:, 0, :], 0.0))
                dve.memset(xs[:, :], 0.0).then_inc(pre, 1)

                def body(p, first):
                    steps.wait(dve, "taken", p)
                    for n, mu in enumerate(("r_mu", "k_mu", "v_mu")):
                        q(dve.tensor_tensor(rkv[:, n, :], pad[:, n, 0:S], pad[:, n, 1:S + 1], ALU.subtract))
                        last = dve.scalar_tensor_tensor(rkv[:, n, :], rkv[:, n, :], c.col(mu, p), pad[:, n, 1:S + 1], ALU.mult, ALU.add)
                        if n < 2:
                            q(last)
                    steps.done(last, "shifted")
                    steps.wait(dve, "rooted", p)
                    q(dve.tensor_scalar(tmp[:, :], tmp[:, :], 1e-12, None, ALU.max))
                    q(dve.reciprocal(tmp[:, :], tmp[:, :]))
                    q(dve.tensor_tensor(kn[:, :], kn[:, :], tmp[:, :], ALU.mult))
                    q(dve.tensor_scalar(ld[:, :], ld[:, :], -DECAY_SCALE, None, ALU.mult))
                    q(dve.tensor_tensor_scan(g[:, :], c.tab("restart"), ld[:, :], 0.0, ALU.mult, ALU.add))
                    steps.done(dve.tensor_tensor(gp[:, :], g[:, :], ld[:, :], ALU.subtract), "decays")
                    steps.wait(dve, "hats0", p)
                    q(dve.tensor_scalar(tmp[:, :], aa[:, :], 1.0, c.col("k_a", p), ALU.subtract, ALU.mult))
                    q(dve.scalar_tensor_tensor(rkv[:, 1, :], tmp[:, :], 1.0, rkv[:, 1, :], ALU.add, ALU.mult))
                    q(dve.tensor_tensor(ahat[:, :], kn[:, :], gp[:, :], ALU.mult))
                    q(dve.tensor_tensor(kn[:, :], kn[:, :], aa[:, :], ALU.mult))
                    q(dve.tensor_tensor(bhat[:, 0, :], kn[:, :], winv[:, :], ALU.mult))
                    q(dve.tensor_tensor(khat[:, 0, :], rkv[:, 1, :], winv[:, :], ALU.mult))
                    for buf in (bhat, khat):
                        for h in range(2):
                            rows = slice(64 * h, 64 * h + 64)
                            q(dve.tensor_copy(buf[rows, 1 + h, :], buf[rows, 0, :]))
                    q(dve.tensor_tensor(rhat[:, :], rkv[:, 0, :], wfull[:, :], ALU.mult))
                    steps.done(dve.scalar_tensor_tensor(tmp[:, :], rkv[:, 0, :], c.col("r_k", p), rkv[:, 1, :], ALU.mult, ALU.mult), "hats")

                    def wide(name_):
                        return c.tab(name_).rearrange("p (o t) -> p o t", o=1).broadcast_to([P, TT, P])
                    for h in range(2):
                        steps.wait(dve, f"pair{h}", p)
                        for n, (dst, mask) in enumerate(((mt, "strict_chunk"), (nt, "strict_chunk"), (rb, "causal_chunk"), (rk, "causal_chunk"))):
                            q(dve.tensor_tensor(dst[:, h, :, :], b[n][:, :].rearrange(by_tile, t=TT), wide(mask), ALU.mult))
                        q(dve.tensor_copy(tri[:, :, :], wide("ident")))
                        steps.done(dve.tensor_copy(inv[:, :, :], wide("ident")), f"pmasked{h}")
                        dve_base = f"pmasked{h}"
                        for n in range(LEVELS):
                            steps.wait(dve, dve_base, p)
                            steps.done(dve.tensor_tensor(level[:, :, :], mt[:, h, :, :], wide(f"level{n}"), ALU.mult), f"lev{h}_{n}")
                            steps.wait(dve, f"tp{h}_{n}", p)
                            q(dve.tensor_tensor(tri[:, :, :], tri[:, :, :], b[5][:, :].rearrange(by_tile, t=TT), ALU.subtract))
                            dst = inv if n < LEVELS - 1 else invs[:, h, :, :]
                            steps.done(dve.tensor_tensor(dst[:, :, :], inv[:, :, :], b[6][:, :].rearrange(by_tile, t=TT), ALU.subtract), f"tri{h}_{n}")
                            dve_base = f"tri{h}_{n}"
                    for n in range(NC):
                        steps.wait(dve, f"up{n}", p)
                        end = wfull[:, (n + 1) * CHUNK - 1:(n + 1) * CHUNK]
                        q(dve.scalar_tensor_tensor(upd[:, :], b[6][:, 0:P], end, c.tab("head_ones"), ALU.mult, ALU.mult))
                        steps.done(dve.scalar_tensor_tensor(state[:, n + 1, :], state[:, n, :], end, upd[:, :], ALU.mult, ALU.add), f"state{n}")
                    steps.wait(dve, "mixed", p)
                    q(dve.tensor_tensor(aa[:, :], rkv[:, 2, :], b[0][:, :], ALU.mult))
                    steps.done(dve.tensor_copy(kn[:, :], b[7][:, :]), "bonus")
                    steps.wait(dve, "meaned", p)
                    steps.done(dve.scalar_tensor_tensor(kn[:, :], b[1][:, :], -1.0 / 64, kn[:, :], ALU.mult, ALU.add), "centred")
                    steps.wait(dve, "croot", p)
                    q(dve.reciprocal(g[:, :], g[:, :]))
                    steps.done(dve.tensor_tensor(kn[:, :], kn[:, :], g[:, :], ALU.mult), "scaled")
                    steps.wait(dve, "affine", p)
                    q(dve.tensor_tensor(kn[:, :], kn[:, :], aa[:, :], ALU.add))
                    steps.done(dve.tensor_tensor(y[:, p, :], kn[:, :], gg[:, :], ALU.mult), "stored")
                rounds(dve, 4, body, q)


def gelu_values(c, name, x, w_d, v):
    nc = c.nc
    chunks = 4
    with Stage(nc, name) as st:
        w = [st.sb(f"w{j}", [P, DT, S]) for j in range(2)]
        acc = st.ps("acc", [P, TT, S])
        landed = [st.sem(f"landed{j}") for j in range(2)]
        made, done = st.sem("made"), st.sem("done")
        with nc.Block() as block:
            @block.sync
            def _(sp):
                def body(r, first):
                    for j in range(2):
                        if not first:
                            sp.wait_ge(made, TT * (2 * r + j - 1))
                        sp.dma_start(w[j][:, :, :], w_d[2 * r + j]).then_inc(landed[j], 16)
                rounds(sp, chunks // 2, body)

            @block.tensor
            def _(pe):
                def body(r, first):
                    for j in range(2):
                        pe.wait_ge(landed[j], 16 * (r + 1))
                        for t in range(TT):
                            if not first or j:
                                pe.wait_ge(done, TT * (2 * r + j - 1) + t + 1)
                            for k in range(DT):
                                last = pe.matmul(acc[:, t, :], x[:, k, tile_cols(t)], w[j][:, k, :], start=k == 0, stop=k == DT - 1)
                            last.then_inc(made, 1)
                rounds(pe, chunks // 2, body)

            @block.scalar
            def _(act):
                def body(r, first):
                    for j in range(2):
                        for t in range(TT):
                            act.wait_ge(made, TT * (2 * r + j) + t + 1)
                            act.activation(v[:, t, bass.ds((2 * r + j) * S, S)], acc[:, t, :], ACT.Gelu_apprx_tanh).then_inc(done, 1)
                rounds(act, chunks // 2, body)


def spatial_gate(c, name, v, u, rows_d, ws_d):
    nc = c.nc
    width = v.shape[2]
    groups, per = 8, 2
    with Stage(nc, name) as st:
        gb, ws, bs = st.sb("gb", [P, 2, width]), st.sb("ws", [P, groups, P]), st.sb("bs", [P, groups, P])
        total, var, mean, rstd = (st.sb(n, [P, TT]) for n in ("total", "var", "mean", "rstd"))
        acc, mixed = st.ps("acc", [P, 2, S]), st.sb("mixed_s", [P, 2, S])
        sq = st.ps("sq", [P, width])
        landed, chain, centred, squared, rooted, ready, made, done = (
            st.sem(n) for n in ("landed", "chain", "centred", "squared", "rooted", "ready", "made", "done"))
        with nc.Block() as block:
            @block.sync
            def _(sp):
                sp.dma_start(gb[:, :, :], rows_d[:, 0:2 * width].rearrange("p (a n) -> p a n", a=2)).then_inc(landed, 16)
                sp.dma_start(bs[:, :, :], rows_d[:, 2 * width:].rearrange("p (a n) -> p a n", a=groups)).then_inc(landed, 16)
                sp.dma_start(ws[:, :, :], ws_d).then_inc(landed, 16)

            @block.scalar
            def _(act):
                for t in range(TT):
                    act.wait_ge(centred, t + 1)
                    if t:
                        act.wait_ge(squared, t)
                    act.activation(sq[:, :], v[:, t, :], ACT.Square, accum_out=var[:, t:t + 1]).then_inc(squared, 1)
                act.wait_ge(rooted, 1)
                act.activation(rstd[:, :], var[:, :], ACT.Sqrt).then_inc(rooted, 1)

            @block.vector
            def _(dve):
                q = InOrder(dve, chain)
                dve.wait_ge(landed, 48)
                mask = c.tab("causal").rearrange("p (o t) -> p o t", o=1).broadcast_to([P, groups, P])
                q(dve.tensor_tensor(ws[:, :, :], ws[:, :, :], mask, ALU.mult))
                for t in range(TT):
                    q(dve.tensor_reduce(total[:, t:t + 1], v[:, t, :], AX_X, ALU.add))
                    q(dve.tensor_scalar(mean[:, t:t + 1], total[:, t:t + 1], 1.0 / width, None, ALU.mult))
                    dve.tensor_scalar(v[:, t, :], v[:, t, :], mean[:, t:t + 1], None, ALU.subtract).then_inc(centred, 1)
                dve.wait_ge(squared, TT)
                dve.tensor_scalar(var[:, :], var[:, :], 1.0 / width, 1e-5, ALU.mult, ALU.add).then_inc(rooted, 1)
                dve.wait_ge(rooted, 2)
                q(dve.reciprocal(rstd[:, :], rstd[:, :]))
                for t in range(TT):
                    q(dve.scalar_tensor_tensor(v[:, t, :], v[:, t, :], rstd[:, t:t + 1], gb[:, 0, :], ALU.mult, ALU.mult))
                    q(dve.tensor_tensor(v[:, t, :], v[:, t, :], gb[:, 1, :], ALU.add))
                q(dve.memset(total[:, :], 0.0))
                dve.memset(total[:, :], 0.0).then_inc(ready, 1)
                for m in range(groups * per):
                    dve.wait_ge(made, m + 1)
                    bias = bs[:, m // per, :].rearrange("p (o t) -> p o t", o=1).broadcast_to([P, TT, P])
                    q(dve.tensor_tensor(mixed[:, m % 2, :].rearrange("p (t f) -> p t f", t=TT),
                                        acc[:, m % 2, :].rearrange("p (t f) -> p t f", t=TT), bias, ALU.add))
                    dve.tensor_tensor(u[:, m, :], u[:, m, :], mixed[:, m % 2, :], ALU.mult).then_inc(done, 1)

            @block.tensor
            def _(pe):
                pe.wait_ge(ready, 1)
                for m in range(groups * per):
                    if m >= 2:
                        pe.wait_ge(done, m - 1)
                    for t in range(TT):
                        last = pe.matmul(acc[:, m % 2, tile_cols(t)], v[:, t, tile_cols(m)], ws[:, m // per, :], start=True, stop=True)
                    last.then_inc(made, 1)


def build(nc, a, out_d):
    with ExitStack() as keep:
        def sb(name, shape, stack=keep):
            return stack.enter_context(nc.sbuf_tensor(name, shape, F32))

        table, column = sb("table", [P, TABLE_WIDTH]), sb("column", [P, COLUMN_WIDTH])
        x, xn = sb("x", [P, DT, S]), sb("xn", [P, DT, S])
        c = Ctx(nc, table, column)
        load_constants(c, a["table"], a["column"], a["x"], x)

        with ExitStack() as s:
            hidden = sb("hidden1", [P, FT, S], s)
            swiglu_up(c, "f1u", a["f1_up"], x, hidden, FT)
            project(c, "f1d", a["f1_down"], hidden, FT, DT, x, residual=x, res_scale=ALPHA, scale=0.5)
        norm(c, "ln1", x, x, DT, True, 1e-5, lambda k: c.col("ln1_g", k), lambda k: c.col("ln1_b", k))
        with ExitStack() as s:
            y_a, y_h, merged = (sb(n, [P, DT, S], s) for n in ("y_attn", "y_hgrn", "merged1"))
            attention(c, "att", x, a["att_w"], y_a, [[0], [0, 1], [1, 2], [2, 3]],
                      qb=lambda p: c.col("att_qb", p), kb=lambda p: c.col("att_kb", p), vb_d=a["att_vb"],
                      sinks=lambda h, n=1: c.col("sinks", h, n), rope=True)
            linear_recurrence(c, "hg", x, a["hg_w"], 8, y_h, "hgrn", c.col("hg_ng"), qb=lambda h: c.col("hg_qb", h),
                              fb=lambda h: c.col("hg_fb", h), vb_d=a["hg_vb"], ogb=lambda h: c.col("hg_ogb", h),
                              lb=c.col("hg_lb", 0, 16))
            merge(c, "mg1", x, a["mg1_w"], [y_a, y_h], [DT, DT], merged, lambda b, m: c.col("gate_b", b * DT + m))
            project(c, "wo1", a["wo1"], merged, DT, DT, x, residual=x, res_scale=ALPHA)
        norm(c, "ln2", x, x, DT, True, 1e-5, lambda k: c.col("ln2_g", k), lambda k: c.col("ln2_b", k))
        with ExitStack() as s:
            hidden = sb("hidden2", [P, FT, S], s)
            swiglu_up(c, "f2u", a["f2_up"], x, hidden, FT)
            project(c, "f2d", a["f2_down"], hidden, FT, DT, x, residual=x, res_scale=ALPHA, scale=0.5)
        norm(c, "ln3", x, x, DT, True, 1e-5, lambda k: c.col("ln3_g", k), lambda k: c.col("ln3_b", k))

        norm(c, "rn1", x, xn, DT, False, 1e-6, lambda k: c.col("mix2_g", k))
        with ExitStack() as s:
            ys = [sb(f"y{n}", [P, 4, S], s) for n in range(4)]
            with ExitStack() as s2:
                low = sb("low", [P, 4, S], s2)
                project(c, "low", a["low_w"], xn, DT, 4, low)
                linear_recurrence(c, "gla", xn, a["gla_w"], 4, ys[1], "gla", c.col("gla_ng"), fb=lambda h: c.col("gla_fb", h),
                                  small=low[:, 0, :], fup_d=a["gla_fup"])
                mlstm(c, "ml", xn, a["ml_w"], 4, ys[2], low[:, 0, :])
                ssd(c, "sd", xn, a["sd_w"], ys[3], low[:, 0, :])
                norm(c, "sdn", ys[3], ys[3], 4, False, 1e-6, lambda k: c.col("sd_ng", k))
                rwkv(c, "rw", xn, a["rw_w"], a["rw_up"], ys[0], low)
            merged = sb("merged2", [P, DT, S], s)
            merge(c, "mg2", xn, a["mg2_w"], ys, [4] * 4, merged)
            project(c, "wo2", a["wo2"], merged, DT, DT, x, residual=x)
        norm(c, "rn2", x, xn, DT, False, 1e-6, lambda k: c.col("ffn2_g", k))
        with ExitStack() as s:
            hidden = sb("hidden3", [P, FT, S], s)
            conv_glu_up(c, "f3u", a["f3_up"], xn, hidden, FT,
                        lambda i, t: c.col("ffn2_cw", i * 2 * FT + t), lambda t: c.col("ffn2_cb", t),
                        lambda i, t: c.col("ffn2_cw", i * 2 * FT + FT + t), lambda t: c.col("ffn2_cb", FT + t))
            project(c, "f3d", a["f3_down"], hidden, FT, DT, x, residual=x)
        norm(c, "rn3", x, x, DT, False, 1e-6, lambda k: c.col("fin2_g", k))

        for layer in range(2):
            norm(c, f"m{layer}", x, xn, DT, False, 1e-6, lambda k: c.col("mix3_g", layer * DT + k))
            with ExitStack() as s:
                if layer == 0:
                    u, v = sb("u", [P, 16, S], s), sb("v", [P, TT, 16 * P], s)
                    project(c, "gmu", a["gm_u"], xn, DT, 16, u, func=ACT.Gelu_apprx_tanh)
                    gelu_values(c, "gmv", xn, a["gm_v"], v)
                    spatial_gate(c, "gms", v, u, a["gm_rows"], a["gm_ws"])
                    project(c, "gmo", a["gm_out"], u, 16, DT, x, residual=x)
                else:
                    y, rows = sb("y_fox", [P, DT, S], s), sb("rows", [P, S], s)
                    forget_rows(c, "fr", xn, a["fox_f"], rows, c.col("fox_fb"))
                    attention(c, "fox", xn, a["fox_w"], y, [list(range(i + 1)) for i in range(TT)], forget=rows)
                    project(c, "foxo", a["fox_o"], y, DT, DT, x, residual=x)
            norm(c, f"n{layer}", x, xn, DT, False, 1e-6, lambda k: c.col("ffn3_g", layer * DT + k))
            with ExitStack() as s:
                hidden = sb(f"hidden4{layer}", [P, 16, S], s)
                conv_glu_up(c, f"g{layer}u", a[f"g{layer}_up"], xn, hidden, 16,
                            lambda i, t: c.col("ffn3_cw", layer * 48 + i * 16 + t), lambda t: c.col("ffn3_cb", layer * 16 + t))
                project(c, f"g{layer}d", a[f"g{layer}_down"], hidden, 16, DT, x, residual=x)
        norm(c, "fin", x, x, DT, False, 1e-6, lambda k: c.col("fin3_g", k), sink_d=out_d)


def lay_out(i):
    i = {k: np.asarray(v) for k, v in i.items()}
    a = {}

    def tiles(w):
        k, m = w.shape
        return w.reshape(k // P, P, m // P, P).transpose(2, 1, 0, 3).reshape(m // P, P, k)

    def stack(*ws):
        return np.stack([tiles(w) for w in ws], 2)

    def columns(v):
        return v.reshape(-1, P).T

    def padded_heads(w, heads):
        out = np.zeros((w.shape[0], heads, P), w.dtype)
        out[:, :, 0:64] = w.reshape(w.shape[0], heads, 64)
        return out.reshape(w.shape[0], heads * P)

    def doubled(w):
        w = w.reshape(w.shape[0], 4, 64)
        return np.stack([w] * 4, 2).reshape(w.shape[0], 16 * 64)

    col = {}
    a["table"] = np.concatenate(list(TABLES.values()), 1)
    a["x"] = i["x"][0].T.reshape(DT, P, S).transpose(1, 0, 2)

    for n in ("ln1_g", "ln1_b", "ln2_g", "ln2_b", "ln3_g", "ln3_b"):
        col[n] = columns(i[n][0])
    for n in (1, 2):
        a[f"f{n}_up"] = stack(i[f"ffn{n}_w1"][0], i[f"ffn{n}_w3"][0])
        a[f"f{n}_down"] = tiles(i[f"ffn{n}_w2"][0])
    cuts = np.cumsum([1024, 256, 256, 1024, 1024, 1024, 1024, 1024])
    q, k, v, f, qh, ih, og, ga, gh = np.split(i["w_in"][0], cuts, 1)
    bq, bk, bv, bf, bqh, bih, bog, bga, bgh = np.split(i["b_in"], cuts, 1)
    a["att_w"] = stack(q, doubled(k), doubled(v))
    a["att_vb"] = doubled(bv).reshape(8, 1, P)
    col["att_qb"], col["att_kb"] = columns(bq[0]), columns(doubled(bk)[0])
    col["sinks"] = np.broadcast_to(i["attn_sinks"][0], (P, 16))
    a["hg_w"] = stack(qh, f, ih, og)
    a["hg_vb"] = bih.reshape(8, 1, P)
    col["hg_qb"], col["hg_fb"], col["hg_ogb"] = columns(bqh[0]), columns(bf[0]), columns(bog[0])
    col["hg_lb"] = columns(i["hgrn_lb_logits"].reshape(-1))
    col["hg_ng"] = columns(i["hgrn_norm_g"][0])
    col["gate_b"] = np.concatenate([columns(bga[0]), columns(bgh[0])], 1)
    gates = [tiles(ga), tiles(gh)]
    outs = [tiles(i["w_proj_attn"][0]), tiles(i["w_proj_hgrn"][0])]
    a["mg1_w"] = np.stack([np.concatenate([g, o], 2) for g, o in zip(gates, outs)], 1)
    a["wo1"] = tiles(i["w_out"][0])

    w = i["w_in_2"][0]
    r2, k2, v2, wlo, alo, glo, gq, gk, gv, gf, go, mqk, mv, mi, mf, mo, sz, sx, sb_, sc, sdt, fg = np.split(w, np.cumsum(
        [512, 512, 512, 64, 64, 128, 256, 256, 512, 16, 512, 512, 512, 4, 4, 512, 512, 512, 256, 256, 8]), 1)
    zero = np.zeros((D, 96), w.dtype)
    small = np.concatenate([mi, mf, sdt, gf, zero], 1)
    a["low_w"] = tiles(np.concatenate([small, wlo, alo, glo, np.zeros((D, P), w.dtype)], 1))
    col["mix2_g"] = columns(i["mix_norm_g_2"][0])
    mu = i["rwkv_mu_2"][0]
    col["r_mu"], col["k_mu"], col["v_mu"], col["lora_mu"] = (columns(m) for m in np.split(mu, [512, 1024, 1536]))
    for n, key in (("w0", "rwkv_w0_2"), ("a0", "rwkv_a0_2"), ("k_k", "rwkv_k_k_2"), ("k_a", "rwkv_k_a_2"),
                   ("r_k", "rwkv_r_k_2"), ("gn_g", "rwkv_gn_g_2"), ("gn_b", "rwkv_gn_b_2")):
        col[n] = columns(i[key][0].reshape(-1))
    a["rw_w"] = stack(r2, k2, v2)
    lows = np.zeros((4, P, 3, P), w.dtype)
    lows[:, 0:64, 0, :] = i["rwkv_w_up_2"][0].reshape(64, 4, P).transpose(1, 0, 2)
    lows[:, 64:128, 1, :] = i["rwkv_a_up_2"][0].reshape(64, 4, P).transpose(1, 0, 2)
    lows[:, :, 2, :] = i["rwkv_g_up_2"][0].reshape(P, 4, P).transpose(1, 0, 2)
    a["rw_up"] = lows
    a["gla_w"] = stack(padded_heads(gq, 4), padded_heads(gk, 4), gv, go)
    fup = np.zeros((4, P, P), w.dtype)
    fup[:, 16:32, 0:64] = i["gla_f_up_2"][0].reshape(16, 4, 64).transpose(1, 0, 2)
    a["gla_fup"] = fup
    col["gla_fb"] = columns(padded_heads(i["gla_f_bias_2"], 4)[0])
    col["gla_ng"] = columns(i["gla_norm_g_2"][0])
    a["ml_w"] = stack(padded_heads(mqk[:, 0:256], 4), padded_heads(mqk[:, 256:512], 4), mv, mo)
    cw = i["mlstm_conv_w_2"][0]
    taps = np.stack([padded_heads(cw[:, 0:256], 4).reshape(4, 4, P), padded_heads(cw[:, 256:], 4).reshape(4, 4, P)], 0)
    col["ml_cw"] = taps.transpose(3, 2, 0, 1).reshape(P, 32)
    cb = i["mlstm_conv_b_2"]
    col["ml_cb"] = np.stack([padded_heads(cb[:, 0:256], 4).reshape(4, P), padded_heads(cb[:, 256:], 4).reshape(4, P)], 1) \
        .reshape(8, P).T
    col["ml_ib"] = np.broadcast_to(i["mlstm_i_bias_2"][0], (P, 4))
    col["ml_fb"] = np.broadcast_to(i["mlstm_f_bias_2"][0], (P, 4))
    col["ml_ng"] = columns(i["mlstm_norm_g_2"][0])
    twice = lambda m: np.repeat(m.reshape(m.shape[0], 2, P), 2, 1).reshape(m.shape[0], 4 * P)
    a["sd_w"] = stack(sx, sz, twice(sb_), twice(sc))
    cw, cb = i["ssd_conv_w_2"][0], i["ssd_conv_b_2"]
    col["sd_cwx"] = cw[:, 0:512].reshape(4, 4, P).transpose(2, 1, 0).reshape(P, 16)
    col["sd_cbx"] = columns(cb[0, 0:512])
    bc = np.stack([twice(cw[:, 512:768]).reshape(4, 4, P), twice(cw[:, 768:]).reshape(4, 4, P)], 0)
    col["sd_cwbc"] = bc.transpose(3, 2, 0, 1).reshape(P, 32)
    bc = np.stack([twice(cb[:, 512:768]).reshape(4, P), twice(cb[:, 768:]).reshape(4, P)], 0)
    col["sd_cbbc"] = bc.transpose(2, 1, 0).reshape(P, 8)
    col["sd_dtb"] = np.broadcast_to(i["ssd_dt_bias_2"][0], (P, 8))
    col["sd_alog"] = np.broadcast_to(i["ssd_a_log_2"][0], (P, 8))
    col["sd_d"] = columns(np.repeat(i["ssd_d_2"][0], 64))
    col["sd_ng"] = columns(i["ssd_norm_g_2"][0])
    proj = i["branch_proj_2"][0]
    a["mg2_w"] = np.stack([np.concatenate([tiles(fg[:, n * D:(n + 1) * D]), tiles(proj[n])], 2) for n in range(4)], 1)
    a["wo2"] = tiles(i["w_out_2"][0])
    up = i["ffn_up_2"][0]
    a["f3_up"], a["f3_down"] = stack(up[:, 0:D_FF], up[:, D_FF:]), tiles(i["ffn_down_2"][0])
    col["ffn2_g"], col["fin2_g"] = columns(i["ffn_norm_g_2"][0]), columns(i["final_norm_g_2"])
    col["ffn2_cw"] = columns(i["ffn_conv_w_2"][0].reshape(-1))
    col["ffn2_cb"] = columns(i["ffn_conv_b_2"][0])

    col["mix3_g"], col["ffn3_g"] = columns(i["mix_norm_g_3"].reshape(-1)), columns(i["ffn_norm_g_3"].reshape(-1))
    col["ffn3_cw"] = columns(i["ffn_conv_w_3"].reshape(-1))
    col["ffn3_cb"] = columns(i["ffn_conv_b_3"].reshape(-1))
    col["fin3_g"] = columns(i["final_norm_g_3"])
    w = i["gm_w_in_3"][0]
    a["gm_u"] = tiles(w[:, 0:2048])
    a["gm_v"] = w[:, 2048:].reshape(DT, P, 4, S).transpose(2, 1, 0, 3)
    rows = np.concatenate([i["gm_ln_g_3"][0], i["gm_ln_b_3"][0], i["gm_b_s_3"][0].reshape(-1)])
    a["gm_rows"] = np.broadcast_to(rows, (P, rows.size))
    a["gm_ws"] = i["gm_w_s_3"][0].transpose(2, 0, 1)
    a["gm_out"] = tiles(i["gm_w_out_3"][0])
    q, k, v, f = np.split(i["fox_w_qkvf_3"][0], [D, 2 * D, 3 * D], 1)
    a["fox_w"] = stack(q, k, v)
    wide = np.zeros((D, P), f.dtype)
    wide[:, 0:16] = f
    a["fox_f"] = tiles(wide)[0]
    fb = np.zeros((P, 1), f.dtype)
    fb[0:16, 0] = i["fox_b_f_3"][0]
    col["fox_fb"] = fb
    a["fox_o"] = tiles(i["fox_w_o_3"][0])
    for n in range(2):
        a[f"g{n}_up"] = stack(i["ffn_w_gate_3"][n], i["ffn_w_up_3"][n])
        a[f"g{n}_down"] = tiles(i["ffn_w_down_3"][n])
    for n, width in COLUMNS:
        assert col[n].shape == (P, width), (n, col[n].shape)
    a["column"] = np.concatenate([col[n] for n, _ in COLUMNS], 1)
    return {k: np.ascontiguousarray(v) for k, v in a.items()}


def kernel(**inputs):
    import concourse.bacc as _bacc
    from concourse.bass_utils import run_bass_kernel_spmd as _run

    nc = _bacc.Bacc("TRN2", target_bir_lowering=False, num_devices=1)
    arrays = {f"in_{name}": array for name, array in lay_out(inputs).items()}
    args = {name[3:]: nc.dram_tensor(name, array.shape, F32, kind="ExternalInput").ap() for name, array in arrays.items()}
    out = nc.dram_tensor("out", (P, DT, S), F32, kind="ExternalOutput").ap()
    build(nc, args, out)
    r = _run(nc, [arrays], core_ids=[0])
    return np.asarray(r.results[0]["out"]).transpose(2, 1, 0).reshape(1, S, D)
```

```python
from contextlib import ExitStack

import numpy as np

import concourse.bass as bass
from concourse import mybir

F32 = mybir.dt.float32
F32R = mybir.dt.float32r
ACT = mybir.ActivationFunctionType
ALU = mybir.AluOpType
AX_X = mybir.AxisListType.X

P = 128
S = 512
TT = S // P
D = 1024
DT = D // P
D_FF = 2816
FT = D_FF // P
CHUNK = 64
NC = S // CHUNK
ALPHA = 2.0 ** 0.25
DECAY_SCALE = 0.6065306597
LEVELS = 6
NEG = -1e30


def tables():
    s = np.arange(P)[:, None]
    t = np.arange(P)[None, :]
    same = (s // CHUNK) == (t // CHUNK)
    out = {
        "ident": (s == t),
        "ones": np.ones((P, P)),
        "head_ones": (s // 64) == (t // 64),
        "causal_chunk": (s <= t) & same,
        "strict_chunk": (s < t) & same,
        "mask_diag": np.where(t <= s, 0.0, NEG),
        "mask_prev": np.where(t > s, 0.0, NEG),
        "causal": (s <= t),
    }
    rot = np.zeros((P, P))
    for base in (0, 64):
        for j in range(8):
            rot[base + 8 + j, base + j] = -1.0
            rot[base + j, base + 8 + j] = 1.0
    out["rot"] = rot
    for n in range(LEVELS):
        half = 1 << n
        block = (s // (2 * half)) == (t // (2 * half))
        out[f"level{n}"] = block & (s % (2 * half) < half) & (t % (2 * half) >= half)
    out["mask_after"] = np.concatenate([np.where(s <= t, 0.0, NEG), np.zeros((P, S - P))], 1)
    out["restart"] = np.broadcast_to((np.arange(S) % CHUNK != 0), (P, S))
    pos = np.arange(S, dtype=np.float32)
    inv = np.float32(500000.0) ** (-np.arange(0, 16, 2, dtype=np.float32) / np.float32(16))
    ang = (pos[:, None] * inv[None, :]).astype(np.float32)
    c, sn = np.ones((P, S), np.float32), np.zeros((P, S), np.float32)
    for base in (0, 8, 64, 72):
        c[base:base + 8] = np.cos(ang).T
        sn[base:base + 8] = np.sin(ang).T
    out["cos"], out["sin"] = c, sn
    return {k: np.ascontiguousarray(v, dtype=np.float32) for k, v in out.items()}


TABLES = tables()
TABLE_AT, _at = {}, 0
for _name, _v in TABLES.items():
    TABLE_AT[_name] = (_at, _v.shape[1])
    _at += _v.shape[1]
TABLE_WIDTH = _at

COLUMNS = [
    ("ln1_g", 8), ("ln1_b", 8), ("ln2_g", 8), ("ln2_b", 8), ("ln3_g", 8), ("ln3_b", 8),
    ("att_qb", 8), ("att_kb", 8), ("att_vb", 8), ("sinks", 16),
    ("hg_qb", 8), ("hg_fb", 8), ("hg_vb", 8), ("hg_ogb", 8), ("hg_lb", 16), ("hg_ng", 1), ("gate_b", 16),
    ("mix2_g", 8), ("lora_mu", 2), ("r_mu", 4), ("k_mu", 4), ("v_mu", 4), ("w0", 4), ("a0", 4),
    ("k_k", 4), ("k_a", 4), ("r_k", 4), ("gn_g", 4), ("gn_b", 4),
    ("gla_fb", 4), ("gla_ng", 1),
    ("ml_cw", 32), ("ml_cb", 8), ("ml_ib", 4), ("ml_fb", 4), ("ml_ng", 4),
    ("sd_cwx", 16), ("sd_cbx", 4), ("sd_cwbc", 32), ("sd_cbbc", 8), ("sd_dtb", 8), ("sd_alog", 8), ("sd_d", 4),
    ("sd_ng", 4), ("ffn2_g", 8), ("ffn2_cw", 132), ("ffn2_cb", 44), ("fin2_g", 8),
    ("mix3_g", 16), ("ffn3_g", 16), ("ffn3_cw", 96), ("ffn3_cb", 32), ("fox_fb", 1), ("fin3_g", 8),
]
COLUMN_AT, _at = {}, 0
for _name, _n in COLUMNS:
    COLUMN_AT[_name] = _at
    _at += _n
COLUMN_WIDTH = _at


class Stage:

    def __init__(self, nc, name):
        self.nc, self.name, self.stack, self.sems = nc, name, ExitStack(), []

    def __enter__(self):
        return self

    def __exit__(self, *e):
        if e[0] is None:
            for sem in self.sems:
                self.nc.gpsimd.sem_clear(sem)
        return self.stack.__exit__(*e)

    def sb(self, name, shape, dtype=F32):
        return self.stack.enter_context(self.nc.sbuf_tensor(f"{self.name}_{name}", shape, dtype))

    def ps(self, name, shape):
        return self.stack.enter_context(self.nc.psum_tensor(f"{self.name}_{name}", shape, F32))

    def sem(self, name):
        self.sems.append(self.stack.enter_context(self.nc.semaphore(f"{self.name}_{name}")))
        return self.sems[-1]


class InOrder:

    def __init__(self, eng, sem):
        self.eng, self.sem, self.base, self.n = eng, sem, 0, 0

    def __call__(self, ins):
        ins.then_inc(self.sem, 1)
        self.n += 1
        self.eng.wait_ge(self.sem, self.base + self.n)

    def free(self, ins):
        ins.then_inc(self.sem, 1)
        self.n += 1


class Steps:

    def __init__(self, sem, names):
        self.sem, self.names = sem, names.split()
        assert len(set(self.names)) == len(self.names)

    def wait(self, eng, name, r=0):
        eng.wait_ge(self.sem, r * len(self.names) + self.names.index(name) + 1)

    def wait_round(self, eng, r):
        eng.wait_ge(self.sem, r * len(self.names))

    def done(self, ins, name):
        assert name in self.names
        ins.then_inc(self.sem, 1)


def rounds(eng, n, body, chain=None):
    start = chain.base + chain.n if chain else 0
    if chain:
        chain.base, chain.n = start, 0
    body(0, True)
    per = chain.n if chain else 0
    if n > 1:
        with eng.Fori(1, n) as r:
            if chain:
                chain.base, chain.n = r * per + start, 0
            body(r, False)
    if chain:
        chain.base, chain.n = start + n * per, 0


def rounds3(eng, n, body, chain=None):
    start = chain.base + chain.n if chain else 0
    if chain:
        chain.base, chain.n = start, 0
    body(0, True, n == 1)
    per = chain.n if chain else 0
    if n > 2:
        with eng.Fori(1, n - 1) as r:
            if chain:
                chain.base, chain.n = r * per + start, 0
            body(r, False, False)
    if n > 1:
        if chain:
            chain.base, chain.n = start + (n - 1) * per, 0
        body(n - 1, False, True)


def tile_cols(k):
    return slice(k * P, (k + 1) * P)


class Ctx:

    def __init__(self, nc, table, column):
        self.nc, self.table, self.column = nc, table, column

    def tab(self, name, part=P):
        at, width = TABLE_AT[name]
        return self.table[0:part, at:at + width]

    def col(self, name, i=0, n=1):
        at = COLUMN_AT[name] + i
        return self.column[:, bass.ds(at, n)]


def load_constants(c, table_d, column_d, x_d, x):
    nc = c.nc
    with Stage(nc, "const") as st:
        landed = st.sem("landed")
        with nc.Block() as block:
            @block.sync
            def _(sp):
                sp.dma_start(c.table[:, :], table_d).then_inc(landed, 16)
                sp.dma_start(c.column[:, :], column_d).then_inc(landed, 16)
                sp.dma_start(x[:, :, :], x_d).then_inc(landed, 16)
                sp.wait_ge(landed, 48)


class Pair:

    def __init__(self, make, name, shape):
        self.hi, self.lo = make(f"{name}_hi", shape, F32R), make(f"{name}_lo", shape, F32R)
        self.value = self.hi.bitcast(F32) if hasattr(self.hi, "bitcast") else self.hi[:].bitcast(F32)


def split(dve, q, source, pair, at, done):
    q(dve.tensor_copy(pair.hi[at], source))
    return dve.tensor_tensor(pair.lo[at], source, pair.value[at], ALU.subtract).then_inc(done, 1)


class Feed:

    def __init__(self, st, cols, per, slots):
        self.per, self.slots = per, slots
        self.raw = st.sb("w_raw", [P, slots, cols])
        self.hi, self.lo = st.sb("w_hi", [P, slots, cols], F32R), st.sb("w_lo", [P, slots, cols], F32R)
        self.hi_value = self.hi[:, :, :].bitcast(F32)
        self.landed = [st.sem(f"w_landed{j}") for j in range(slots)]
        self.rounded, self.parted, self.used = st.sem("w_rounded"), st.sem("w_parted"), st.sem("w_used")

    def at(self, r, m):
        return r * self.per + m, m % self.slots

    def load(self, sp, r, m, first, source):
        s, slot = self.at(r, m)
        if not first or m >= self.slots:
            sp.wait_ge(self.parted, s - self.slots + 1)
        cols = source.shape[-1]
        sp.dma_start(self.raw[:, slot, 0:cols], source).then_inc(self.landed[slot], 16)

    def round(self, act, r, m, first, cols):
        s, slot = self.at(r, m)
        act.wait_ge(self.landed[slot], (r * (self.per // self.slots) + m // self.slots + 1) * 16)
        if not first or m >= self.slots:
            act.wait_ge(self.used, s - self.slots + 1)
        act.activation(self.hi[:, slot, 0:cols], self.raw[:, slot, 0:cols], ACT.Copy).then_inc(self.rounded, 1)

    def rest(self, dve, r, m, cols):
        s, slot = self.at(r, m)
        dve.wait_ge(self.rounded, s + 1)
        dve.tensor_tensor(self.lo[:, slot, 0:cols], self.raw[:, slot, 0:cols], self.hi_value[:, slot, 0:cols],
                          ALU.subtract).then_inc(self.parted, 1)

    def products(self, pe, r, m, out, x, k0, kt, start=True, stop=True, some=None):
        s, slot = self.at(r, m)
        some = range(kt) if some is None else some
        if some[0] == 0:
            pe.wait_ge(self.parted, s + 1)
        for k in some:
            for n, (w, v) in enumerate(((self.hi, x.hi), (self.hi, x.lo), (self.lo, x.hi))):
                last = pe.matmul(out, w[:, slot, tile_cols(k)], v[:, k0 + k, :], start=start and k == 0 and n == 0,
                                 stop=stop and k == kt - 1 and n == 2)
        if some[-1] == kt - 1:
            last.then_inc(self.used, 1)


def norm(c, name, x, out, kt, centre, eps, g, b=None, pair=None, sink_d=None):
    nc = c.nc
    width = kt * P
    with Stage(nc, name) as st:
        mean_p, var_p = st.ps("mean", [P, S]), st.ps("var", [P, S])
        sq, xc = st.sb("sq", [P, 2, S]), st.sb("xc", [P, 2, S])
        res = st.sb("res", [P, 2, S])
        rstd, var, mean = st.sb("rstd", [P, S]), st.sb("var_s", [P, S]), st.sb("mean_s", [P, S])
        centred_x = st.sb("cx", [P, kt, S]) if centre else x
        mean_ready, mean_here, centred, squared, summed, var_ready = (
            st.sem(n) for n in ("mean_ready", "mean_here", "centred", "squared", "summed", "var_ready"))
        rstd_ready, scaled, normed, chain, achain, parted, stored = (
            st.sem(n) for n in ("rstd_ready", "scaled", "normed", "chain", "achain", "parted", "stored"))

        def result(k):
            return out[:, k, :] if out is not None else res[:, k % 2, :]

        with nc.Block() as block:
            @block.tensor
            def _(pe):
                if centre:
                    for k in range(kt):
                        last = pe.matmul(mean_p[:, :], c.tab("ones"), x[:, k, :], start=k == 0, stop=k == kt - 1)
                    last.then_inc(mean_ready, 1)
                for k in range(kt):
                    pe.wait_ge(squared, k + 1)
                    pe.matmul(var_p[:, :], c.tab("ones"), sq[:, k % 2, :], start=k == 0,
                              stop=k == kt - 1).then_inc(summed, 1)

            @block.scalar
            def _(act):
                act.preload_act_table_set("natural_log_exp_and_others")
                q = InOrder(act, achain)
                for k in range(kt):
                    if centre:
                        act.wait_ge(centred, k + 1)
                    if k >= 2:
                        act.wait_ge(summed, k - 1)
                    act.activation(sq[:, k % 2, :], centred_x[:, k, :], ACT.Square).then_inc(squared, 1)
                act.wait_ge(var_ready, 1)
                q(act.activation(rstd[:, :], var[:, :], ACT.Ln))
                act.activation(rstd[:, :], rstd[:, :], ACT.Exp, scale=-0.5).then_inc(rstd_ready, 1)
                for k in range(kt):
                    act.wait_ge(scaled, k + 1)
                    if out is None and k >= 2:
                        act.wait_ge(parted, k - 1)
                    act.activation(result(k), xc[:, k % 2, :], ACT.Identity, scale=g(k),
                                   bias=b(k) if b else 0.0).then_inc(normed, 1)

            @block.vector
            def _(dve):
                q = InOrder(dve, chain)
                if centre:
                    dve.wait_ge(mean_ready, 1)
                    dve.tensor_scalar(mean[:, :], mean_p[:, :], 1.0 / width, None, ALU.mult).then_inc(mean_here, 1)
                    dve.wait_ge(mean_here, 1)
                    for k in range(kt):
                        dve.tensor_tensor(centred_x[:, k, :], x[:, k, :], mean[:, :], ALU.subtract).then_inc(centred, 1)
                dve.wait_ge(summed, kt)
                dve.tensor_scalar(var[:, :], var_p[:, :], 1.0 / width, eps, ALU.mult, ALU.add).then_inc(var_ready, 1)
                dve.wait_ge(rstd_ready, 1)
                for k in range(kt + 1):
                    if k < kt:
                        if k >= 2:
                            dve.wait_ge(normed, k - 1)
                        dve.tensor_tensor(xc[:, k % 2, :], centred_x[:, k, :], rstd[:, :], ALU.mult).then_inc(scaled, 1)
                    if k and pair is not None:
                        dve.wait_ge(normed, k)
                        split(dve, q, result(k - 1), pair, (slice(None), k - 1, slice(None)), parted)

            if sink_d is not None:
                @block.sync
                def _(sp):
                    sp.wait_ge(normed, kt)
                    sp.dma_start(sink_d, out[:, :, :]).then_inc(stored, 16)
                    sp.wait_ge(stored, 16)


def split_all(c, name, x, kt, pair):
    nc = c.nc
    with Stage(nc, name) as st:
        chain, parted = st.sem("chain"), st.sem("parted")
        with nc.Block() as block:
            @block.vector
            def _(dve):
                q = InOrder(dve, chain)
                for k in range(kt):
                    split(dve, q, x[:, k, :], pair, (slice(None), k, slice(None)), parted)


class Piece:

    def __init__(self, tile, bank, x, kt, k0=0, start=True, stop=True, source=None):
        self.tile, self.bank, self.x, self.kt, self.k0, self.start, self.stop = tile, bank, x, kt, k0, start, stop
        self.source = source


def linear(c, st, n, pieces, acc, done, act_epilogue, dve_epilogue, chain, slots=2):
    nc = c.nc
    per = len(pieces)
    tiles = pieces[-1].tile + 1
    feed = Feed(st, max(p.kt for p in pieces) * P, per, slots)
    ends = [m + 1 == per or pieces[m + 1].tile != pieces[m].tile for m in range(per)]
    with nc.Block() as block:
        @block.sync
        def _(sp):
            def body(r, first):
                for m, p in enumerate(pieces):
                    feed.load(sp, r, m, first, p.source(r))
            rounds(sp, n, body)

        @block.tensor
        def _(pe):
            def body(r, first):
                for m, p in enumerate(pieces):
                    if (m == 0 or ends[m - 1]) and (not first or p.tile >= 2):
                        pe.wait_ge(done, r * tiles + p.tile - 1)
                    feed.products(pe, r, m, acc[:, p.tile % 2, p.bank, :], p.x, p.k0, p.kt, p.start, p.stop)
            rounds(pe, n, body)

        @block.scalar
        def _(act):
            for m in range(slots):
                feed.round(act, 0, m, True, pieces[m].kt * P)

            def body(r, first, last):
                for m, p in enumerate(pieces):
                    if m + slots < per or not last:
                        feed.round(act, r, m + slots, False, pieces[(m + slots) % per].kt * P)
                    if ends[m]:
                        act.wait_ge(feed.used, r * per + m + 1)
                        act_epilogue(act, r, p.tile, first)
            rounds3(act, n, body)

        @block.vector
        def _(dve):
            for m in range(slots):
                feed.rest(dve, 0, m, pieces[m].kt * P)
            q = InOrder(dve, chain)

            def body(r, first, last):
                for m, p in enumerate(pieces):
                    if m + slots < per or not last:
                        feed.rest(dve, r, m + slots, pieces[(m + slots) % per].kt * P)
                    if ends[m]:
                        dve_epilogue(dve, q, r, p.tile, first)
            rounds3(dve, n, body, q)


def swiglu_up(c, name, w_d, x, hidden, n):
    with Stage(c.nc, name) as st:
        acc = st.ps("acc", [P, 2, 2, S])
        gate, prod = st.sb("gate", [P, 2, S]), st.sb("prod", [P, 2, S])
        gated, chain, done = st.sem("gated"), st.sem("chain"), st.sem("done")

        def act_epilogue(act, r, i, first):
            if not first or i >= 2:
                act.wait_ge(done, 2 * r + i - 1)
            act.activation(gate[:, i, :], acc[:, i, 0, :], ACT.Silu).then_inc(gated, 1)

        def dve_epilogue(dve, q, r, i, first):
            dve.wait_ge(gated, 2 * r + i + 1)
            q(dve.tensor_tensor(prod[:, i, :], gate[:, i, :], acc[:, i, 1, :], ALU.mult))
            split(dve, q, prod[:, i, :], hidden, (slice(None), 2 * r + i, slice(None)), done)

        pieces = [Piece(i, part, x, DT, source=lambda r, i=i, part=part: w_d[2 * r + i, :, part, :])
                  for i in range(2) for part in range(2)]
        linear(c, st, n // 2, pieces, acc, done, act_epilogue, dve_epilogue, chain)


def project(c, name, w_d, src, kt, n, out=None, residual=None, res_scale=1.0, scale=1.0, func=ACT.Copy, pair=None):
    with Stage(c.nc, name) as st:
        acc, tmp = st.ps("acc", [P, 2, 1, S]), st.sb("tmp", [P, 2, S])
        scaled, chain, done = st.sem("scaled"), st.sem("chain"), st.sem("done")
        cuts = 1 if kt <= 11 else 2
        kc = kt // cuts

        def act_epilogue(act, r, i, first):
            if not first or i >= 2:
                act.wait_ge(done, 2 * r + i - 1)
            act.activation(tmp[:, i, :], acc[:, i, 0, :], func, scale=scale).then_inc(scaled, 1)

        def dve_epilogue(dve, q, r, i, first):
            dve.wait_ge(scaled, 2 * r + i + 1)
            if residual is not None:
                dve.scalar_tensor_tensor(out[:, 2 * r + i, :], residual[:, 2 * r + i, :], res_scale,
                                         tmp[:, i, :], ALU.mult, ALU.add).then_inc(done, 1)
            elif pair is not None:
                split(dve, q, tmp[:, i, :], pair, (slice(None), 2 * r + i, slice(None)), done)
            else:
                dve.tensor_copy(out[:, 2 * r + i, :], tmp[:, i, :]).then_inc(done, 1)

        pieces = [Piece(i, 0, src, kc, k0=h * kc, start=h == 0, stop=h == cuts - 1,
                        source=lambda r, i=i, h=h: w_d[2 * r + i, :, h * kc * P:(h + 1) * kc * P])
                  for i in range(2) for h in range(cuts)]
        linear(c, st, n // 2, pieces, acc, done, act_epilogue, dve_epilogue, chain)


def conv_glu_up(c, name, w_d, x, hidden, n, gate_w, gate_b, val_w=None, val_b=None):
    sides = 2 if val_w is not None else 1
    with Stage(c.nc, name) as st:
        acc = st.ps("acc", [P, 2, 2, S])
        pad = st.sb("pad", [P, 2, 2, S + 2])
        conv = st.sb("conv", [P, 2, S])
        gate, prod = st.sb("gate", [P, 2, S]), st.sb("prod", [P, 2, S])
        zeroed, padded, chain, convolved, gated, done = (
            st.sem(n) for n in ("zeroed", "padded", "chain", "convolved", "gated", "done"))
        with c.nc.Block() as block:
            @block.vector
            def _(dve):
                dve.memset(pad[:, :, :, 0:2], 0.0).then_inc(zeroed, 1)

        def act_epilogue(act, r, i, first):
            if not first or i >= 2:
                act.wait_ge(done, 2 * r + i - 1)
            for side in range(sides):
                act.activation(pad[:, i, side, 2:], acc[:, i, side, :], ACT.Copy).then_inc(padded, 1)
            act.wait_ge(convolved, 2 * r + i + 1)
            act.activation(gate[:, i, :], gate[:, i, :], ACT.Silu).then_inc(gated, 1)

        def dve_epilogue(dve, q, r, i, first):
            t = 2 * r + i
            for side in range(sides):
                cw, cb = (gate_w, gate_b) if side == 0 else (val_w, val_b)
                dve.wait_ge(padded, sides * t + side + 1)
                a = gate[:, i, :] if side == 0 else conv[:, i, :]
                q(dve.tensor_scalar(a, pad[:, i, side, 0:S], cw(0, t), cb(t), ALU.mult, ALU.add))
                q(dve.scalar_tensor_tensor(a, pad[:, i, side, 1:S + 1], cw(1, t), a, ALU.mult, ALU.add))
                last = dve.scalar_tensor_tensor(a, pad[:, i, side, 2:S + 2], cw(2, t), a, ALU.mult, ALU.add)
                if side:
                    q(last)
                else:
                    last.then_inc(convolved, 1)
            dve.wait_ge(gated, t + 1)
            value = conv[:, i, :] if sides == 2 else acc[:, i, 1, :]
            q(dve.tensor_tensor(prod[:, i, :], gate[:, i, :], value, ALU.mult))
            split(dve, q, prod[:, i, :], hidden, (slice(None), t, slice(None)), done)

        pieces = [Piece(i, part, x, DT, source=lambda r, i=i, part=part: w_d[2 * r + i, :, part, :])
                  for i in range(2) for part in range(2)]
        linear(c, st, n // 2, pieces, acc, done, act_epilogue, dve_epilogue, chain)


def merge(c, name, x, w_d, branches, kt, so_far=None, out=None, pair=None, gate_b=None):
    with Stage(c.nc, name) as st:
        acc = st.ps("acc", [P, 2, 2, S])
        gate, part = st.sb("gate", [P, 2, S]), st.sb("part", [P, 2, S])
        gated, chain, done = st.sem("gated"), st.sem("chain"), st.sem("done")

        def act_epilogue(act, m, b, first):
            if not first or b >= 2:
                act.wait_ge(done, 2 * m + b - 1)
            act.activation(gate[:, b, :], acc[:, b, 0, :], ACT.Sigmoid,
                           bias=gate_b(b, m) if gate_b else 0.0).then_inc(gated, 1)

        def dve_epilogue(dve, q, m, b, first):
            dve.wait_ge(gated, 2 * m + b + 1)
            if b == 0:
                if not first:
                    dve.wait_ge(done, 2 * m)
                dve.tensor_tensor(part[:, 0, :], gate[:, 0, :], acc[:, 0, 1, :], ALU.mult).then_inc(done, 1)
                return
            q(dve.tensor_tensor(part[:, 1, :], gate[:, 1, :], acc[:, 1, 1, :], ALU.mult))
            dve.wait_ge(done, 2 * m + 1)
            if so_far is not None:
                q(dve.tensor_tensor(part[:, 1, :], part[:, 1, :], so_far[:, m, :], ALU.add))
            if pair is None:
                dve.tensor_tensor(out[:, m, :], part[:, 0, :], part[:, 1, :], ALU.add).then_inc(done, 1)
            else:
                q(dve.tensor_tensor(part[:, 1, :], part[:, 0, :], part[:, 1, :], ALU.add))
                split(dve, q, part[:, 1, :], pair, (slice(None), m, slice(None)), done)

        pieces = []
        for b in range(2):
            pieces += [Piece(b, 0, x, DT, source=lambda m, b=b: w_d[m, b, :, 0:D]),
                       Piece(b, 1, branches[b], kt, source=lambda m, b=b: w_d[m, b, :, D:D + kt * P])]
        linear(c, st, DT, pieces, acc, done, act_epilogue, dve_epilogue, chain)


class Ahead:

    def __init__(self, st, c, x, w_d, n, inbox, banks, slots, bias=None):
        self.c, self.x, self.w_d, self.n = c, x, w_d, n
        self.inbox, self.banks, self.bias = inbox, banks, bias or {}
        self.per = len(inbox)
        self.slots = slots
        self.feed = Feed(st, D, self.per, slots)
        self.moved = st.sem("moved")

    def sync(self, sp, r, first):
        for m in range(self.per):
            self.feed.load(sp, r, m, first, self.w_d[r, :, m, :])

    def sync_end(self, sp):
        for m in range(self.feed.slots):
            self.feed.load(sp, self.n, m, False, self.w_d[0, :, m, :])

    def tensor(self, pe, r, m, first=False, some=None):
        if (some is None or some[0] == 0) and (not first or m >= len(self.banks)):
            pe.wait_ge(self.moved, r * self.per + m - len(self.banks) + 1)
        self.feed.products(pe, r, m, self.banks[m % len(self.banks)], self.x, 0, DT, some=some)

    def tensor_share(self, pe, r, share, shares):
        n = self.per * DT // shares
        for m in range(self.per):
            some = [k for k in range(DT) if share * n <= m * DT + k < (share + 1) * n]
            if some:
                self.tensor(pe, r, m, some=some)

    def scalar(self, act, r, m):
        act.wait_ge(self.feed.used, r * self.per + m + 1)
        bank = self.banks[m % len(self.banks)]
        if m in self.bias:
            act.activation(self.inbox[m], bank, ACT.Identity, bias=self.bias[m](r)).then_inc(self.moved, 1)
        else:
            act.activation(self.inbox[m], bank, ACT.Copy).then_inc(self.moved, 1)
        self.feed.round(act, r, m + self.feed.slots, False, D)

    def vector(self, dve, r, m):
        self.feed.rest(dve, r, m + self.feed.slots, D)

    def tensor_start(self, pe):
        for m in range(self.per):
            self.tensor(pe, 0, m, True)

    def scalar_start(self, act):
        for m in range(self.feed.slots):
            self.feed.round(act, 0, m, True, D)
        for m in range(self.per):
            self.scalar(act, 0, m)

    def vector_start(self, dve):
        for m in range(self.feed.slots):
            self.feed.rest(dve, 0, m, D)
        for m in range(self.per):
            self.vector(dve, 0, m)

    def landed(self, eng, r, m=None):
        eng.wait_ge(self.moved, (r + 1) * self.per if m is None else r * self.per + m + 1)


def attention(c, name, x, w_d, y, spans, qb=None, kb=None, vb=None, sinks=None, forget=None, rope=False):
    nc = c.nc
    scale = 0.125
    pairs = DT
    with Stage(nc, name) as st:
        box = st.sb("box", [P, 3, S])
        qz, vz = st.sb("qz", [P, 2, S]), st.sb("vz", [P, 2, TT, P])
        kk = st.sb("kk", [P, S])
        qr, kr, rq = box[:, 0, :], box[:, 1, :], st.sb("rq", [P, S])
        out = st.sb("out", [P, S])
        prob, probT = st.sb("prob", [P, 2, S]), st.sb("probT", [P, 4, S])
        pick, sink = st.sb("pick", [P, 2, P]), st.sb("sink", [P, 2])
        top, nmax, rsum, esink, rinv = (st.sb(n, [P, 8]) for n in ("top", "nmax", "rsum", "esink", "rinv"))
        sc, tr, o, pj = st.ps("sc", [P, 3, S]), st.ps("tr", [P, 2, S]), st.ps("o", [P, S]), st.ps("pj", [P, 2, S])
        vturned, zeroed, parted, outed, turned, roped, q_ready, k_ready, v_ready = (
            st.sem(n) for n in ("vturned", "zeroed", "parted", "outed", "turned", "roped", "q_ready", "k_ready", "v_ready"))
        scored, maxed, exped, normed, transposed, copied, weighed, stored, chain, achain, picked = (
            st.sem(n) for n in ("scored", "maxed", "exped", "normed", "transposed", "copied", "weighed", "stored",
                                "chain", "achain", "picked"))
        ahead = Ahead(st, c, x, w_d, pairs, [box[:, m, :] for m in range(3)], [pj[:, m, :] for m in range(2)], 3,
                      {0: qb, 1: kb, 2: vb} if qb else {})
        fetch = {4: 0, 7: 1}

        with nc.Block() as block:
            @block.sync
            def _(sp):
                rounds(sp, pairs, lambda p, first: ahead.sync(sp, p, first))
                ahead.sync_end(sp)

            @block.tensor
            def _(pe):
                ahead.tensor_start(pe)

                def body(p, first, last_round):
                    if rope:
                        ahead.landed(pe, p, 1)
                        if not first:
                            pe.wait_ge(exped, 8 * p)
                        pe.matmul(sc[:, 2, :], c.tab("rot"), qr[:, :], start=True, stop=True).then_inc(turned, 1)
                        pe.matmul(sc[:, 0, :], c.tab("rot"), kr[:, :], start=True, stop=True).then_inc(turned, 1)
                    ahead.landed(pe, p)
                    if not first:
                        pe.wait_ge(copied, 8 * p)
                    for t in range(TT):
                        last = pe.transpose(tr[:, 1, tile_cols(t)], box[:, 2, tile_cols(t)], c.tab("ident"))
                    last.then_inc(vturned, 1)
                    pe.wait_ge(q_ready, 2 * (p + 1))
                    pe.wait_ge(k_ready, p + 1)
                    if forget is not None:
                        pe.wait_ge(picked, 2 * (p + 1))

                    def scores(u):
                        i, h = u // 2, u % 2
                        if u >= 3:
                            pe.wait_ge(exped, 8 * p + u - 2)
                        elif not first:
                            pe.wait_ge(exped, 8 * p)
                        k0, n = spans[i][0] * P, len(spans[i]) * P
                        pe.matmul(sc[:, u % 3, 0:n], qz[:, h, tile_cols(i)], kk[:, k0:k0 + n], start=True, stop=False)
                        if forget is not None:
                            pe.matmul(sc[:, u % 3, 0:n], pick[:, h, :], forget[:, k0:k0 + n], start=False, stop=False)
                        if rope and i:
                            pe.matmul(sc[:, u % 3, 0:P], c.tab("ident"), c.tab("mask_prev"), start=False, stop=False)
                        pe.matmul(sc[:, u % 3, n - P:n], c.tab("ident"), c.tab("mask_diag"), start=False,
                                  stop=True).then_inc(scored, 1)

                    for u in range(3):
                        scores(u)
                    pe.wait_ge(v_ready, 2 * (p + 1))
                    for u in range(8):
                        i, h = u // 2, u % 2
                        if not last_round:
                            ahead.tensor_share(pe, p + 1, u, 8)
                        pe.wait_ge(normed, 8 * p + u + 1)
                        if not first or u >= 2:
                            pe.wait_ge(copied, 8 * p + u - 1)
                        for b in range(len(spans[i])):
                            last = pe.transpose(tr[:, u % 2, tile_cols(b)], prob[:, u % 2, tile_cols(b)], c.tab("ident"))
                        last.then_inc(transposed, 1)
                        if u + 3 < 8:
                            scores(u + 3)
                        if h:
                            pe.wait_ge(copied, 8 * p + u + 1)
                            if i == 0 and not first:
                                pe.wait_ge(stored, p)
                            n = len(spans[i])
                            for g in range(2):
                                for b in range(n):
                                    last = pe.matmul(o[:, tile_cols(i)], vz[:, g, spans[i][b], :],
                                                     probT[:, (u - 1 + g) % 4, tile_cols(b)],
                                                     start=g == 0 and b == 0, stop=g == 1 and b == n - 1)
                            last.then_inc(weighed, 1)
                rounds3(pe, pairs, body)

            @block.scalar
            def _(act):
                act.wait_ge(zeroed, 2)
                act.preload_act_table_set("exp_and_others")
                q = InOrder(act, achain)
                ahead.scalar_start(act)

                def body(p, first, last_round):
                    if not first:
                        act.wait_ge(scored, 8 * p)
                        act.wait_ge(weighed, 4 * p)
                    if not rope:
                        ahead.landed(act, p)
                        for h in range(2):
                            half = slice(64 * h, 64 * h + 64)
                            act.activation(qz[half, h, :], box[half, 0, :], ACT.Copy).then_inc(q_ready, 1)
                        act.activation(kk[:, :], box[:, 1, :], ACT.Copy).then_inc(k_ready, 1)
                    act.wait_ge(vturned, p + 1)
                    for h in range(2):
                        half = slice(64 * h, 64 * h + 64)
                        act.activation(vz[:, h, :, half], tr[:, 1, :].rearrange("p (t f) -> p t f", t=TT)[:, :, half],
                                       ACT.Copy).then_inc(v_ready, 1)

                    if sinks is not None:
                        q(act.activation(sink[:, :], sinks(2 * p, 2), ACT.Copy))

                    def exps(u):
                        i = u // 2
                        n = len(spans[i]) * P
                        act.wait_ge(maxed, 8 * p + u + 1)
                        if sinks is not None:
                            q(act.activation(esink[:, u:u + 1], sink[:, u % 2:u % 2 + 1], ACT.Exp, bias=nmax[:, u:u + 1]))
                        if not first or u >= 2:
                            act.wait_ge(transposed, 8 * p + u - 1)
                        act.activation(prob[:, u % 2, 0:n], sc[:, u % 3, 0:n], ACT.Exp, scale=scale,
                                       bias=nmax[:, u:u + 1], accum_out=rsum[:, u:u + 1]).then_inc(exped, 1)

                    def copies(u):
                        i = u // 2
                        n = len(spans[i]) * P
                        act.wait_ge(transposed, 8 * p + u + 1)
                        if not first or u >= 4:
                            act.wait_ge(weighed, 4 * p + i - 1)
                        act.activation(probT[:, u % 4, 0:n], tr[:, u % 2, 0:n], ACT.Copy).then_inc(copied, 1)

                    exps(0)
                    exps(1)
                    for u in range(8):
                        if u in fetch and not last_round:
                            if fetch[u] == 0:
                                act.wait_ge(q_ready, 2 * (p + 1))
                                act.wait_ge(k_ready, p + 1)
                            ahead.scalar(act, p + 1, fetch[u])
                        copies(u)
                        if u + 2 < 8:
                            exps(u + 2)
                    act.wait_ge(weighed, 4 * (p + 1))
                    if not first:
                        act.wait_ge(parted, p)
                    act.activation(out[:, :], o[:, :], ACT.Copy).then_inc(stored, 1)
                    if not last_round:
                        ahead.scalar(act, p + 1, 2)
                rounds3(act, pairs, body, q)

            @block.vector
            def _(dve):
                dve.memset(qz[:, :, :], 0.0).then_inc(zeroed, 1)
                dve.memset(vz[:, :, :, :], 0.0).then_inc(zeroed, 1)
                dve.wait_ge(zeroed, 2)
                q = InOrder(dve, chain)
                ahead.vector_start(dve)

                def store(p):
                    dve.wait_ge(stored, p + 1)
                    dve.tensor_copy(y.hi[:, p, :], out[:, :]).then_inc(outed, 1)
                    dve.wait_ge(outed, p + 1)
                    dve.tensor_tensor(y.lo[:, p, :], out[:, :], y.value[:, p, :], ALU.subtract).then_inc(parted, 1)

                def body(p, first, last_round):
                    if forget is not None:
                        if not first:
                            dve.wait_ge(scored, 8 * p)
                        for h in range(2):
                            pick_row(dve, c, pick[:, h, :], 2 * p + h).then_inc(picked, 1)
                    if rope:
                        if not first:
                            dve.wait_ge(scored, 8 * p)
                        for part, (raw, src) in enumerate(((qr, 2), (kr, 0))):
                            dve.wait_ge(turned, 2 * p + part + 1)
                            q(dve.tensor_tensor(rq[:, :], sc[:, src, :], c.tab("sin"), ALU.mult))
                            q(dve.tensor_tensor(raw[:, :], raw[:, :], c.tab("cos"), ALU.mult))
                            if part == 0:
                                for h in range(2):
                                    half = slice(64 * h, 64 * h + 64)
                                    dve.tensor_tensor(qz[half, h, :], raw[half, :], rq[half, :], ALU.add).then_inc(q_ready, 1)
                                dve.wait_ge(q_ready, 2 * (p + 1))
                            else:
                                dve.tensor_tensor(kk[:, :], raw[:, :], rq[:, :], ALU.add).then_inc(k_ready, 1)

                    def maxima(u):
                        n = len(spans[u // 2]) * P
                        dve.wait_ge(scored, 8 * p + u + 1)
                        q(dve.tensor_reduce(top[:, u:u + 1], sc[:, u % 3, 0:n], AX_X, ALU.max))
                        if sinks is None:
                            dve.tensor_scalar(nmax[:, u:u + 1], top[:, u:u + 1], -scale, None, ALU.mult).then_inc(maxed, 1)
                        else:
                            q(dve.tensor_scalar(top[:, u:u + 1], top[:, u:u + 1], scale, sinks(2 * p + u % 2), ALU.mult, ALU.max))
                            dve.tensor_scalar(nmax[:, u:u + 1], top[:, u:u + 1], -1.0, None, ALU.mult).then_inc(maxed, 1)

                    def normalise(u):
                        n = len(spans[u // 2]) * P
                        dve.wait_ge(exped, 8 * p + u + 1)
                        if sinks is not None:
                            q(dve.tensor_tensor(rsum[:, u:u + 1], rsum[:, u:u + 1], esink[:, u:u + 1], ALU.add))
                        q(dve.reciprocal(rinv[:, u:u + 1], rsum[:, u:u + 1]))
                        dve.tensor_scalar(prob[:, u % 2, 0:n], prob[:, u % 2, 0:n], rinv[:, u:u + 1], None,
                                          ALU.mult).then_inc(normed, 1)

                    maxima(0)
                    maxima(1)
                    for u in range(8):
                        if u in fetch and not last_round:
                            ahead.vector(dve, p + 1, fetch[u])
                        if u == 1 and not first:
                            store(p - 1)
                        normalise(u)
                        if u + 2 < 8:
                            maxima(u + 2)
                    if last_round:
                        store(p)
                    else:
                        ahead.vector(dve, p + 1, 2)
                rounds3(dve, pairs, body, q)


def pick_row(dve, c, out, row):
    return dve.tensor_scalar(out, c.tab("ones"), c.table[:, bass.ds(TABLE_AT["ident"][0] + row, 1)], None, ALU.mult)


def forget_rows(c, name, x, w_d, out, bias):
    nc = c.nc
    with Stage(nc, name) as st:
        feed = Feed(st, D, 1, 1)
        row, neg = st.sb("row", [P, S]), st.sb("neg", [P, S])
        acc = st.ps("acc", [P, S])
        achain, chain = st.sem("achain"), st.sem("chain")
        steps = Steps(st.sem("steps"), "biased least soft done")
        with nc.Block() as block:
            @block.sync
            def _(sp):
                feed.load(sp, 0, 0, True, w_d)

            @block.tensor
            def _(pe):
                feed.products(pe, 0, 0, acc[:, :], x, 0, DT)

            @block.scalar
            def _(act):
                q = InOrder(act, achain)
                feed.round(act, 0, 0, True, D)
                act.wait_ge(feed.used, 1)
                steps.done(act.activation(row[:, :], acc[:, :], ACT.Identity, bias=bias), "biased")
                steps.wait(act, "least")
                q(act.activation(row[:, :], row[:, :], ACT.Abs))
                q(act.activation(row[:, :], row[:, :], ACT.Exp, scale=-1.0))
                steps.done(act.activation(row[:, :], row[:, :], ACT.Ln, bias=1.0), "soft")

            @block.vector
            def _(dve):
                q = InOrder(dve, chain)
                feed.rest(dve, 0, 0, D)
                steps.wait(dve, "biased")
                steps.done(dve.tensor_scalar(neg[:, :], row[:, :], 0.0, None, ALU.min), "least")
                steps.wait(dve, "soft")
                q(dve.tensor_tensor(neg[:, :], neg[:, :], row[:, :], ALU.subtract))
                q(dve.tensor_scalar(neg[:, :], neg[:, :], -8.0, None, ALU.mult))
                q(dve.memset(row[:, :], 1.0))
                q(dve.memset(out[:, :], 0.0))
                steps.done(dve.tensor_tensor_scan(out[0:16, :], row[0:16, :], neg[0:16, :], 0.0, ALU.mult, ALU.add), "done")


def log_sigmoid_act(act, q, u, v):
    q(act.activation(u, v, ACT.Abs))
    q(act.activation(u, u, ACT.Exp, scale=-1.0))
    return act.activation(u, u, ACT.Ln, bias=1.0)


def linear_recurrence(c, name, x, w_d, heads, y, kind, norm_g, qb=None, fb=None, vb=None, ogb=None, lb=None,
                      small=None, fup_d=None):
    nc = c.nc
    gla = kind == "gla"
    with Stage(nc, name) as st:
        lower = st.sem("lower")
        box = st.sb("box", [P, 5, S])
        fup = st.sb("fup", [P, P])
        q_, f_, og, g, u, qd, kinv, kend, eg = (st.sb(n, [P, S]) for n in ("q", "f", "og", "g", "u", "qd", "kinv", "kend", "eg"))
        v = st.sb("v", [P, TT, P])
        a = st.sb("a", [P, TT, P])
        kt = st.sb("kt", [P, 2, TT, P])
        state = st.sb("state", [P, NC, P])
        lbc, olb = st.sb("lbc", [P, 8]), st.sb("olb", [P, 8])
        b = [st.ps(f"b{i}", [P, S]) for i in range(8)]
        zeroed, achain, chain, masked = st.sem("zeroed"), st.sem("achain"), st.sem("chain"), st.sem("masked")
        fup_landed, fup_used = st.sem("fup_landed"), st.sem("fup_used")
        steps = Steps(st.sem("steps"),
                      "activated gated logged summed decays folded scored kcopied updated "
                      "states mixed squared meaned rooted stored")
        bias = {} if gla else {0: qb, 1: fb, 2: vb, 3: ogb}
        ahead = Ahead(st, c, x, w_d, heads, [box[:, m, :] for m in range(4)], [b[6][:, :], b[7][:, :]], 2, bias)

        def low_rank(pe, r, first=False):
            if gla:
                pe.wait_ge(fup_landed, 16 * (r + 1))
                if not first:
                    steps.wait(pe, "kcopied", r - 1)
                pe.matmul(b[5][:, :], fup[:, :], small[:, :], start=True, stop=True).then_inc(fup_used, 1)

        with nc.Block() as block:
            @block.sync
            def _(sp):
                def body(h, first):
                    if gla:
                        if not first:
                            sp.wait_ge(fup_used, h)
                        sp.dma_start(fup[:, :], fup_d[h]).then_inc(fup_landed, 16)
                    ahead.sync(sp, h, first)
                rounds(sp, heads, body)
                ahead.sync_end(sp)

            @block.tensor
            def _(pe):
                ahead.tensor_start(pe)
                low_rank(pe, 0, True)

                def body(h, first, last_round):
                    if not last_round:
                        ahead.tensor(pe, h + 1, 0)
                        ahead.tensor(pe, h + 1, 1)
                    steps.wait(pe, "folded", h)
                    for t in range(TT):
                        pe.matmul(b[3][:, tile_cols(t)], kinv[:, tile_cols(t)], qd[:, tile_cols(t)], start=True, stop=True)
                    for t in range(TT):
                        pe.transpose(b[5][:, tile_cols(t)], box[:, 2, tile_cols(t)], c.tab("ident"))
                    for t in range(TT):
                        last = pe.transpose(b[4][:, tile_cols(t)], kend[:, tile_cols(t)], c.tab("ident"))
                    steps.done(last, "scored")
                    steps.wait(pe, "kcopied", h)
                    for n in range(NC - 1):
                        last = pe.matmul(b[n // 4][:, tile_cols(n % 4)], kt[:, n % 2, n // 2, :], v[:, n // 2, :],
                                         start=True, stop=True)
                    steps.done(last, "updated")
                    pe.wait_ge(masked, h + 1)
                    for t in range(TT):
                        pe.matmul(b[2][:, tile_cols(t)], v[:, t, :], a[:, t, :], start=t == 0, stop=False, skip_group_check=True)
                    steps.wait(pe, "states", h)
                    for n in range(1, NC):
                        cols = slice(n * CHUNK, (n + 1) * CHUNK)
                        last = pe.matmul(b[2][:, cols], state[:, n, :], qd[:, cols], start=False, stop=n == NC - 1,
                                         skip_group_check=True)
                    steps.done(last, "mixed")
                    if not last_round:
                        ahead.tensor(pe, h + 1, 2)
                    steps.wait(pe, "squared", h)
                    steps.done(pe.matmul(b[3][:, :], c.tab("ones"), u[:, :], start=True, stop=True), "meaned")
                    if not last_round:
                        ahead.tensor(pe, h + 1, 3)
                        low_rank(pe, h + 1)
                rounds3(pe, heads, body)

            @block.scalar
            def _(act):
                act.wait_ge(zeroed, 1)
                q = InOrder(act, achain)
                if not gla:
                    act.wait_ge(lower, 1)
                    act.activation(lbc[:, :], olb[:, :], ACT.Sigmoid).then_inc(lower, 1)
                ahead.scalar_start(act)

                def body(h, first, last_round):
                    ahead.landed(act, h)
                    if not first:
                        steps.wait(act, "stored", h - 1)
                    if gla:
                        act.wait_ge(fup_used, h + 1)
                        q(act.activation(box[:, 4, :], b[5][:, :], ACT.Identity, bias=fb(h)))
                    if gla:
                        q.free(act.activation(og[:, :], box[:, 3, :], ACT.Sigmoid))
                        act.preload_act_table_set("natural_log_exp_and_others")
                        steps.done(log_sigmoid_act(act, q, u[:, :], box[:, 4, :]), "activated")
                    else:
                        q(act.activation(og[:, :], box[:, 3, :], ACT.Sigmoid))
                        q(act.activation(q_[:, :], box[:, 0, :], ACT.Sigmoid))
                        steps.done(act.activation(f_[:, :], box[:, 1, :], ACT.Sigmoid), "activated")
                        act.preload_act_table_set("natural_log_exp_and_others")
                    steps.wait(act, "gated", h)
                    steps.done(act.activation(g[:, :], f_[:, :], ACT.Copy if gla else ACT.Ln), "logged")
                    steps.wait(act, "summed", h)
                    r = 1.0 / 16 if gla else 1.0
                    q(act.activation(u[:, :], g[:, :], ACT.Exp, scale=-r))
                    steps.done(act.activation(eg[:, :], g[:, :], ACT.Exp, scale=r), "decays")
                    if not last_round:
                        ahead.scalar(act, h + 1, 0)
                        ahead.scalar(act, h + 1, 1)
                    steps.wait(act, "scored", h)
                    q(act.activation(v[:, :, :], b[5][:, :].rearrange("p (t f) -> p t f", t=TT), ACT.Copy))
                    for half in range(2):
                        rows = slice(64 * half, 64 * half + 64)
                        last = act.activation(kt[rows, half, :, :], b[4][rows, :].rearrange("p (t f) -> p t f", t=TT), ACT.Copy)
                        if half == 0:
                            q(last)
                    steps.done(last, "kcopied")
                    steps.wait(act, "mixed", h)
                    steps.done(act.activation(u[:, :], b[2][:, :], ACT.Square), "squared")
                    if not last_round:
                        ahead.scalar(act, h + 1, 2)
                    steps.wait(act, "meaned", h)
                    q(act.activation(g[:, :], b[3][:, :], ACT.Copy, scale=1.0 / P, bias=1e-6))
                    q(act.activation(g[:, :], g[:, :], ACT.Ln))
                    steps.done(act.activation(g[:, :], g[:, :], ACT.Exp, scale=-0.5), "rooted")
                    if not last_round:
                        ahead.scalar(act, h + 1, 3)
                rounds3(act, heads, body, q)

            @block.vector
            def _(dve):
                dve.memset(kt[:, :, :, :], 0.0).then_inc(zeroed, 1)
                q = InOrder(dve, chain)

                def lbc_at(h):
                    return lbc[:, bass.ds(h, 1)]

                def olb_at(h):
                    return olb[:, bass.ds(h, 1)]

                if not gla:
                    dve.tensor_tensor(olb[:, :], lb[:, 0:8], lb[:, 8:16], ALU.subtract).then_inc(lower, 1)
                    dve.wait_ge(lower, 2)
                    q(dve.tensor_scalar(olb[:, :], lbc[:, :], -1.0, 1.0, ALU.mult, ALU.add))
                ahead.vector_start(dve)

                def body(h, first, last_round):
                    steps.wait(dve, "activated", h)
                    if gla:
                        q(dve.scalar_tensor_tensor(f_[:, :], box[:, 4, :], 0.0, u[:, :], ALU.min, ALU.subtract))
                        q(dve.tensor_scalar(q_[:, :], box[:, 0, :], 0.125, None, ALU.mult))
                        q(dve.tensor_copy(kinv[:, :], box[:, 1, :]))
                        steps.done(dve.tensor_tensor(og[:, :], og[:, :], box[:, 3, :], ALU.mult), "gated")
                    else:
                        q(dve.tensor_scalar(f_[:, :], f_[:, :], olb_at(h), lbc_at(h), ALU.mult, ALU.add))
                        q(dve.tensor_scalar(kinv[:, :], f_[:, :], -1.0, 1.0, ALU.mult, ALU.add))
                        q(dve.tensor_tensor(q_[:, :], q_[:, :], box[:, 0, :], ALU.mult))
                        steps.done(dve.tensor_tensor(og[:, :], og[:, :], box[:, 3, :], ALU.mult), "gated")
                    steps.wait(dve, "logged", h)
                    steps.done(dve.tensor_tensor_scan(g[:, :], c.tab("restart"), g[:, :], 0.0, ALU.mult, ALU.add), "summed")
                    steps.wait(dve, "decays", h)
                    q(dve.tensor_tensor(qd[:, :], q_[:, :], eg[:, :], ALU.mult))
                    q(dve.tensor_tensor(kinv[:, :], kinv[:, :], u[:, :], ALU.mult))
                    chunked = "p (n t) -> p n t"
                    ends = eg[:, :].rearrange(chunked, n=NC)[:, :, CHUNK - 1:CHUNK].broadcast_to([P, NC, CHUNK])
                    steps.done(dve.tensor_tensor(kend[:, :].rearrange(chunked, n=NC), kinv[:, :].rearrange(chunked, n=NC),
                                                 ends, ALU.mult), "folded")
                    if not last_round:
                        ahead.vector(dve, h + 1, 0)
                        ahead.vector(dve, h + 1, 1)
                    steps.wait(dve, "scored", h)
                    mask = c.tab("causal_chunk").rearrange("p (o t) -> p o t", o=1).broadcast_to([P, TT, P])
                    dve.tensor_tensor(a[:, :, :], b[3][:, :].rearrange("p (t f) -> p t f", t=TT), mask, ALU.mult).then_inc(masked, 1)
                    steps.wait(dve, "updated", h)
                    q(dve.tensor_copy(state[:, 1, :], b[0][:, 0:P]))
                    for n in range(1, NC - 1):
                        last = dve.scalar_tensor_tensor(state[:, n + 1, :], state[:, n, :], eg[:, (n + 1) * CHUNK - 1:(n + 1) * CHUNK],
                                                        b[n // 4][:, tile_cols(n % 4)], ALU.mult, ALU.add)
                        if n < NC - 2:
                            q(last)
                    steps.done(last, "states")
                    if not last_round:
                        ahead.vector(dve, h + 1, 2)
                    steps.wait(dve, "rooted", h)
                    q(dve.scalar_tensor_tensor(g[:, :], g[:, :], norm_g, og[:, :], ALU.mult, ALU.mult))
                    q(dve.tensor_tensor(g[:, :], g[:, :], b[2][:, :], ALU.mult))
                    q(dve.tensor_copy(y.hi[:, h, :], g[:, :]))
                    steps.done(dve.tensor_tensor(y.lo[:, h, :], g[:, :], y.value[:, h, :], ALU.subtract), "stored")
                    if not last_round:
                        ahead.vector(dve, h + 1, 3)
                rounds3(dve, heads, body, q)


def causal_conv(dve, q, out, pad, taps, weight, bias, done=None):
    q(dve.tensor_scalar(out, pad[:, 0:S], weight(0), bias, ALU.mult, ALU.add))
    for i in range(1, taps):
        last = dve.scalar_tensor_tensor(out, pad[:, i:i + S], weight(i), out, ALU.mult, ALU.add)
        if done is None or i < taps - 1:
            q(last)
        else:
            last.then_inc(done, 1)


def mlstm(c, name, x, w_d, heads, y, small):
    nc = c.nc
    with Stage(nc, name) as st:
        box = st.sb("box", [P, 2, S])
        pick = st.sb("pick", [P, 2, P])
        pad, qk = st.sb("pad", [P, 2, S + 3]), st.sb("qk", [P, 2, S])
        v, og = st.sb("v", [P, TT, P]), st.sb("og", [P, S])
        li, lf, u, bsum, a, top, em, hh, one = (st.sb(n, [P, S]) for n in ("li", "lf", "u", "bsum", "a", "top", "em", "hh", "one"))
        diag, acol = st.sb("diag", [P, P]), st.sb("acol", [P, TT])
        e = st.sb("e", [P, TT, S])
        b = [st.ps(f"b{i}", [P, S]) for i in range(8)]
        zeroed, achain, chain, convolved, vturned, v_ready = (
            st.sem(n) for n in ("zeroed", "achain", "chain", "convolved", "vturned", "v_ready"))
        steps = Steps(st.sem("steps"), "picked rows taken gates exps scored weighted mixed absden divided "
                                       "squared meaned rooted stored")
        ahead = Ahead(st, c, x, w_d, heads, [pad[:, 0, 3:], pad[:, 1, 3:], box[:, 0, :], box[:, 1, :]],
                      [b[6][:, :], b[7][:, :]], 2)
        with nc.Block() as block:
            @block.sync
            def _(sp):
                rounds(sp, heads, lambda h, first: ahead.sync(sp, h, first))
                ahead.sync_end(sp)

            @block.tensor
            def _(pe):
                ahead.tensor_start(pe)

                def body(h, first, last_round):
                    steps.wait(pe, "picked", h)
                    for n in range(2):
                        last = pe.matmul(b[4 + n][:, :], pick[:, n, :], small[:, :], start=True, stop=True)
                    steps.done(last, "rows")
                    if not last_round:
                        ahead.tensor(pe, h + 1, 0)
                        ahead.tensor(pe, h + 1, 1)
                    steps.wait(pe, "exps", h)
                    for j in range(TT):
                        last = pe.matmul(b[j][:, 0:S - j * P], qk[:, 1, tile_cols(j)], qk[:, 0, j * P:S], start=True, stop=True)
                    steps.done(last, "scored")
                    for t in range(TT):
                        last = pe.transpose(b[4][:, tile_cols(t)], box[:, 0, tile_cols(t)], c.tab("ident"))
                    last.then_inc(vturned, 1)
                    if not last_round:
                        ahead.tensor(pe, h + 1, 2)
                    pe.wait_ge(v_ready, h + 1)
                    steps.wait(pe, "weighted", h)
                    for out, lhs in ((b[4], v), (b[5], None)):
                        for j in range(TT):
                            last = pe.matmul(out[:, j * P:S], c.tab("ones") if lhs is None else lhs[:, j, :],
                                             e[:, j, 0:S - j * P], start=j == 0, stop=j == TT - 1)
                    steps.done(last, "mixed")
                    if not last_round:
                        ahead.tensor(pe, h + 1, 3)
                    steps.wait(pe, "squared", h)
                    steps.done(pe.matmul(b[0][:, :], c.tab("ones"), u[:, :], start=True, stop=True), "meaned")
                rounds3(pe, heads, body)

            @block.scalar
            def _(act):
                act.wait_ge(zeroed, 2)
                q = InOrder(act, achain)
                ahead.scalar_start(act)

                def body(h, first, last_round):
                    ahead.landed(act, h)
                    if not first:
                        steps.wait(act, "stored", h - 1)
                    q.free(act.activation(og[:, :], box[:, 1, :], ACT.Sigmoid))
                    act.preload_act_table_set("natural_log_exp_and_others")
                    steps.wait(act, "rows", h)
                    q(act.activation(li[:, :], b[4][:, :], ACT.Identity, bias=c.col("ml_ib", h)))
                    q(act.activation(lf[:, :], b[5][:, :], ACT.Identity, bias=c.col("ml_fb", h)))
                    steps.done(log_sigmoid_act(act, q, u[:, :], lf[:, :]), "taken")
                    act.wait_ge(convolved, h + 1)
                    for n in range(2):
                        q.free(act.activation(qk[:, n, :], qk[:, n, :], ACT.Silu))
                    if not last_round:
                        ahead.scalar(act, h + 1, 0)
                        ahead.scalar(act, h + 1, 1)
                    act.preload_act_table_set("natural_log_exp_and_others")
                    steps.wait(act, "gates", h)
                    q(act.activation(em[:, :], em[:, :], ACT.Exp, scale=-1.0))
                    for j in range(TT):
                        last = act.activation(e[:, j, 0:S - j * P], e[:, j, 0:S - j * P], ACT.Exp, bias=acol[:, j:j + 1])
                        if j < TT - 1:
                            q(last)
                    steps.done(last, "exps")
                    act.wait_ge(vturned, h + 1)
                    act.activation(v[:, :, :], b[4][:, :].rearrange("p (t f) -> p t f", t=TT), ACT.Copy).then_inc(v_ready, 1)
                    if not last_round:
                        ahead.scalar(act, h + 1, 2)
                    steps.wait(act, "mixed", h)
                    steps.done(act.activation(u[:, :], b[5][:, :], ACT.Abs), "absden")
                    if not last_round:
                        ahead.scalar(act, h + 1, 3)
                    steps.wait(act, "divided", h)
                    steps.done(act.activation(u[:, :], hh[:, :], ACT.Square), "squared")
                    steps.wait(act, "meaned", h)
                    q(act.activation(u[:, :], b[0][:, :], ACT.Copy, scale=1.0 / P, bias=1e-6))
                    q(act.activation(u[:, :], u[:, :], ACT.Ln))
                    steps.done(act.activation(u[:, :], u[:, :], ACT.Exp, scale=-0.5), "rooted")
                rounds3(act, heads, body, q)

            @block.vector
            def _(dve):
                dve.memset(pad[:, :, 0:3], 0.0).then_inc(zeroed, 1)
                dve.memset(one[:, :], 1.0).then_inc(zeroed, 1)
                dve.wait_ge(zeroed, 2)
                q = InOrder(dve, chain)
                ahead.vector_start(dve)

                def body(h, first, last_round):
                    if not first:
                        steps.wait_round(dve, h)
                    q(pick_row(dve, c, pick[:, 0, :], h))
                    steps.done(pick_row(dve, c, pick[:, 1, :], h + 4), "picked")
                    ahead.landed(dve, h)
                    for n in range(2):
                        causal_conv(dve, q, qk[:, n, :], pad[:, n, :], 4, lambda i: c.col("ml_cw", h * 8 + n * 4 + i),
                                    c.col("ml_cb", h * 2 + n), convolved if n else None)
                    steps.wait(dve, "taken", h)
                    q(dve.tensor_scalar(lf[:, :], lf[:, :], 0.0, None, ALU.min))
                    q(dve.tensor_tensor(lf[:, :], lf[:, :], u[:, :], ALU.subtract))
                    q(dve.tensor_tensor_scan(bsum[:, :], one[:, :], lf[:, :], 0.0, ALU.mult, ALU.add))
                    q(dve.tensor_tensor(a[:, :], li[:, :], bsum[:, :], ALU.subtract))
                    q(dve.tensor_tensor_scan(top[:, :], one[:, :], a[:, :], 0.0, ALU.mult, ALU.max))
                    for j in range(TT):
                        q(dve.tensor_tensor_reduce(diag[:, :], a[:, tile_cols(j)], c.tab("ident"), 1.0, 0.0, ALU.mult,
                                                   ALU.add, acol[:, j:j + 1]))
                        q(dve.tensor_tensor(e[:, j, 0:S - j * P], c.tab("mask_after")[:, 0:S - j * P], top[:, j * P:S], ALU.subtract))
                    steps.done(dve.tensor_tensor(em[:, :], bsum[:, :], top[:, :], ALU.add), "gates")
                    if not last_round:
                        ahead.vector(dve, h + 1, 0)
                        ahead.vector(dve, h + 1, 1)
                    steps.wait(dve, "scored", h)
                    for j in range(TT):
                        ej = e[:, j, 0:S - j * P]
                        last = dve.scalar_tensor_tensor(ej, b[j][:, 0:S - j * P], 0.125, ej, ALU.mult, ALU.mult)
                        if j < TT - 1:
                            q(last)
                    steps.done(last, "weighted")
                    if not last_round:
                        ahead.vector(dve, h + 1, 2)
                    steps.wait(dve, "absden", h)
                    q(dve.tensor_tensor(hh[:, :], u[:, :], em[:, :], ALU.max))
                    q(dve.reciprocal(hh[:, :], hh[:, :]))
                    steps.done(dve.tensor_tensor(hh[:, :], hh[:, :], b[4][:, :], ALU.mult), "divided")
                    if not last_round:
                        ahead.vector(dve, h + 1, 3)
                    steps.wait(dve, "rooted", h)
                    q(dve.scalar_tensor_tensor(u[:, :], u[:, :], c.col("ml_ng", h), og[:, :], ALU.mult, ALU.mult))
                    q(dve.tensor_tensor(u[:, :], u[:, :], hh[:, :], ALU.mult))
                    q(dve.tensor_copy(y.hi[:, h, :], u[:, :]))
                    steps.done(dve.tensor_tensor(y.lo[:, h, :], u[:, :], y.value[:, h, :], ALU.subtract), "stored")
                rounds3(dve, heads, body, q)


def ssd(c, name, x, w_d, y, small):
    nc = c.nc
    with Stage(nc, name) as st:
        box = st.sb("box", [P, S])
        pick = st.sb("pick", [P, 2, P])
        pad, conv = st.sb("pad", [P, 3, S + 3]), st.sb("conv", [P, 3, S])
        z, one, la = st.sb("z", [P, S]), st.sb("one", [P, S]), st.sb("la", [P, 2, S])
        dt, u = st.sb("dt", [P, 2, S]), st.sb("u", [P, 2, S])
        rate, acol, dcol = st.sb("rate", [P, 2]), st.sb("acol", [P, 2, TT]), st.sb("dcol", [P, 2, TT])
        diag = st.sb("diag", [P, P])
        e = st.sb("e", [P, 2, TT, S])
        xz = st.sb("xz", [P, 2, TT, P])
        b = [st.ps(f"b{i}", [P, S]) for i in range(8)]
        zeroed, achain, chain, summed, expd = (st.sem(n) for n in ("zeroed", "achain", "chain", "summed", "expd"))
        steps = Steps(st.sem("steps"), "picked rows taken convolved activated turned weighted mixed stored")
        ahead = Ahead(st, c, x, w_d, 4, [pad[:, 0, 3:], box[:, :], pad[:, 1, 3:], pad[:, 2, 3:]],
                      [b[6][:, :], b[7][:, :]], 1)
        with nc.Block() as block:
            @block.sync
            def _(sp):
                rounds(sp, 4, lambda i, first: ahead.sync(sp, i, first))
                ahead.sync_end(sp)

            @block.tensor
            def _(pe):
                ahead.tensor_start(pe)

                def body(i, first, last_round):
                    steps.wait(pe, "picked", i)
                    for h in range(2):
                        last = pe.matmul(b[4 + h][:, :], pick[:, h, :], small[:, :], start=True, stop=True)
                    steps.done(last, "rows")
                    steps.wait(pe, "activated", i)
                    for t in range(TT):
                        pe.transpose(b[0][:, tile_cols(t)], conv[:, 0, tile_cols(t)], c.tab("ident"))
                    for j in range(TT):
                        last = pe.matmul(b[1 + j][:, 0:S - j * P], conv[:, 1, tile_cols(j)], conv[:, 2, j * P:S], start=True, stop=True)
                    steps.done(last, "turned")
                    if not last_round:
                        for m in range(4):
                            ahead.tensor(pe, i + 1, m)
                    steps.wait(pe, "weighted", i)
                    for h in range(2):
                        for j in range(TT):
                            last = pe.matmul(b[5][:, j * P:S], xz[:, h, j, :], e[:, h, j, 0:S - j * P],
                                             start=h == 0 and j == 0, stop=h == 1 and j == TT - 1)
                    steps.done(last, "mixed")
                rounds3(pe, 4, body)

            @block.scalar
            def _(act):
                act.wait_ge(zeroed, 3)
                q = InOrder(act, achain)
                ahead.scalar_start(act)

                def body(i, first, last_round):
                    act.preload_act_table_set("natural_log_exp_and_others")
                    steps.wait(act, "rows", i)
                    for h in range(2):
                        q(act.activation(dt[:, h, :], b[4 + h][:, :], ACT.Identity, bias=c.col("sd_dtb", 2 * i + h)))
                        last = log_sigmoid_act(act, q, u[:, h, :], dt[:, h, :])
                        if h == 0:
                            q(last)
                    steps.done(last, "taken")
                    q(act.activation(rate[:, 0:1], c.col("sd_alog", 2 * i), ACT.Exp))
                    q(act.activation(rate[:, 1:2], c.col("sd_alog", 2 * i + 1), ACT.Exp))
                    ahead.landed(act, i)
                    q(act.activation(z[:, :], box[:, :], ACT.Silu))
                    steps.wait(act, "convolved", i)
                    steps.done(act.activation(conv[:, :, :], conv[:, :, :], ACT.Silu), "activated")
                    act.preload_act_table_set("natural_log_exp_and_others")
                    for h in range(2):
                        for j in range(TT):
                            act.wait_ge(summed, 8 * i + 4 * h + j + 1)
                            act.activation(e[:, h, j, 0:S - j * P], e[:, h, j, 0:S - j * P], ACT.Exp,
                                           bias=acol[:, h, j:j + 1]).then_inc(expd, 1)
                            if j % 2 and not last_round:
                                ahead.scalar(act, i + 1, 2 * h + j // 2)
                rounds3(act, 4, body, q)

            @block.vector
            def _(dve):
                dve.memset(pad[:, :, 0:3], 0.0).then_inc(zeroed, 1)
                dve.memset(one[:, :], 1.0).then_inc(zeroed, 1)
                dve.memset(xz[:, :, :, :], 0.0).then_inc(zeroed, 1)
                dve.wait_ge(zeroed, 3)
                q = InOrder(dve, chain)
                ahead.vector_start(dve)

                def body(i, first, last_round):
                    if not first:
                        steps.wait_round(dve, i)
                    q(pick_row(dve, c, pick[:, 0, :], 2 * i + 8))
                    steps.done(pick_row(dve, c, pick[:, 1, :], 2 * i + 9), "picked")
                    ahead.landed(dve, i)
                    causal_conv(dve, q, conv[:, 0, :], pad[:, 0, :], 4, lambda k: c.col("sd_cwx", i * 4 + k), c.col("sd_cbx", i))
                    for n in range(2):
                        causal_conv(dve, q, conv[:, 1 + n, :], pad[:, 1 + n, :], 4,
                                    lambda k: c.col("sd_cwbc", i * 8 + n * 4 + k), c.col("sd_cbbc", i * 2 + n))
                    steps.wait(dve, "taken", i)
                    q(dve.tensor_scalar(dt[:, :, :], dt[:, :, :], 0.0, None, ALU.max))
                    steps.done(dve.tensor_tensor(dt[:, :, :], dt[:, :, :], u[:, :, :], ALU.add), "convolved")
                    steps.wait(dve, "activated", i)
                    for h in range(2):
                        q(dve.tensor_scalar(la[:, h, :], dt[:, h, :], rate[:, h:h + 1], -1.0, ALU.mult, ALU.mult))
                        for j in range(TT):
                            ej = e[:, h, j, 0:S - j * P]
                            q(dve.tensor_tensor_scan(ej, one[:, 0:S - j * P], la[:, h, j * P:S], 0.0, ALU.mult, ALU.add))
                            q(dve.tensor_tensor_reduce(diag[:, :], ej[:, 0:P], c.tab("ident"), -1.0, 0.0, ALU.mult, ALU.add,
                                                       acol[:, h, j:j + 1]))
                            q(dve.tensor_tensor_reduce(diag[:, :], dt[:, h, tile_cols(j)], c.tab("ident"), 1.0, 0.0, ALU.mult,
                                                       ALU.add, dcol[:, h, j:j + 1]))
                            dve.tensor_tensor(ej[:, 0:P], ej[:, 0:P], c.tab("mask_after")[:, 0:P], ALU.add).then_inc(summed, 1)
                            if j % 2 and not last_round:
                                ahead.vector(dve, i + 1, 2 * h + j // 2)
                    steps.wait(dve, "turned", i)
                    for h in range(2):
                        for j in range(TT):
                            ej = e[:, h, j, 0:S - j * P]
                            dve.wait_ge(expd, 8 * i + 4 * h + j + 1)
                            q(dve.tensor_tensor(ej, ej, b[1 + j][:, 0:S - j * P], ALU.mult))
                            last = dve.tensor_scalar(xz[:, h, j, 64 * h:64 * h + 64], b[0][:, j * P + 64 * h:j * P + 64 * h + 64],
                                                     dcol[:, h, j:j + 1], None, ALU.mult)
                            if (h, j) != (1, TT - 1):
                                q(last)
                    steps.done(last, "weighted")
                    steps.wait(dve, "mixed", i)
                    q(dve.scalar_tensor_tensor(conv[:, 0, :], conv[:, 0, :], c.col("sd_d", i), b[5][:, :], ALU.mult, ALU.add))
                    steps.done(dve.tensor_tensor(y[:, i, :], conv[:, 0, :], z[:, :], ALU.mult), "stored")
                rounds3(dve, 4, body, q)


class Events:

    def __init__(self, st, **per):
        self.per = per
        self.sems = {name: st.sem(name) for name in per}

    def done(self, ins, name):
        ins.then_inc(self.sems[name], 1)

    def wait(self, eng, name, r, i=None):
        i = self.per[name] - 1 if i is None else i
        eng.wait_ge(self.sems[name], r * self.per[name] + i + 1)


def rwkv(c, name, x, w_d, up_d, y, lora):
    nc = c.nc
    with Stage(nc, name) as st:
        up = st.sb("up", [P, 3, P])
        pad = st.sb("pad", [P, 3, S + 1])
        rkv = st.sb("rkv", [P, 3, S])
        ld, g, gp, aa, kn, tmp, gg, rhat, ahat, winv, wfull, bhat, khat = (
            st.sb(n, [P, S]) for n in ("ld", "g", "gp", "aa", "kn", "tmp", "gg", "rhat", "ahat", "winv", "wfull", "bhat", "khat"))
        bt, kt = st.sb("bt", [P, 2, TT, P]), st.sb("kt", [P, 2, TT, P])
        v, ta, tnv = (st.sb(n, [P, TT, P]) for n in ("v", "ta", "tnv"))
        mt, nt, rb, rk = (st.sb(n, [P, 2, TT, P]) for n in ("mt", "nt", "rb", "rk"))
        tri, inv, part, level = (st.sb(n, [P, 2, TT, P]) for n in ("tri", "inv", "part", "level"))
        state = st.sb("state", [P, NC, P])
        b = [st.ps(f"b{i}", [P, S]) for i in range(8)]
        landed, achain, chain, pre = (st.sem(n) for n in ("landed", "achain", "chain", "pre"))
        steps = LEVELS - 1
        ev = Events(st, lora_up=1, gates=1, kshifted=1, squared=1, normed=1, decays=1, exps=1, clamped=1, rooted=1, hats=1,
                    mt_made=2, turned=1, tcopied=1, bonus_made=1, bonused=1, inv0=2, tri_made=2, side_made=6, sided=6,
                    part0=steps, part1=steps, lpart0=steps, lpart1=steps, tp0=steps, tp1=steps, level0=steps, level1=steps,
                    updated0=steps + 1, updated1=steps + 1, nv_made=1, nv_here=1, ta_made=1, ta_here=1, g_made=1, gt_here=1,
                    h_made=1, r_made=1, rfolded=1, grown=NC - 2, state=NC - 1, mixed=1, gathered0=1, gathered1=1, meaned=1,
                    centred=1, csquared=1, varied=1, croot=1, scaled=1, affine=1, stored=1)
        ahead = Ahead(st, c, x, w_d, 4, [pad[:, n, 1:] for n in range(3)], [b[7][:, :]], 1)
        fetch = {1: 0, 3: 1}
        by_tile = "p (t f) -> p t f"
        heads = [slice(64 * h, 64 * h + 64) for h in range(2)]

        def bank(n):
            return b[n][:, :].rearrange(by_tile, t=TT)

        def growth(n):
            return mt[:, n // TT, n % TT, :], nt[:, n // TT, n % TT, :]

        with nc.Block() as block:
            @block.sync
            def _(sp):
                def body(p, first):
                    ahead.sync(sp, p, first)
                    if not first:
                        ev.wait(sp, "lora_up", p - 1)
                    sp.dma_start(up[:, :, :], up_d[p]).then_inc(landed, 16)
                rounds(sp, 4, body)
                ahead.sync_end(sp)

            @block.tensor
            def _(pe):
                ahead.tensor_start(pe)

                def body(p, first, last_round):
                    pe.wait_ge(landed, 16 * (p + 1))
                    if first:
                        pe.wait_ge(pre, 3)
                    for n, out in enumerate((0, 3, 6)):
                        last = pe.matmul(b[out][:, :], up[:, n, :], lora[:, 1 if n < 2 else 2, :], start=True, stop=True)
                    ev.done(last, "lora_up")
                    ev.wait(pe, "squared", p)
                    ev.done(pe.matmul(b[4][:, :], c.tab("head_ones"), tmp[:, :], start=True, stop=True), "normed")
                    ev.wait(pe, "hats", p)

                    def pair(out, l, r_, h):
                        for t in range(TT):
                            last = pe.matmul(b[out][:, tile_cols(t)], l[heads[h], tile_cols(t)], r_[heads[h], tile_cols(t)],
                                             start=True, stop=True)
                        return last
                    for h in range(2):
                        ev.done(pair(3 * h, bhat, ahat, h), "mt_made")
                    for out, src in ((1, bhat[:, :]), (2, khat[:, :]), (4, rkv[:, 2, :]), (5, ahat[:, :])):
                        for t in range(TT):
                            last = pe.transpose(b[out][:, tile_cols(t)], src[:, tile_cols(t)], c.tab("ident"))
                    ev.done(last, "turned")
                    ev.done(pe.matmul(b[6][:, :], c.tab("head_ones"), tmp[:, :], start=True, stop=True), "bonus_made")
                    for h in range(2):
                        ev.wait(pe, "inv0", p, h)
                        for t in range(TT):
                            last = pe.transpose(b[3 * h][:, tile_cols(t)], inv[:, h, t, :], c.tab("ident"))
                        ev.done(last, "tri_made")

                    sides = [(khat, ahat, 0), (khat, ahat, 1), (bhat, rhat, 0), (bhat, rhat, 1), (khat, rhat, 0), (khat, rhat, 1)]

                    def side(k):
                        if k == 0:
                            ev.wait(pe, "bonused", p)
                        else:
                            ev.wait(pe, "sided", p, k - 1)
                        ev.done(pair(6, *sides[k]), "side_made")

                    for i in range(steps):
                        for h in range(2):
                            ev.wait(pe, f"level{h}", p, i)
                            ev.wait(pe, f"updated{h}", p, i)
                            for t in range(TT):
                                last = pe.matmul(b[3 * h][:, tile_cols(t)], level[:, h, t, :], tri[:, h, t, :], start=True, stop=True)
                            ev.done(last, f"part{h}")
                        if i < 3:
                            side(2 * i)
                        if i == 3:
                            ev.wait(pe, "sided", p)
                            for h in range(2):
                                for t in range(TT):
                                    last = pe.matmul(bank(6)[:, t, heads[h]], nt[:, h, t, :], v[:, t, heads[h]], start=True, stop=True)
                            ev.done(last, "nv_made")
                        if not last_round:
                            ahead.tensor_share(pe, p + 1, i, steps + 1)
                        if i == 0:
                            ev.wait(pe, "tcopied", p)
                        for h in range(2):
                            ev.wait(pe, f"lpart{h}", p, i)
                            if i < steps - 1:
                                for t in range(TT):
                                    pe.matmul(b[3 * h + 1][:, tile_cols(t)], inv[:, h, t, :], part[:, h, t, :], start=True, stop=True)
                            for t in range(TT):
                                last = pe.matmul(b[3 * h + 2][:, tile_cols(t)], part[:, h, t, :], inv[:, h, t, :], start=True, stop=True)
                            ev.done(last, f"tp{h}")
                        if i < 3:
                            side(2 * i + 1)
                    ev.wait(pe, "nv_here", p)
                    for h in range(2):
                        ev.wait(pe, f"updated{h}", p)
                        for out, r_ in ((0, ta), (3, tnv)):
                            for t in range(TT):
                                last = pe.matmul(bank(out)[:, t, heads[h]], inv[:, h, t, :], r_[:, t, heads[h]], start=True, stop=True)
                    ev.done(last, "ta_made")
                    if not last_round:
                        ahead.tensor_share(pe, p + 1, steps, steps + 1)
                    ev.wait(pe, "ta_here", p)
                    for n in range(1, NC - 1):
                        out = bank(1 + n // TT)[:, n % TT, :]
                        pe.matmul(out, c.tab("ident"), c.tab("ident"), start=True, stop=False)
                        last = pe.matmul(out, ta[:, n // 2, :], bt[:, n % 2, n // 2, :], start=False, stop=True)
                    ev.done(last, "g_made")
                    for n in range(NC - 1):
                        out = bank(4 + n // TT)[:, n % TT, :]
                        pe.matmul(out, kt[:, n % 2, n // 2, :], v[:, n // 2, :], start=True, stop=False)
                        last = pe.matmul(out, bt[:, n % 2, n // 2, :], tnv[:, n // 2, :], start=False, stop=True)
                    ev.done(last, "h_made")
                    for h in range(2):
                        for t in range(TT):
                            last = pe.matmul(bank(3 * h)[:, t, :], ta[:, t, :], rb[:, h, t, :], start=True, stop=True)
                    ev.done(last, "r_made")
                    ev.wait(pe, "gt_here", p)
                    for n in range(1, NC - 1):
                        ev.wait(pe, "state", p, n - 1)
                        ev.done(pe.matmul(bank(6)[:, n % TT, :], growth(n)[0], state[:, n, :], start=True, stop=True), "grown")
                        if n <= TT:
                            t = n - 1
                            for h in range(2):
                                pe.matmul(bank(1 + h)[:, t, :], tnv[:, t, :], rb[:, h, t, :], start=t == 0, stop=False,
                                          skip_group_check=True)
                                pe.matmul(bank(1 + h)[:, t, :], v[:, t, :], rk[:, h, t, :], start=False, stop=False,
                                          skip_group_check=True)
                    ev.wait(pe, "rfolded", p)
                    for n in range(1, NC):
                        cols = slice(n * CHUNK, (n + 1) * CHUNK)
                        if n == NC - 1:
                            ev.wait(pe, "state", p)
                        for h in range(2):
                            last = pe.matmul(b[1 + h][:, cols], state[:, n, :], rhat[:, cols], start=False, stop=n == NC - 1,
                                             skip_group_check=True)
                    ev.done(last, "mixed")
                    ev.wait(pe, "gathered0", p)
                    ev.wait(pe, "gathered1", p)
                    ev.done(pe.matmul(b[4][:, :], c.tab("head_ones"), kn[:, :], start=True, stop=True), "meaned")
                    ev.wait(pe, "csquared", p)
                    ev.done(pe.matmul(b[5][:, :], c.tab("head_ones"), tmp[:, :], start=True, stop=True), "varied")
                rounds3(pe, 4, body)

            @block.scalar
            def _(act):
                q = InOrder(act, achain)
                act.wait_ge(pre, 1)
                act.activation(lora[0:64, 1, :], lora[0:64, 1, :], ACT.Tanh).then_inc(pre, 1)
                act.activation(lora[:, 2, :], lora[:, 2, :], ACT.Sigmoid).then_inc(pre, 1)
                ahead.scalar_start(act)

                def body(p, first, last_round):
                    if not first:
                        ev.wait(act, "stored", p - 1)
                    ev.wait(act, "lora_up", p)
                    q.free(act.activation(ld[:, :], b[0][:, :], ACT.Sigmoid, bias=c.col("w0", p)))
                    q.free(act.activation(aa[:, :], b[3][:, :], ACT.Sigmoid, bias=c.col("a0", p)))
                    ev.done(act.activation(gg[:, :], b[6][:, :], ACT.Copy), "gates")
                    act.preload_act_table_set("natural_log_exp_and_others")
                    ev.wait(act, "kshifted", p)
                    q(act.activation(kn[:, :], rkv[:, 1, :], ACT.Copy, scale=c.col("k_k", p)))
                    ev.done(act.activation(tmp[:, :], kn[:, :], ACT.Square), "squared")
                    ev.wait(act, "decays", p)
                    q.free(act.activation(wfull[:, :], g[:, :], ACT.Exp))
                    q.free(act.activation(winv[:, :], g[:, :], ACT.Exp, scale=-1.0))
                    ev.done(act.activation(gp[:, :], gp[:, :], ACT.Exp), "exps")
                    ev.wait(act, "clamped", p)
                    q(act.activation(tmp[:, :], tmp[:, :], ACT.Ln))
                    ev.done(act.activation(tmp[:, :], tmp[:, :], ACT.Exp, scale=-0.5), "rooted")
                    ev.wait(act, "turned", p)
                    for dst, n in ((bt, 1), (kt, 2)):
                        for half in range(2):
                            rows = heads[half]
                            q.free(act.activation(dst[rows, half, :, :], b[n][rows, :].rearrange(by_tile, t=TT), ACT.Copy))
                    q.free(act.activation(v[:, :, :], bank(4), ACT.Copy))
                    ev.done(act.activation(ta[:, :, :], bank(5), ACT.Copy), "tcopied")
                    for i in range(steps):
                        for h in range(2):
                            ev.wait(act, f"part{h}", p, i)
                            ev.done(act.activation(part[:, h, :, :], bank(3 * h), ACT.Copy), f"lpart{h}")
                        if i == 3:
                            ev.wait(act, "nv_made", p)
                            ev.done(act.activation(tnv[:, :, :], bank(6), ACT.Copy), "nv_here")
                        if i in fetch and not last_round:
                            ahead.scalar(act, p + 1, fetch[i])
                    ev.wait(act, "ta_made", p)
                    q.free(act.activation(ta[:, :, :], bank(0), ACT.Copy, scale=-1.0))
                    ev.done(act.activation(tnv[:, :, :], bank(3), ACT.Copy, scale=-1.0), "ta_here")
                    if not last_round:
                        ahead.scalar(act, p + 1, 2)
                    ev.wait(act, "mixed", p)
                    ev.done(act.activation(kn[heads[1], :], b[2][heads[1], :], ACT.Copy), "gathered1")
                    ev.wait(act, "centred", p)
                    ev.done(act.activation(tmp[:, :], kn[:, :], ACT.Square), "csquared")
                    ev.wait(act, "varied", p)
                    q(act.activation(g[:, :], b[5][:, :], ACT.Copy, scale=1.0 / 64, bias=64e-5))
                    q(act.activation(g[:, :], g[:, :], ACT.Ln))
                    ev.done(act.activation(g[:, :], g[:, :], ACT.Exp, scale=-0.5), "croot")
                    ev.wait(act, "scaled", p)
                    ev.done(act.activation(kn[:, :], kn[:, :], ACT.Identity, scale=c.col("gn_g", p), bias=c.col("gn_b", p)), "affine")
                rounds3(act, 4, body, q)

            @block.vector
            def _(dve):
                q = InOrder(dve, chain)
                q(dve.memset(pad[:, :, 0:1], 0.0))
                for n in (1, 2):
                    q(dve.tensor_tensor(tmp[:, 1:S], lora[:, n, 0:S - 1], lora[:, n, 1:S], ALU.subtract))
                    q(dve.tensor_scalar(tmp[:, 0:1], lora[:, n, 0:1], -1.0, None, ALU.mult))
                    q(dve.scalar_tensor_tensor(lora[:, n, :], tmp[:, :], c.col("lora_mu", n - 1), lora[:, n, :], ALU.mult, ALU.add))
                q(dve.memset(bt[:, :, :, :], 0.0))
                dve.memset(kt[:, :, :, :], 0.0).then_inc(pre, 1)
                ahead.vector_start(dve)

                def wide(name_):
                    return c.tab(name_).rearrange("p (o t) -> p o t", o=1).broadcast_to([P, TT, P])

                def body(p, first, last_round):
                    def shift(n, mu, done=None):
                        q(dve.tensor_tensor(rkv[:, n, :], pad[:, n, 0:S], pad[:, n, 1:S + 1], ALU.subtract))
                        last = dve.scalar_tensor_tensor(rkv[:, n, :], rkv[:, n, :], c.col(mu, p), pad[:, n, 1:S + 1], ALU.mult, ALU.add)
                        if done:
                            ev.done(last, done)
                        else:
                            q.free(last)
                    ahead.landed(dve, p)
                    shift(1, "k_mu", "kshifted")
                    ev.wait(dve, "gates", p)
                    q(dve.tensor_scalar(ld[:, :], ld[:, :], -DECAY_SCALE, None, ALU.mult))
                    q(dve.tensor_tensor_scan(g[:, :], c.tab("restart"), ld[:, :], 0.0, ALU.mult, ALU.add))
                    ev.done(dve.tensor_tensor(gp[:, :], g[:, :], ld[:, :], ALU.subtract), "decays")
                    shift(0, "r_mu")
                    ev.wait(dve, "normed", p)
                    ev.done(dve.tensor_scalar(tmp[:, :], b[4][:, :], 1e-24, None, ALU.max), "clamped")
                    shift(2, "v_mu")
                    ev.wait(dve, "decays", p)
                    q(dve.tensor_scalar(ld[:, :], aa[:, :], 1.0, c.col("k_a", p), ALU.subtract, ALU.mult))
                    q(dve.scalar_tensor_tensor(rkv[:, 1, :], ld[:, :], 1.0, rkv[:, 1, :], ALU.add, ALU.mult))
                    ev.wait(dve, "exps", p)
                    q.free(dve.tensor_tensor(rhat[:, :], rkv[:, 0, :], wfull[:, :], ALU.mult))
                    q.free(dve.tensor_tensor(khat[:, :], rkv[:, 1, :], winv[:, :], ALU.mult))
                    ev.wait(dve, "rooted", p)
                    q(dve.tensor_tensor(kn[:, :], kn[:, :], tmp[:, :], ALU.mult))
                    q.free(dve.tensor_tensor(ahat[:, :], kn[:, :], gp[:, :], ALU.mult))
                    q(dve.tensor_tensor(bhat[:, :], aa[:, :], winv[:, :], ALU.mult))
                    q.free(dve.tensor_tensor(bhat[:, :], bhat[:, :], kn[:, :], ALU.mult))
                    ev.done(dve.scalar_tensor_tensor(tmp[:, :], rkv[:, 0, :], c.col("r_k", p), rkv[:, 1, :], ALU.mult, ALU.mult), "hats")
                    for h in range(2):
                        ev.wait(dve, "mt_made", p, h)
                        q(dve.tensor_tensor(mt[:, h, :, :], bank(3 * h), wide("strict_chunk"), ALU.mult))
                        q(dve.tensor_tensor(level[:, h, :, :], mt[:, h, :, :], wide("level0"), ALU.mult))
                        ev.done(dve.tensor_tensor(inv[:, h, :, :], wide("ident"), level[:, h, :, :], ALU.subtract), "inv0")
                    ev.wait(dve, "inv0", p)
                    for h in range(2):
                        ev.done(dve.tensor_tensor(level[:, h, :, :], mt[:, h, :, :], wide("level1"), ALU.mult), f"level{h}")
                    for h in range(2):
                        ev.wait(dve, "tri_made", p, h)
                        ev.done(dve.tensor_copy(tri[:, h, :, :], bank(3 * h)), f"updated{h}")
                    ev.wait(dve, "bonus_made", p)
                    ev.done(dve.tensor_tensor(aa[:, :], rkv[:, 2, :], b[6][:, :], ALU.mult), "bonused")

                    sides = [(nt, 0, "strict_chunk"), (nt, 1, "strict_chunk"), (rb, 0, "causal_chunk"), (rb, 1, "causal_chunk"),
                             (rk, 0, "causal_chunk"), (rk, 1, "causal_chunk")]

                    def side(k):
                        dst, h, mask = sides[k]
                        ev.wait(dve, "side_made", p, k)
                        ev.done(dve.tensor_tensor(dst[:, h, :, :], bank(6), wide(mask), ALU.mult), "sided")

                    for i in range(steps):
                        if i < steps - 1:
                            for h in range(2):
                                ev.wait(dve, f"part{h}", p, i)
                                ev.done(dve.tensor_tensor(level[:, h, :, :], mt[:, h, :, :], wide(f"level{i + 2}"), ALU.mult), f"level{h}")
                        if i < 3:
                            side(2 * i)
                        for h in range(2):
                            ev.wait(dve, f"tp{h}", p, i)
                            ev.wait(dve, f"updated{h}", p, i)
                            if i < steps - 1:
                                q.free(dve.tensor_tensor(tri[:, h, :, :], tri[:, h, :, :], bank(3 * h + 1), ALU.subtract))
                            ev.done(dve.tensor_tensor(inv[:, h, :, :], inv[:, h, :, :], bank(3 * h + 2), ALU.subtract), f"updated{h}")
                        if i < 3:
                            side(2 * i + 1)
                        if i in fetch and not last_round:
                            ahead.vector(dve, p + 1, fetch[i])
                    ev.wait(dve, "g_made", p)
                    mask = c.tab("head_ones").rearrange("p (o t) -> p o t", o=1).broadcast_to([P, TT - 1, P])
                    q.free(dve.tensor_tensor(mt[:, 0, 1:TT, :], bank(1)[:, 1:TT, :], mask, ALU.mult))
                    ev.done(dve.tensor_tensor(mt[:, 1, 0:TT - 1, :], bank(2)[:, 0:TT - 1, :], mask, ALU.mult), "gt_here")
                    ev.wait(dve, "h_made", p)

                    def end(n):
                        return wfull[:, (n + 1) * CHUNK - 1:(n + 1) * CHUNK]
                    for n in range(NC - 1):
                        dst = state[:, 1, :] if n == 0 else growth(n)[1]
                        h_n = dve.scalar_tensor_tensor(dst, bank(4 + n // TT)[:, n % TT, :], end(n), c.tab("head_ones"), ALU.mult, ALU.mult)
                        if n == 0:
                            ev.done(h_n, "state")
                            continue
                        q(h_n)
                        ev.wait(dve, "grown", p, n - 1)
                        ev.done(dve.scalar_tensor_tensor(state[:, n + 1, :], bank(6)[:, n % TT, :], end(n), dst, ALU.mult, ALU.add), "state")
                        if n == 2:
                            ev.wait(dve, "r_made", p)
                            q.free(dve.tensor_tensor(rhat[heads[0], :], rhat[heads[0], :], b[0][heads[0], :], ALU.add))
                            ev.done(dve.tensor_tensor(rhat[heads[1], :], rhat[heads[1], :], b[3][heads[1], :], ALU.add), "rfolded")
                    if not last_round:
                        ahead.vector(dve, p + 1, 2)
                    ev.wait(dve, "mixed", p)
                    ev.done(dve.tensor_copy(kn[heads[0], :], b[1][heads[0], :]), "gathered0")
                    ev.wait(dve, "meaned", p)
                    ev.done(dve.scalar_tensor_tensor(kn[:, :], b[4][:, :], -1.0 / 64, kn[:, :], ALU.mult, ALU.add), "centred")
                    ev.wait(dve, "croot", p)
                    ev.done(dve.tensor_tensor(kn[:, :], kn[:, :], g[:, :], ALU.mult), "scaled")
                    ev.wait(dve, "affine", p)
                    q(dve.tensor_tensor(kn[:, :], kn[:, :], aa[:, :], ALU.add))
                    q(dve.tensor_tensor(kn[:, :], kn[:, :], gg[:, :], ALU.mult))
                    q(dve.tensor_copy(y.hi[:, p, :], kn[:, :]))
                    ev.done(dve.tensor_tensor(y.lo[:, p, :], kn[:, :], y.value[:, p, :], ALU.subtract), "stored")
                rounds3(dve, 4, body, q)


def gelu_values(c, name, x, w_d, v):
    nc = c.nc
    chunks, halves, kc = 4, 2, DT // 2
    with Stage(nc, name) as st:
        feed = Feed(st, kc * S, halves, 2)
        acc = st.ps("acc", [P, 2, TT, S])
        made, done = st.sem("made"), st.sem("done")
        with nc.Block() as block:
            @block.sync
            def _(sp):
                def body(r, first):
                    for m in range(halves):
                        feed.load(sp, r, m, first, w_d[r, :, m, :])
                rounds(sp, chunks, body)

            @block.tensor
            def _(pe):
                for r in range(chunks):
                    for m in range(halves):
                        s, slot = feed.at(r, m)
                        pe.wait_ge(feed.parted, s + 1)
                        for t in range(TT):
                            if m == 0 and r >= 2:
                                pe.wait_ge(done, TT * (r - 2) + t + 1)
                            for k in range(kc):
                                for n, (a_, w_) in enumerate(((x.hi, feed.hi), (x.lo, feed.hi), (x.hi, feed.lo))):
                                    last = pe.matmul(acc[:, r % 2, t, :], a_[:, m * kc + k, tile_cols(t)],
                                                     w_[:, slot, k * S:(k + 1) * S], start=m == 0 and k == 0 and n == 0,
                                                     stop=m == halves - 1 and k == kc - 1 and n == 2)
                            if m == halves - 1 and t < TT - 1:
                                last.then_inc(made, 1)
                        last.then_inc(feed.used, 1)

            @block.scalar
            def _(act):
                for m in range(2):
                    feed.round(act, 0, m, True, kc * S)
                for r in range(chunks):
                    for m in range(halves):
                        if r < chunks - 1:
                            feed.round(act, r + 1, m, False, kc * S)
                    for t in range(TT):
                        if t < TT - 1:
                            act.wait_ge(made, (TT - 1) * r + t + 1)
                        else:
                            act.wait_ge(feed.used, halves * (r + 1))
                        act.activation(v[:, t, r * S:(r + 1) * S], acc[:, r % 2, t, :], ACT.Gelu_apprx_tanh).then_inc(done, 1)

            @block.vector
            def _(dve):
                def body(r, first):
                    for m in range(halves):
                        feed.rest(dve, r, m, kc * S)
                rounds(dve, chunks, body)


def spatial_gate(c, name, v, u, rows_d, ws_d, pair):
    nc = c.nc
    width = v.shape[2]
    groups, per = 8, 2
    with Stage(nc, name) as st:
        gb, ws, bs = st.sb("gb", [P, 2, width]), st.sb("ws", [P, groups, P]), st.sb("bs", [P, groups, P])
        total, var, mean, rstd = (st.sb(n, [P, TT]) for n in ("total", "var", "mean", "rstd"))
        acc, mixed = st.ps("acc", [P, 2, S]), st.sb("mixed_s", [P, 2, S])
        sq = st.ps("sq", [P, width])
        landed, chain, centred, squared, rooted, ready, made, done = (
            st.sem(n) for n in ("landed", "chain", "centred", "squared", "rooted", "ready", "made", "done"))
        with nc.Block() as block:
            @block.sync
            def _(sp):
                sp.dma_start(gb[:, :, :], rows_d[:, 0:2 * width].rearrange("p (a n) -> p a n", a=2)).then_inc(landed, 16)
                sp.dma_start(bs[:, :, :], rows_d[:, 2 * width:].rearrange("p (a n) -> p a n", a=groups)).then_inc(landed, 16)
                sp.dma_start(ws[:, :, :], ws_d).then_inc(landed, 16)

            @block.scalar
            def _(act):
                for t in range(TT):
                    act.wait_ge(centred, t + 1)
                    if t:
                        act.wait_ge(squared, t)
                    act.activation(sq[:, :], v[:, t, :], ACT.Square, accum_out=var[:, t:t + 1]).then_inc(squared, 1)
                act.wait_ge(rooted, 1)
                act.activation(rstd[:, :], var[:, :], ACT.Sqrt).then_inc(rooted, 1)

            @block.vector
            def _(dve):
                q = InOrder(dve, chain)
                dve.wait_ge(landed, 48)
                mask = c.tab("causal").rearrange("p (o t) -> p o t", o=1).broadcast_to([P, groups, P])
                q(dve.tensor_tensor(ws[:, :, :], ws[:, :, :], mask, ALU.mult))
                for t in range(TT):
                    q(dve.tensor_reduce(total[:, t:t + 1], v[:, t, :], AX_X, ALU.add))
                    q(dve.tensor_scalar(mean[:, t:t + 1], total[:, t:t + 1], 1.0 / width, None, ALU.mult))
                    dve.tensor_scalar(v[:, t, :], v[:, t, :], mean[:, t:t + 1], None, ALU.subtract).then_inc(centred, 1)
                dve.wait_ge(squared, TT)
                dve.tensor_scalar(var[:, :], var[:, :], 1.0 / width, 1e-5, ALU.mult, ALU.add).then_inc(rooted, 1)
                dve.wait_ge(rooted, 2)
                q(dve.reciprocal(rstd[:, :], rstd[:, :]))
                for t in range(TT):
                    q(dve.scalar_tensor_tensor(v[:, t, :], v[:, t, :], rstd[:, t:t + 1], gb[:, 0, :], ALU.mult, ALU.mult))
                    q(dve.tensor_tensor(v[:, t, :], v[:, t, :], gb[:, 1, :], ALU.add))
                q(dve.memset(total[:, :], 0.0))
                dve.memset(total[:, :], 0.0).then_inc(ready, 1)
                for m in range(groups * per):
                    dve.wait_ge(made, m + 1)
                    bias = bs[:, m // per, :].rearrange("p (o t) -> p o t", o=1).broadcast_to([P, TT, P])
                    q(dve.tensor_tensor(mixed[:, m % 2, :].rearrange("p (t f) -> p t f", t=TT),
                                        acc[:, m % 2, :].rearrange("p (t f) -> p t f", t=TT), bias, ALU.add))
                    q(dve.tensor_tensor(mixed[:, m % 2, :], u[:, m, :], mixed[:, m % 2, :], ALU.mult))
                    split(dve, q, mixed[:, m % 2, :], pair, (slice(None), m, slice(None)), done)

            @block.tensor
            def _(pe):
                pe.wait_ge(ready, 1)
                for m in range(groups * per):
                    if m >= 2:
                        pe.wait_ge(done, m - 1)
                    for t in range(TT):
                        last = pe.matmul(acc[:, m % 2, tile_cols(t)], v[:, t, tile_cols(m)], ws[:, m // per, :], start=True, stop=True)
                    last.then_inc(made, 1)


def build(nc, a, out_d):
    with ExitStack() as keep:
        def sb(name, shape, stack=keep):
            return stack.enter_context(nc.sbuf_tensor(name, shape, F32))

        def pair(name, tiles_, stack):
            return Pair(lambda n, shape, dtype: stack.enter_context(nc.sbuf_tensor(n, shape, dtype)), name, [P, tiles_, S])

        table, column = sb("table", [P, TABLE_WIDTH]), sb("column", [P, COLUMN_WIDTH])
        x = sb("x", [P, DT, S])
        c = Ctx(nc, table, column)
        load_constants(c, a["table"], a["column"], a["x"], x)

        with ExitStack() as blocks:
            xn = pair("xn", DT, blocks)
            split_all(c, "sx", x, DT, xn)
            with ExitStack() as s:
                hidden = pair("hidden1", FT, s)
                swiglu_up(c, "f1u", a["f1_up"], xn, hidden, FT)
                project(c, "f1d", a["f1_down"], hidden, FT, DT, x, residual=x, res_scale=ALPHA, scale=0.5)
            norm(c, "ln1", x, x, DT, True, 1e-5, lambda k: c.col("ln1_g", k), lambda k: c.col("ln1_b", k), xn)
            with ExitStack() as s:
                y_a = pair("y_attn", DT, s)
                attention(c, "att", xn, a["att_w"], y_a, [[0], [0, 1], [1, 2], [2, 3]],
                          qb=lambda p: c.col("att_qb", p), kb=lambda p: c.col("att_kb", p), vb=lambda p: c.col("att_vb", p),
                          sinks=lambda h, n=1: c.col("sinks", h, n), rope=True)
                y_h = pair("y_hgrn", DT, s)
                linear_recurrence(c, "hg", xn, a["hg_w"], 8, y_h, "hgrn", c.col("hg_ng"), qb=lambda h: c.col("hg_qb", h),
                                  fb=lambda h: c.col("hg_fb", h), vb=lambda h: c.col("hg_vb", h), ogb=lambda h: c.col("hg_ogb", h),
                                  lb=c.col("hg_lb", 0, 16))
                merged = pair("merged1", DT, s)
                merge(c, "mg1", xn, a["mg1_w"], [y_a, y_h], DT, pair=merged, gate_b=lambda b, m: c.col("gate_b", b * DT + m))
                project(c, "wo1", a["wo1"], merged, DT, DT, x, residual=x, res_scale=ALPHA)
            norm(c, "ln2", x, x, DT, True, 1e-5, lambda k: c.col("ln2_g", k), lambda k: c.col("ln2_b", k), xn)
            with ExitStack() as s:
                hidden = pair("hidden2", FT, s)
                swiglu_up(c, "f2u", a["f2_up"], xn, hidden, FT)
                project(c, "f2d", a["f2_down"], hidden, FT, DT, x, residual=x, res_scale=ALPHA, scale=0.5)
            norm(c, "ln3", x, x, DT, True, 1e-5, lambda k: c.col("ln3_g", k), lambda k: c.col("ln3_b", k))

            norm(c, "rn1", x, None, DT, False, 1e-6, lambda k: c.col("mix2_g", k), pair=xn)
            with ExitStack() as s:
                low = sb("low", [P, 4, S], s)
                project(c, "low", a["low_w"], xn, DT, 4, low)
                y_0 = pair("y_0", 4, s)
                rwkv(c, "rw", xn, a["rw_w"], a["rw_up"], y_0, low)
                y_1, part = pair("y_1", 4, s), sb("part", [P, DT, S], s)
                linear_recurrence(c, "gla", xn, a["gla_w"], 4, y_1, "gla", c.col("gla_ng"), fb=lambda h: c.col("gla_fb", h),
                                  small=low[:, 0, :], fup_d=a["gla_fup"])
                merge(c, "mg2", xn, a["mg2_w"][:, 0:2], [y_0, y_1], 4, out=part)
                mlstm(c, "ml", xn, a["ml_w"], 4, y_0, low[:, 0, :])
                with ExitStack() as s2:
                    y_s = sb("y_ssd", [P, 4, S], s2)
                    ssd(c, "sd", xn, a["sd_w"], y_s, low[:, 0, :])
                    norm(c, "sdn", y_s, None, 4, False, 1e-6, lambda k: c.col("sd_ng", k), pair=y_1)
                merged = pair("merged2", DT, s)
                merge(c, "mg3", xn, a["mg2_w"][:, 2:4], [y_0, y_1], 4, so_far=part, pair=merged)
                project(c, "wo2", a["wo2"], merged, DT, DT, x, residual=x)
            norm(c, "rn2", x, None, DT, False, 1e-6, lambda k: c.col("ffn2_g", k), pair=xn)
            with ExitStack() as s:
                hidden = pair("hidden3", FT, s)
                conv_glu_up(c, "f3u", a["f3_up"], xn, hidden, FT,
                            lambda i, t: c.col("ffn2_cw", i * 2 * FT + t), lambda t: c.col("ffn2_cb", t),
                            lambda i, t: c.col("ffn2_cw", i * 2 * FT + FT + t), lambda t: c.col("ffn2_cb", FT + t))
                project(c, "f3d", a["f3_down"], hidden, FT, DT, x, residual=x)
            norm(c, "rn3", x, x, DT, False, 1e-6, lambda k: c.col("fin2_g", k))

        with ExitStack() as s:
            u, v = sb("u", [P, 16, S], s), sb("v", [P, TT, 16 * P], s)
            with ExitStack() as s2:
                xn = pair("xm", DT, s2)
                norm(c, "m0", x, None, DT, False, 1e-6, lambda k: c.col("mix3_g", k), pair=xn)
                project(c, "gmu", a["gm_u"], xn, DT, 16, u, func=ACT.Gelu_apprx_tanh)
                gelu_values(c, "gmv", xn, a["gm_v"], v)
            mixed = pair("mixed", 16, s)
            spatial_gate(c, "gms", v, u, a["gm_rows"], a["gm_ws"], mixed)
            project(c, "gmo", a["gm_out"], mixed, 16, DT, x, residual=x)
        with ExitStack() as blocks:
            xn = pair("xo", DT, blocks)
            for layer in range(2):
                if layer:
                    norm(c, "m1", x, None, DT, False, 1e-6, lambda k: c.col("mix3_g", DT + k), pair=xn)
                    with ExitStack() as s:
                        y, rows = pair("y_fox", DT, s), sb("rows", [P, S], s)
                        forget_rows(c, "fr", xn, a["fox_f"], rows, c.col("fox_fb"))
                        attention(c, "fox", xn, a["fox_w"], y, [list(range(i + 1)) for i in range(TT)], forget=rows)
                        project(c, "foxo", a["fox_o"], y, DT, DT, x, residual=x)
                norm(c, f"n{layer}", x, None, DT, False, 1e-6, lambda k: c.col("ffn3_g", layer * DT + k), pair=xn)
                with ExitStack() as s:
                    hidden = pair(f"hidden4{layer}", 16, s)
                    conv_glu_up(c, f"g{layer}u", a[f"g{layer}_up"], xn, hidden, 16,
                                lambda i, t: c.col("ffn3_cw", layer * 48 + i * 16 + t), lambda t: c.col("ffn3_cb", layer * 16 + t))
                    project(c, f"g{layer}d", a[f"g{layer}_down"], hidden, 16, DT, x, residual=x)
        norm(c, "fin", x, x, DT, False, 1e-6, lambda k: c.col("fin3_g", k), sink_d=out_d)


def lay_out(i):
    i = {k: np.asarray(v) for k, v in i.items()}
    a = {}

    def tiles(w):
        k, m = w.shape
        return w.reshape(k // P, P, m // P, P).transpose(2, 1, 0, 3).reshape(m // P, P, k)

    def stack(*ws):
        return np.stack([tiles(w) for w in ws], 2)

    def columns(v):
        return v.reshape(-1, P).T

    def padded_heads(w, heads):
        out = np.zeros((w.shape[0], heads, P), w.dtype)
        out[:, :, 0:64] = w.reshape(w.shape[0], heads, 64)
        return out.reshape(w.shape[0], heads * P)

    def doubled(w):
        w = w.reshape(w.shape[0], 4, 64)
        return np.stack([w] * 4, 2).reshape(w.shape[0], 16 * 64)

    col = {}
    a["table"] = np.concatenate(list(TABLES.values()), 1)
    a["x"] = i["x"][0].T.reshape(DT, P, S).transpose(1, 0, 2)

    for n in ("ln1_g", "ln1_b", "ln2_g", "ln2_b", "ln3_g", "ln3_b"):
        col[n] = columns(i[n][0])
    for n in (1, 2):
        a[f"f{n}_up"] = stack(i[f"ffn{n}_w1"][0], i[f"ffn{n}_w3"][0])
        a[f"f{n}_down"] = tiles(i[f"ffn{n}_w2"][0])
    cuts = np.cumsum([1024, 256, 256, 1024, 1024, 1024, 1024, 1024])
    q, k, v, f, qh, ih, og, ga, gh = np.split(i["w_in"][0], cuts, 1)
    bq, bk, bv, bf, bqh, bih, bog, bga, bgh = np.split(i["b_in"], cuts, 1)
    a["att_w"] = stack(q, doubled(k), doubled(v))
    col["att_vb"] = columns(doubled(bv)[0])
    col["att_qb"], col["att_kb"] = columns(bq[0]), columns(doubled(bk)[0])
    col["sinks"] = np.broadcast_to(i["attn_sinks"][0], (P, 16))
    a["hg_w"] = stack(qh, f, ih, og)
    col["hg_vb"] = columns(bih[0])
    col["hg_qb"], col["hg_fb"], col["hg_ogb"] = columns(bqh[0]), columns(bf[0]), columns(bog[0])
    col["hg_lb"] = columns(i["hgrn_lb_logits"].reshape(-1))
    col["hg_ng"] = columns(i["hgrn_norm_g"][0])
    col["gate_b"] = np.concatenate([columns(bga[0]), columns(bgh[0])], 1)
    gates = [tiles(ga), tiles(gh)]
    outs = [tiles(i["w_proj_attn"][0]), tiles(i["w_proj_hgrn"][0])]
    a["mg1_w"] = np.stack([np.concatenate([g, o], 2) for g, o in zip(gates, outs)], 1)
    a["wo1"] = tiles(i["w_out"][0])

    w = i["w_in_2"][0]
    r2, k2, v2, wlo, alo, glo, gq, gk, gv, gf, go, mqk, mv, mi, mf, mo, sz, sx, sb_, sc, sdt, fg = np.split(w, np.cumsum(
        [512, 512, 512, 64, 64, 128, 256, 256, 512, 16, 512, 512, 512, 4, 4, 512, 512, 512, 256, 256, 8]), 1)
    zero = np.zeros((D, 96), w.dtype)
    small = np.concatenate([mi, mf, sdt, gf, zero], 1)
    a["low_w"] = tiles(np.concatenate([small, wlo, alo, glo, np.zeros((D, P), w.dtype)], 1))
    col["mix2_g"] = columns(i["mix_norm_g_2"][0])
    mu = i["rwkv_mu_2"][0]
    col["r_mu"], col["k_mu"], col["v_mu"], col["lora_mu"] = (columns(m) for m in np.split(mu, [512, 1024, 1536]))
    for n, key in (("w0", "rwkv_w0_2"), ("a0", "rwkv_a0_2"), ("k_k", "rwkv_k_k_2"), ("k_a", "rwkv_k_a_2"),
                   ("r_k", "rwkv_r_k_2"), ("gn_g", "rwkv_gn_g_2"), ("gn_b", "rwkv_gn_b_2")):
        col[n] = columns(i[key][0].reshape(-1))
    a["rw_w"] = stack(r2, k2, v2)
    lows = np.zeros((4, P, 3, P), w.dtype)
    lows[:, 0:64, 0, :] = i["rwkv_w_up_2"][0].reshape(64, 4, P).transpose(1, 0, 2)
    lows[:, 64:128, 1, :] = i["rwkv_a_up_2"][0].reshape(64, 4, P).transpose(1, 0, 2)
    lows[:, :, 2, :] = i["rwkv_g_up_2"][0].reshape(P, 4, P).transpose(1, 0, 2)
    a["rw_up"] = lows
    a["gla_w"] = stack(padded_heads(gq, 4), padded_heads(gk, 4), gv, go)
    fup = np.zeros((4, P, P), w.dtype)
    fup[:, 16:32, 0:64] = i["gla_f_up_2"][0].reshape(16, 4, 64).transpose(1, 0, 2)
    a["gla_fup"] = fup
    col["gla_fb"] = columns(padded_heads(i["gla_f_bias_2"], 4)[0])
    col["gla_ng"] = columns(i["gla_norm_g_2"][0])
    a["ml_w"] = stack(padded_heads(mqk[:, 0:256], 4), padded_heads(mqk[:, 256:512], 4), mv, mo)
    cw = i["mlstm_conv_w_2"][0]
    taps = np.stack([padded_heads(cw[:, 0:256], 4).reshape(4, 4, P), padded_heads(cw[:, 256:], 4).reshape(4, 4, P)], 0)
    col["ml_cw"] = taps.transpose(3, 2, 0, 1).reshape(P, 32)
    cb = i["mlstm_conv_b_2"]
    col["ml_cb"] = np.stack([padded_heads(cb[:, 0:256], 4).reshape(4, P), padded_heads(cb[:, 256:], 4).reshape(4, P)], 1) \
        .reshape(8, P).T
    col["ml_ib"] = np.broadcast_to(i["mlstm_i_bias_2"][0], (P, 4))
    col["ml_fb"] = np.broadcast_to(i["mlstm_f_bias_2"][0], (P, 4))
    col["ml_ng"] = columns(i["mlstm_norm_g_2"][0])
    twice = lambda m: np.repeat(m.reshape(m.shape[0], 2, P), 2, 1).reshape(m.shape[0], 4 * P)
    a["sd_w"] = stack(sx, sz, twice(sb_), twice(sc))
    cw, cb = i["ssd_conv_w_2"][0], i["ssd_conv_b_2"]
    col["sd_cwx"] = cw[:, 0:512].reshape(4, 4, P).transpose(2, 1, 0).reshape(P, 16)
    col["sd_cbx"] = columns(cb[0, 0:512])
    bc = np.stack([twice(cw[:, 512:768]).reshape(4, 4, P), twice(cw[:, 768:]).reshape(4, 4, P)], 0)
    col["sd_cwbc"] = bc.transpose(3, 2, 0, 1).reshape(P, 32)
    bc = np.stack([twice(cb[:, 512:768]).reshape(4, P), twice(cb[:, 768:]).reshape(4, P)], 0)
    col["sd_cbbc"] = bc.transpose(2, 1, 0).reshape(P, 8)
    col["sd_dtb"] = np.broadcast_to(i["ssd_dt_bias_2"][0], (P, 8))
    col["sd_alog"] = np.broadcast_to(i["ssd_a_log_2"][0], (P, 8))
    col["sd_d"] = columns(np.repeat(i["ssd_d_2"][0], 64))
    col["sd_ng"] = columns(i["ssd_norm_g_2"][0])
    proj = i["branch_proj_2"][0]
    a["mg2_w"] = np.stack([np.concatenate([tiles(fg[:, n * D:(n + 1) * D]), tiles(proj[n])], 2) for n in range(4)], 1)
    a["wo2"] = tiles(i["w_out_2"][0])
    up = i["ffn_up_2"][0]
    a["f3_up"], a["f3_down"] = stack(up[:, 0:D_FF], up[:, D_FF:]), tiles(i["ffn_down_2"][0])
    col["ffn2_g"], col["fin2_g"] = columns(i["ffn_norm_g_2"][0]), columns(i["final_norm_g_2"])
    col["ffn2_cw"] = columns(i["ffn_conv_w_2"][0].reshape(-1))
    col["ffn2_cb"] = columns(i["ffn_conv_b_2"][0])

    col["mix3_g"], col["ffn3_g"] = columns(i["mix_norm_g_3"].reshape(-1)), columns(i["ffn_norm_g_3"].reshape(-1))
    col["ffn3_cw"] = columns(i["ffn_conv_w_3"].reshape(-1))
    col["ffn3_cb"] = columns(i["ffn_conv_b_3"].reshape(-1))
    col["fin3_g"] = columns(i["final_norm_g_3"])
    w = i["gm_w_in_3"][0]
    a["gm_u"] = tiles(w[:, 0:2048])
    a["gm_v"] = w[:, 2048:].reshape(2, DT // 2, P, 4, S).transpose(3, 2, 0, 1, 4).reshape(4, P, 2, DT // 2 * S)
    rows = np.concatenate([i["gm_ln_g_3"][0], i["gm_ln_b_3"][0], i["gm_b_s_3"][0].reshape(-1)])
    a["gm_rows"] = np.broadcast_to(rows, (P, rows.size))
    a["gm_ws"] = i["gm_w_s_3"][0].transpose(2, 0, 1)
    a["gm_out"] = tiles(i["gm_w_out_3"][0])
    q, k, v, f = np.split(i["fox_w_qkvf_3"][0], [D, 2 * D, 3 * D], 1)
    a["fox_w"] = stack(q, k, v)
    wide = np.zeros((D, P), f.dtype)
    wide[:, 0:16] = f
    a["fox_f"] = tiles(wide)[0]
    fb = np.zeros((P, 1), f.dtype)
    fb[0:16, 0] = i["fox_b_f_3"][0]
    col["fox_fb"] = fb
    a["fox_o"] = tiles(i["fox_w_o_3"][0])
    for n in range(2):
        a[f"g{n}_up"] = stack(i["ffn_w_gate_3"][n], i["ffn_w_up_3"][n])
        a[f"g{n}_down"] = tiles(i["ffn_w_down_3"][n])
    for n, width in COLUMNS:
        assert col[n].shape == (P, width), (n, col[n].shape)
    a["column"] = np.concatenate([col[n] for n, _ in COLUMNS], 1)
    return {k: np.ascontiguousarray(v) for k, v in a.items()}


def kernel(**inputs):
    import concourse.bacc as _bacc
    from concourse.bass_utils import run_bass_kernel_spmd as _run

    nc = _bacc.Bacc("TRN2", target_bir_lowering=False, num_devices=1)
    arrays = {f"in_{name}": array for name, array in lay_out(inputs).items()}
    args = {name[3:]: nc.dram_tensor(name, array.shape, F32, kind="ExternalInput").ap() for name, array in arrays.items()}
    out = nc.dram_tensor("out", (P, DT, S), F32, kind="ExternalOutput").ap()
    build(nc, args, out)
    r = _run(nc, [arrays], core_ids=[0])
    return np.asarray(r.results[0]["out"]).transpose(2, 1, 0).reshape(1, S, D)
```

```python
from contextlib import ExitStack

import numpy as np

import concourse.bass as bass
from concourse import mybir

F32 = mybir.dt.float32
F32R = mybir.dt.float32r
ACT = mybir.ActivationFunctionType
ALU = mybir.AluOpType
AX_X = mybir.AxisListType.X

P = 128
S = 512
TT = S // P
D = 1024
DT = D // P
D_FF = 2816
FT = D_FF // P
CHUNK = 64
NC = S // CHUNK
ALPHA = 2.0 ** 0.25
DECAY_SCALE = 0.6065306597
LEVELS = 6
NEG = -1e30


def tables():
    s = np.arange(P)[:, None]
    t = np.arange(P)[None, :]
    same = (s // CHUNK) == (t // CHUNK)
    out = {
        "ident": (s == t),
        "ones": np.ones((P, P)),
        "head_ones": (s // 64) == (t // 64),
        "causal_chunk": (s <= t) & same,
        "strict_chunk": (s < t) & same,
        "mask_diag": np.where(t <= s, 0.0, NEG),
        "mask_prev": np.where(t > s, 0.0, NEG),
        "causal": (s <= t),
    }
    rot = np.zeros((P, P))
    for base in (0, 64):
        for j in range(8):
            rot[base + 8 + j, base + j] = -1.0
            rot[base + j, base + 8 + j] = 1.0
    out["rot"] = rot
    for n in range(LEVELS):
        half = 1 << n
        block = (s // (2 * half)) == (t // (2 * half))
        out[f"level{n}"] = block & (s % (2 * half) < half) & (t % (2 * half) >= half)
    out["mask_after"] = np.concatenate([np.where(s <= t, 0.0, NEG), np.zeros((P, S - P))], 1)
    out["restart"] = np.broadcast_to((np.arange(S) % CHUNK != 0), (P, S))
    pos = np.arange(S, dtype=np.float32)
    inv = np.float32(500000.0) ** (-np.arange(0, 16, 2, dtype=np.float32) / np.float32(16))
    ang = (pos[:, None] * inv[None, :]).astype(np.float32)
    c, sn = np.ones((P, S), np.float32), np.zeros((P, S), np.float32)
    for base in (0, 8, 64, 72):
        c[base:base + 8] = np.cos(ang).T
        sn[base:base + 8] = np.sin(ang).T
    out["cos"], out["sin"] = c, sn
    return {k: np.ascontiguousarray(v, dtype=np.float32) for k, v in out.items()}


TABLES = tables()
TABLE_AT, _at = {}, 0
for _name, _v in TABLES.items():
    TABLE_AT[_name] = (_at, _v.shape[1])
    _at += _v.shape[1]
TABLE_WIDTH = _at

COLUMNS = [
    ("ln1_g", 8), ("ln1_b", 8), ("ln2_g", 8), ("ln2_b", 8), ("ln3_g", 8), ("ln3_b", 8),
    ("att_qb", 8), ("att_kb", 4), ("att_vb", 4), ("sinks", 16),
    ("hg_qb", 8), ("hg_fb", 8), ("hg_vb", 8), ("hg_ogb", 8), ("hg_lb", 16), ("hg_ng", 1), ("gate_b", 16),
    ("mix2_g", 8), ("lora_mu", 2), ("r_mu", 4), ("k_mu", 4), ("v_mu", 4), ("w0", 4), ("a0", 4),
    ("k_k", 4), ("k_a", 4), ("r_k", 4), ("gn_g", 4), ("gn_b", 4),
    ("gla_fb", 4), ("gla_ng", 1),
    ("ml_cw", 32), ("ml_cb", 8), ("ml_ib", 4), ("ml_fb", 4), ("ml_ng", 4),
    ("sd_cwx", 16), ("sd_cbx", 4), ("sd_cwbc", 32), ("sd_cbbc", 8), ("sd_dtb", 8), ("sd_alog", 8), ("sd_d", 4),
    ("sd_ng", 4), ("ffn2_g", 8), ("ffn2_cw", 132), ("ffn2_cb", 44), ("fin2_g", 8),
    ("mix3_g", 16), ("gm_g", 16), ("gm_b", 16), ("ffn3_g", 16), ("ffn3_cw", 96), ("ffn3_cb", 32), ("fox_fb", 1), ("fin3_g", 8),
]
COLUMN_AT, _at = {}, 0
for _name, _n in COLUMNS:
    COLUMN_AT[_name] = _at
    _at += _n
COLUMN_WIDTH = _at


class Stage:

    def __init__(self, nc, name):
        self.nc, self.name, self.stack, self.sems = nc, name, ExitStack(), []

    def __enter__(self):
        return self

    def __exit__(self, *e):
        if e[0] is None:
            for sem in self.sems:
                self.nc.gpsimd.sem_clear(sem)
        return self.stack.__exit__(*e)

    def sb(self, name, shape, dtype=F32):
        return self.stack.enter_context(self.nc.sbuf_tensor(f"{self.name}_{name}", shape, dtype))

    def ps(self, name, shape):
        return self.stack.enter_context(self.nc.psum_tensor(f"{self.name}_{name}", shape, F32))

    def sem(self, name):
        self.sems.append(self.stack.enter_context(self.nc.semaphore(f"{self.name}_{name}")))
        return self.sems[-1]


class InOrder:

    def __init__(self, eng, sem):
        self.eng, self.sem, self.base, self.n = eng, sem, 0, 0

    def __call__(self, ins):
        ins.then_inc(self.sem, 1)
        self.n += 1
        self.eng.wait_ge(self.sem, self.base + self.n)

    def free(self, ins):
        ins.then_inc(self.sem, 1)
        self.n += 1


class Steps:

    def __init__(self, sem, names):
        self.sem, self.names = sem, names.split()
        assert len(set(self.names)) == len(self.names)

    def wait(self, eng, name, r=0):
        eng.wait_ge(self.sem, r * len(self.names) + self.names.index(name) + 1)

    def wait_round(self, eng, r):
        eng.wait_ge(self.sem, r * len(self.names))

    def done(self, ins, name):
        assert name in self.names
        ins.then_inc(self.sem, 1)


def rounds(eng, n, body, chain=None):
    start = chain.base + chain.n if chain else 0
    if chain:
        chain.base, chain.n = start, 0
    body(0, True)
    per = chain.n if chain else 0
    if n > 1:
        with eng.Fori(1, n) as r:
            if chain:
                chain.base, chain.n = r * per + start, 0
            body(r, False)
    if chain:
        chain.base, chain.n = start + n * per, 0


def rounds3(eng, n, body, chain=None):
    start = chain.base + chain.n if chain else 0
    if chain:
        chain.base, chain.n = start, 0
    body(0, True, n == 1)
    per = chain.n if chain else 0
    if n > 2:
        with eng.Fori(1, n - 1) as r:
            if chain:
                chain.base, chain.n = r * per + start, 0
            body(r, False, False)
    if n > 1:
        if chain:
            chain.base, chain.n = start + (n - 1) * per, 0
        body(n - 1, False, True)


def tile_cols(k):
    return slice(k * P, (k + 1) * P)


class Ctx:

    def __init__(self, nc, table, column):
        self.nc, self.table, self.column = nc, table, column

    def tab(self, name, part=P):
        at, width = TABLE_AT[name]
        return self.table[0:part, at:at + width]

    def col(self, name, i=0, n=1):
        at = COLUMN_AT[name] + i
        return self.column[:, bass.ds(at, n)]


def load_constants(c, table_d, column_d, x_d, x):
    nc = c.nc
    with Stage(nc, "const") as st:
        landed = st.sem("landed")
        with nc.Block() as block:
            @block.sync
            def _(sp):
                sp.dma_start(c.table[:, :], table_d).then_inc(landed, 16)
                sp.dma_start(c.column[:, :], column_d).then_inc(landed, 16)
                sp.dma_start(x[:, :, :], x_d).then_inc(landed, 16)
                sp.wait_ge(landed, 48)


class Pair:

    def __init__(self, make, name, shape):
        self.hi, self.lo = make(f"{name}_hi", shape, F32R), make(f"{name}_lo", shape, F32R)
        self.value = self.hi.bitcast(F32) if hasattr(self.hi, "bitcast") else self.hi[:].bitcast(F32)


def split(dve, q, source, pair, at, done):
    q(dve.tensor_copy(pair.hi[at], source))
    return dve.tensor_tensor(pair.lo[at], source, pair.value[at], ALU.subtract).then_inc(done, 1)


class Feed:

    def __init__(self, st, cols, per, slots):
        self.per, self.slots = per, slots
        self.raw = st.sb("w_raw", [P, slots, cols])
        self.hi, self.lo = st.sb("w_hi", [P, slots, cols], F32R), st.sb("w_lo", [P, slots, cols], F32R)
        self.hi_value = self.hi[:, :, :].bitcast(F32)
        self.landed = [st.sem(f"w_landed{j}") for j in range(slots)]
        self.rounded, self.parted, self.used = st.sem("w_rounded"), st.sem("w_parted"), st.sem("w_used")

    def at(self, r, m):
        return r * self.per + m, m % self.slots

    def load(self, sp, r, m, first, source):
        s, slot = self.at(r, m)
        if not first or m >= self.slots:
            sp.wait_ge(self.parted, s - self.slots + 1)
        cols = source.shape[-1]
        sp.dma_start(self.raw[:, slot, 0:cols], source).then_inc(self.landed[slot], 16)

    def round(self, act, r, m, first, cols):
        s, slot = self.at(r, m)
        act.wait_ge(self.landed[slot], (r * (self.per // self.slots) + m // self.slots + 1) * 16)
        if not first or m >= self.slots:
            act.wait_ge(self.used, s - self.slots + 1)
        act.activation(self.hi[:, slot, 0:cols], self.raw[:, slot, 0:cols], ACT.Copy).then_inc(self.rounded, 1)

    def rest(self, dve, r, m, cols):
        s, slot = self.at(r, m)
        dve.wait_ge(self.rounded, s + 1)
        dve.tensor_tensor(self.lo[:, slot, 0:cols], self.raw[:, slot, 0:cols], self.hi_value[:, slot, 0:cols],
                          ALU.subtract).then_inc(self.parted, 1)

    def products(self, pe, r, m, out, x, k0, kt, start=True, stop=True, some=None):
        s, slot = self.at(r, m)
        some = range(kt) if some is None else some
        if some[0] == 0:
            pe.wait_ge(self.parted, s + 1)
        for k in some:
            for n, (w, v) in enumerate(((self.hi, x.hi), (self.hi, x.lo), (self.lo, x.hi))):
                last = pe.matmul(out, w[:, slot, tile_cols(k)], v[:, k0 + k, :], start=start and k == 0 and n == 0,
                                 stop=stop and k == kt - 1 and n == 2)
        if some[-1] == kt - 1:
            last.then_inc(self.used, 1)


def norm(c, name, x, out, kt, centre, eps, g, b=None, pair=None, sink_d=None):
    nc = c.nc
    width = kt * P
    with Stage(nc, name) as st:
        mean_p, var_p = st.ps("mean", [P, S]), st.ps("var", [P, S])
        deep = 3
        sq, xc = st.sb("sq", [P, 2, S]), st.sb("xc", [P, deep, S])
        res = st.sb("res", [P, deep, S])
        rstd, var, mean = st.sb("rstd", [P, S]), st.sb("var_s", [P, S]), st.sb("mean_s", [P, S])
        centred_x = st.sb("cx", [P, kt, S]) if centre else x
        mean_ready, mean_here, centred, squared, summed, var_ready = (
            st.sem(n) for n in ("mean_ready", "mean_here", "centred", "squared", "summed", "var_ready"))
        rstd_ready, scaled, normed, achain, rounded, parted, stored = (
            st.sem(n) for n in ("rstd_ready", "scaled", "normed", "achain", "rounded", "parted", "stored"))

        def result(k):
            return out[:, k, :] if out is not None else res[:, k % deep, :]

        with nc.Block() as block:
            @block.tensor
            def _(pe):
                if centre:
                    for k in range(kt):
                        last = pe.matmul(mean_p[:, :], c.tab("ones"), x[:, k, :], start=k == 0, stop=k == kt - 1)
                    last.then_inc(mean_ready, 1)
                for k in range(kt):
                    pe.wait_ge(squared, k + 1)
                    pe.matmul(var_p[:, :], c.tab("ones"), sq[:, k % 2, :], start=k == 0,
                              stop=k == kt - 1).then_inc(summed, 1)

            @block.scalar
            def _(act):
                act.preload_act_table_set("natural_log_exp_and_others")
                q = InOrder(act, achain)
                for k in range(kt):
                    if centre:
                        act.wait_ge(centred, k + 1)
                    if k >= 2:
                        act.wait_ge(summed, k - 1)
                    act.activation(sq[:, k % 2, :], centred_x[:, k, :], ACT.Square).then_inc(squared, 1)
                act.wait_ge(var_ready, 1)
                q(act.activation(rstd[:, :], var[:, :], ACT.Ln))
                act.activation(rstd[:, :], rstd[:, :], ACT.Exp, scale=-0.5).then_inc(rstd_ready, 1)
                for k in range(kt + 1):
                    if k < kt:
                        act.wait_ge(scaled, k + 1)
                        if out is None and k >= deep:
                            act.wait_ge(parted, k - deep + 1)
                        act.activation(result(k), xc[:, k % deep, :], ACT.Identity, scale=g(k),
                                       bias=b(k) if b else 0.0).then_inc(normed, 1)
                    if k and pair is not None:
                        act.wait_ge(normed, k)
                        act.activation(pair.hi[:, k - 1, :], result(k - 1), ACT.Copy).then_inc(rounded, 1)

            @block.vector
            def _(dve):
                if centre:
                    dve.wait_ge(mean_ready, 1)
                    dve.tensor_scalar(mean[:, :], mean_p[:, :], 1.0 / width, None, ALU.mult).then_inc(mean_here, 1)
                    dve.wait_ge(mean_here, 1)
                    for k in range(kt):
                        dve.tensor_tensor(centred_x[:, k, :], x[:, k, :], mean[:, :], ALU.subtract).then_inc(centred, 1)
                dve.wait_ge(summed, kt)
                dve.tensor_scalar(var[:, :], var_p[:, :], 1.0 / width, eps, ALU.mult, ALU.add).then_inc(var_ready, 1)
                dve.wait_ge(rstd_ready, 1)
                for k in range(kt + 2):
                    if k < kt:
                        if k >= deep:
                            dve.wait_ge(normed, k - deep + 1)
                        dve.tensor_tensor(xc[:, k % deep, :], centred_x[:, k, :], rstd[:, :], ALU.mult).then_inc(scaled, 1)
                    if k >= 2 and pair is not None:
                        dve.wait_ge(rounded, k - 1)
                        dve.tensor_tensor(pair.lo[:, k - 2, :], result(k - 2), pair.value[:, k - 2, :],
                                          ALU.subtract).then_inc(parted, 1)

            if sink_d is not None:
                @block.sync
                def _(sp):
                    sp.wait_ge(normed, kt)
                    sp.dma_start(sink_d, out[:, :, :]).then_inc(stored, 16)
                    sp.wait_ge(stored, 16)


def split_all(c, name, x, kt, pair):
    nc = c.nc
    with Stage(nc, name) as st:
        chain, parted = st.sem("chain"), st.sem("parted")
        with nc.Block() as block:
            @block.vector
            def _(dve):
                q = InOrder(dve, chain)
                for k in range(kt):
                    split(dve, q, x[:, k, :], pair, (slice(None), k, slice(None)), parted)


class Piece:

    def __init__(self, tile, bank, x, kt, k0=0, start=True, stop=True, source=None):
        self.tile, self.bank, self.x, self.kt, self.k0, self.start, self.stop = tile, bank, x, kt, k0, start, stop
        self.source = source


def linear(c, st, n, pieces, acc, done, act_epilogue, dve_epilogue, chain, slots=2):
    nc = c.nc
    per = len(pieces)
    tiles = pieces[-1].tile + 1
    feed = Feed(st, max(p.kt for p in pieces) * P, per, slots)
    ends = [m + 1 == per or pieces[m + 1].tile != pieces[m].tile for m in range(per)]
    with nc.Block() as block:
        @block.sync
        def _(sp):
            def body(r, first):
                for m, p in enumerate(pieces):
                    feed.load(sp, r, m, first, p.source(r))
            rounds(sp, n, body)

        @block.tensor
        def _(pe):
            def body(r, first):
                for m, p in enumerate(pieces):
                    if (m == 0 or ends[m - 1]) and (not first or p.tile >= 2):
                        pe.wait_ge(done, r * tiles + p.tile - 1)
                    feed.products(pe, r, m, acc[:, p.tile % 2, p.bank, :], p.x, p.k0, p.kt, p.start, p.stop)
            rounds(pe, n, body)

        @block.scalar
        def _(act):
            for m in range(slots):
                feed.round(act, 0, m, True, pieces[m].kt * P)

            def body(r, first, last):
                for m, p in enumerate(pieces):
                    if m + slots < per or not last:
                        feed.round(act, r, m + slots, False, pieces[(m + slots) % per].kt * P)
                    if ends[m]:
                        act.wait_ge(feed.used, r * per + m + 1)
                        act_epilogue(act, r, p.tile, first)
            rounds3(act, n, body)

        @block.vector
        def _(dve):
            for m in range(slots):
                feed.rest(dve, 0, m, pieces[m].kt * P)
            q = InOrder(dve, chain)

            def body(r, first, last):
                for m, p in enumerate(pieces):
                    if m + slots < per or not last:
                        feed.rest(dve, r, m + slots, pieces[(m + slots) % per].kt * P)
                    if ends[m]:
                        dve_epilogue(dve, q, r, p.tile, first)
            rounds3(dve, n, body, q)


def swiglu_up(c, name, w_d, x, hidden, n):
    with Stage(c.nc, name) as st:
        acc = st.ps("acc", [P, 2, 2, S])
        gate, prod = st.sb("gate", [P, 2, S]), st.sb("prod", [P, 2, S])
        gated, chain, done = st.sem("gated"), st.sem("chain"), st.sem("done")

        def act_epilogue(act, r, i, first):
            if not first or i >= 2:
                act.wait_ge(done, 2 * r + i - 1)
            act.activation(gate[:, i, :], acc[:, i, 0, :], ACT.Silu).then_inc(gated, 1)

        def dve_epilogue(dve, q, r, i, first):
            dve.wait_ge(gated, 2 * r + i + 1)
            q(dve.tensor_tensor(prod[:, i, :], gate[:, i, :], acc[:, i, 1, :], ALU.mult))
            split(dve, q, prod[:, i, :], hidden, (slice(None), 2 * r + i, slice(None)), done)

        pieces = [Piece(i, part, x, DT, source=lambda r, i=i, part=part: w_d[2 * r + i, :, part, :])
                  for i in range(2) for part in range(2)]
        linear(c, st, n // 2, pieces, acc, done, act_epilogue, dve_epilogue, chain)


def project(c, name, w_d, src, kt, n, out=None, residual=None, res_scale=1.0, scale=1.0, func=ACT.Copy, pair=None):
    with Stage(c.nc, name) as st:
        acc, tmp = st.ps("acc", [P, 2, 1, S]), st.sb("tmp", [P, 2, S])
        scaled, chain, done = st.sem("scaled"), st.sem("chain"), st.sem("done")
        cuts = 1 if kt <= 11 else 2
        kc = kt // cuts

        def act_epilogue(act, r, i, first):
            if not first or i >= 2:
                act.wait_ge(done, 2 * r + i - 1)
            act.activation(tmp[:, i, :], acc[:, i, 0, :], func, scale=scale).then_inc(scaled, 1)

        def dve_epilogue(dve, q, r, i, first):
            dve.wait_ge(scaled, 2 * r + i + 1)
            if residual is not None:
                dve.scalar_tensor_tensor(out[:, 2 * r + i, :], residual[:, 2 * r + i, :], res_scale,
                                         tmp[:, i, :], ALU.mult, ALU.add).then_inc(done, 1)
            elif pair is not None:
                split(dve, q, tmp[:, i, :], pair, (slice(None), 2 * r + i, slice(None)), done)
            else:
                dve.tensor_copy(out[:, 2 * r + i, :], tmp[:, i, :]).then_inc(done, 1)

        pieces = [Piece(i, 0, src, kc, k0=h * kc, start=h == 0, stop=h == cuts - 1,
                        source=lambda r, i=i, h=h: w_d[2 * r + i, :, h * kc * P:(h + 1) * kc * P])
                  for i in range(2) for h in range(cuts)]
        linear(c, st, n // 2, pieces, acc, done, act_epilogue, dve_epilogue, chain)


def conv_glu_up(c, name, w_d, x, hidden, n, gate_w, gate_b, val_w=None, val_b=None):
    sides = 2 if val_w is not None else 1
    with Stage(c.nc, name) as st:
        acc = st.ps("acc", [P, 2, 2, S])
        pad = st.sb("pad", [P, 2, 2, S + 2])
        conv = st.sb("conv", [P, 2, S])
        gate, prod = st.sb("gate", [P, 2, S]), st.sb("prod", [P, 2, S])
        zeroed, padded, chain, convolved, gated, done = (
            st.sem(n) for n in ("zeroed", "padded", "chain", "convolved", "gated", "done"))
        with c.nc.Block() as block:
            @block.vector
            def _(dve):
                dve.memset(pad[:, :, :, 0:2], 0.0).then_inc(zeroed, 1)

        def act_epilogue(act, r, i, first):
            if not first or i >= 2:
                act.wait_ge(done, 2 * r + i - 1)
            for side in range(sides):
                act.activation(pad[:, i, side, 2:], acc[:, i, side, :], ACT.Copy).then_inc(padded, 1)
            act.wait_ge(convolved, 2 * r + i + 1)
            act.activation(gate[:, i, :], gate[:, i, :], ACT.Silu).then_inc(gated, 1)

        def dve_epilogue(dve, q, r, i, first):
            t = 2 * r + i
            for side in range(sides):
                cw, cb = (gate_w, gate_b) if side == 0 else (val_w, val_b)
                dve.wait_ge(padded, sides * t + side + 1)
                a = gate[:, i, :] if side == 0 else conv[:, i, :]
                q(dve.tensor_scalar(a, pad[:, i, side, 0:S], cw(0, t), cb(t), ALU.mult, ALU.add))
                q(dve.scalar_tensor_tensor(a, pad[:, i, side, 1:S + 1], cw(1, t), a, ALU.mult, ALU.add))
                last = dve.scalar_tensor_tensor(a, pad[:, i, side, 2:S + 2], cw(2, t), a, ALU.mult, ALU.add)
                if side:
                    q(last)
                else:
                    last.then_inc(convolved, 1)
            dve.wait_ge(gated, t + 1)
            value = conv[:, i, :] if sides == 2 else acc[:, i, 1, :]
            q(dve.tensor_tensor(prod[:, i, :], gate[:, i, :], value, ALU.mult))
            split(dve, q, prod[:, i, :], hidden, (slice(None), t, slice(None)), done)

        pieces = [Piece(i, part, x, DT, source=lambda r, i=i, part=part: w_d[2 * r + i, :, part, :])
                  for i in range(2) for part in range(2)]
        linear(c, st, n // 2, pieces, acc, done, act_epilogue, dve_epilogue, chain)


def merge(c, name, x, w_d, branches, kt, so_far=None, out=None, pair=None, gate_b=None):
    with Stage(c.nc, name) as st:
        acc = st.ps("acc", [P, 2, 2, S])
        gate, part = st.sb("gate", [P, 2, S]), st.sb("part", [P, 2, S])
        gated, chain, done = st.sem("gated"), st.sem("chain"), st.sem("done")

        def act_epilogue(act, m, b, first):
            if not first or b >= 2:
                act.wait_ge(done, 2 * m + b - 1)
            act.activation(gate[:, b, :], acc[:, b, 0, :], ACT.Sigmoid,
                           bias=gate_b(b, m) if gate_b else 0.0).then_inc(gated, 1)

        def dve_epilogue(dve, q, m, b, first):
            dve.wait_ge(gated, 2 * m + b + 1)
            if b == 0:
                if not first:
                    dve.wait_ge(done, 2 * m)
                dve.tensor_tensor(part[:, 0, :], gate[:, 0, :], acc[:, 0, 1, :], ALU.mult).then_inc(done, 1)
                return
            q(dve.tensor_tensor(part[:, 1, :], gate[:, 1, :], acc[:, 1, 1, :], ALU.mult))
            dve.wait_ge(done, 2 * m + 1)
            if so_far is not None:
                q(dve.tensor_tensor(part[:, 1, :], part[:, 1, :], so_far[:, m, :], ALU.add))
            if pair is None:
                dve.tensor_tensor(out[:, m, :], part[:, 0, :], part[:, 1, :], ALU.add).then_inc(done, 1)
            else:
                q(dve.tensor_tensor(part[:, 1, :], part[:, 0, :], part[:, 1, :], ALU.add))
                split(dve, q, part[:, 1, :], pair, (slice(None), m, slice(None)), done)

        pieces = []
        for b in range(2):
            pieces += [Piece(b, 0, x, DT, source=lambda m, b=b: w_d[m, b, :, 0:D]),
                       Piece(b, 1, branches[b], kt, source=lambda m, b=b: w_d[m, b, :, D:D + kt * P])]
        linear(c, st, DT, pieces, acc, done, act_epilogue, dve_epilogue, chain)


class Ahead:

    def __init__(self, st, c, x, w_d, n, inbox, banks, slots, bias=None):
        self.c, self.x, self.w_d, self.n = c, x, w_d, n
        self.inbox, self.banks, self.bias = inbox, banks, bias or {}
        self.per = len(inbox)
        self.slots = slots
        self.feed = Feed(st, D, self.per, slots)
        self.moved = st.sem("moved")

    def sync(self, sp, r, first):
        for m in range(self.per):
            self.feed.load(sp, r, m, first, self.w_d[r, :, m, :])

    def sync_end(self, sp):
        for m in range(self.slots):
            self.feed.load(sp, self.n, m, False, self.w_d[0, :, m, :])

    def tensor(self, pe, r, m, first=False, some=None):
        if (some is None or some[0] == 0) and (not first or m >= len(self.banks)):
            pe.wait_ge(self.moved, r * self.per + m - len(self.banks) + 1)
        self.feed.products(pe, r, m, self.banks[m % len(self.banks)], self.x, 0, DT, some=some)

    def tensor_share(self, pe, r, share, shares):
        n = self.per * DT // shares
        for m in range(self.per):
            some = [k for k in range(DT) if share * n <= m * DT + k < (share + 1) * n]
            if some:
                self.tensor(pe, r, m, some=some)

    def move(self, act, r, m):
        act.wait_ge(self.feed.used, r * self.per + m + 1)
        bank = self.banks[m % len(self.banks)]
        if m in self.bias:
            act.activation(self.inbox[m], bank, ACT.Identity, bias=self.bias[m](r)).then_inc(self.moved, 1)
        else:
            act.activation(self.inbox[m], bank, ACT.Copy).then_inc(self.moved, 1)

    def round_next(self, act, r, m):
        self.feed.round(act, r, m + self.slots, False, D)

    def scalar(self, act, r, m):
        self.move(act, r, m)
        self.round_next(act, r, m)

    def vector(self, dve, r, m):
        self.feed.rest(dve, r, m + self.slots, D)

    def tensor_start(self, pe):
        for m in range(self.per):
            self.tensor(pe, 0, m, True)

    def scalar_start(self, act):
        for m in range(self.slots):
            self.feed.round(act, 0, m, True, D)
        for m in range(self.per):
            self.scalar(act, 0, m)

    def vector_start(self, dve):
        for m in range(self.slots):
            self.feed.rest(dve, 0, m, D)
        for m in range(self.per):
            self.vector(dve, 0, m)

    def landed(self, eng, r, m=None):
        eng.wait_ge(self.moved, (r + 1) * self.per if m is None else r * self.per + m + 1)


def attention(c, name, x, w_d, y, spans, group, qb=None, kb=None, vb=None, sinks=None, forget=None, rope=False):
    nc = c.nc
    scale = 0.125
    pairs, units = DT // group, 8 * group
    keys = 1 if forget is None else 2
    with Stage(nc, name) as st:
        box = st.sb("box", [P, group + 2, S])
        qz, vz = st.sb("qz", [P, 2 * group, S]), st.sb("vz", [P, 2, TT, P])
        kk = st.sb("kk", [P, keys, S])
        rq, pick = st.sb("rq", [P, S]), st.sb("pick", [P, 2, P])
        out = st.sb("out", [P, S])
        prob, probT = st.sb("prob", [P, 2, S]), st.sb("probT", [P, 4, S])
        sink = st.sb("sink", [P, 2 * group])
        top, nmax, rsum, esink, rinv = (st.sb(n, [P, units]) for n in ("top", "nmax", "rsum", "esink", "rinv"))
        sc, tr, o, pj = st.ps("sc", [P, 3, S]), st.ps("tr", [P, 2, S]), st.ps("o", [P, S]), st.ps("pj", [P, 2, S])
        vturned, zeroed, parted, outed, turned, q_ready, k_ready, v_ready = (
            st.sem(n) for n in ("vturned", "zeroed", "parted", "outed", "turned", "q_ready", "k_ready", "v_ready"))
        scored, maxed, exped, normed, transposed, copied, weighed, stored, chain, achain, rows_made, rows_here, picked = (
            st.sem(n) for n in ("scored", "maxed", "exped", "normed", "transposed", "copied", "weighed", "stored",
                                "chain", "achain", "rows_made", "rows_here", "picked"))
        bias = {m: (lambda r, m=m: qb(r * group + m)) for m in range(group)} | {group: kb, group + 1: vb} if qb else {}
        ahead = Ahead(st, c, x, w_d, pairs, [box[:, m, :] for m in range(group + 2)], [pj[:, m, :] for m in range(2)],
                      3 if group == 1 else 2, bias)
        fetch = {3: 0, 6: 1, 7: 2} if group == 1 else {3: 0, 7: 1, 11: 2, 15: 3}
        halves = [slice(64 * h, 64 * h + 64) for h in range(2)]

        def unit(u):
            return u // 8, u % 8 // 2, u % 2

        with nc.Block() as block:
            @block.sync
            def _(sp):
                rounds(sp, pairs, lambda r, first: ahead.sync(sp, r, first))
                ahead.sync_end(sp)

            @block.tensor
            def _(pe):
                ahead.tensor_start(pe)

                def body(p, first, last_round):
                    if rope:
                        ahead.landed(pe, p, group)
                        if not first:
                            pe.wait_ge(exped, units * p)
                        for m in range(group + 1):
                            pe.matmul(sc[:, 2 - m, :], c.tab("rot"), box[:, m, :], start=True, stop=True).then_inc(turned, 1)
                    if forget is not None:
                        pe.wait_ge(picked, 2 * (p + 1))
                        if not first:
                            pe.wait_ge(exped, units * p)
                        for h in range(2):
                            pe.matmul(sc[:, 1 + h, :], pick[:, h, :], forget[:, :], start=True, stop=True).then_inc(rows_made, 1)
                    ahead.landed(pe, p)
                    if not first:
                        pe.wait_ge(copied, units * p)
                    for t in range(TT):
                        last = pe.transpose(tr[:, 1, tile_cols(t)], box[:, group + 1, tile_cols(t)], c.tab("ident"))
                    last.then_inc(vturned, 1)
                    if not last_round:
                        for share in range(2):
                            ahead.tensor_share(pe, p + 1, share, units)
                    pe.wait_ge(q_ready, 2 * group * (p + 1))
                    pe.wait_ge(k_ready, keys * (p + 1))
                    if forget is not None:
                        pe.wait_ge(rows_here, 2 * (p + 1))

                    def scores(u):
                        g, i, h = unit(u)
                        if u >= 3:
                            pe.wait_ge(exped, units * p + u - 2)
                        elif not first:
                            pe.wait_ge(exped, units * p)
                        k0, n = spans[i][0] * P, len(spans[i]) * P
                        pe.matmul(sc[:, u % 3, 0:n], qz[:, 2 * g + h, tile_cols(i)], kk[:, h % keys, k0:k0 + n], start=True, stop=False)
                        if rope and i:
                            pe.matmul(sc[:, u % 3, 0:P], c.tab("ident"), c.tab("mask_prev"), start=False, stop=False)
                        pe.matmul(sc[:, u % 3, n - P:n], c.tab("ident"), c.tab("mask_diag"), start=False,
                                  stop=True).then_inc(scored, 1)

                    for u in range(3):
                        scores(u)
                    pe.wait_ge(v_ready, 2 * (p + 1))
                    for u in range(units):
                        g, i, h = unit(u)
                        if not last_round and u + 2 < units:
                            ahead.tensor_share(pe, p + 1, u + 2, units)
                        pe.wait_ge(normed, units * p + u + 1)
                        if not first or u >= 2:
                            pe.wait_ge(copied, units * p + u - 1)
                        for b in range(len(spans[i])):
                            last = pe.transpose(tr[:, u % 2, tile_cols(b)], prob[:, u % 2, tile_cols(b)], c.tab("ident"))
                        last.then_inc(transposed, 1)
                        if u + 3 < units:
                            scores(u + 3)
                        if h:
                            pe.wait_ge(copied, units * p + u + 1)
                            if i == 0 and not (first and g == 0):
                                pe.wait_ge(stored, group * p + g)
                            n = len(spans[i])
                            for b2 in range(2):
                                for b in range(n):
                                    last = pe.matmul(o[:, tile_cols(i)], vz[:, b2, spans[i][b], :],
                                                     probT[:, (u - 1 + b2) % 4, tile_cols(b)],
                                                     start=b2 == 0 and b == 0, stop=b2 == 1 and b == n - 1)
                            last.then_inc(weighed, 1)
                rounds3(pe, pairs, body)

            @block.scalar
            def _(act):
                act.wait_ge(zeroed, 3 if forget is None else 5)
                act.preload_act_table_set("exp_and_others")
                q = InOrder(act, achain)
                ahead.scalar_start(act)

                def body(p, first, last_round):
                    if not first:
                        act.wait_ge(scored, units * p)
                        act.wait_ge(weighed, units // 2 * p)
                    if not rope:
                        ahead.landed(act, p)
                        for m in range(2 * group):
                            act.activation(qz[halves[m % 2], m, :], box[halves[m % 2], m // 2, :], ACT.Copy).then_inc(q_ready, 1)
                        for h in range(keys):
                            act.activation(kk[halves[h], h, :], box[halves[h], group, :], ACT.Copy).then_inc(k_ready, 1)
                    if forget is not None:
                        for h in range(2):
                            row = slice(64 - 64 * h, 65 - 64 * h)
                            act.wait_ge(rows_made, 2 * p + h + 1)
                            act.activation(kk[row, h, :], sc[row, 1 + h, :], ACT.Copy).then_inc(rows_here, 1)
                    act.wait_ge(vturned, p + 1)
                    for h in range(2):
                        act.activation(vz[:, h, :, halves[h]], tr[:, 1, :].rearrange("p (t f) -> p t f", t=TT)[:, :, halves[h]],
                                       ACT.Copy).then_inc(v_ready, 1)
                    if not first:
                        ahead.round_next(act, p, group + 1)

                    if sinks is not None:
                        q(act.activation(sink[:, :], sinks(2 * group * p, 2 * group), ACT.Copy))

                    def exps(u):
                        g, i, h = unit(u)
                        n = len(spans[i]) * P
                        act.wait_ge(maxed, units * p + u + 1)
                        if sinks is not None:
                            q(act.activation(esink[:, u:u + 1], sink[:, 2 * g + h:2 * g + h + 1], ACT.Exp, bias=nmax[:, u:u + 1]))
                        if not first or u >= 2:
                            act.wait_ge(transposed, units * p + u - 1)
                        act.activation(prob[:, u % 2, 0:n], sc[:, u % 3, 0:n], ACT.Exp, scale=scale,
                                       bias=nmax[:, u:u + 1], accum_out=rsum[:, u:u + 1]).then_inc(exped, 1)

                    def copies(u):
                        n = len(spans[unit(u)[1]]) * P
                        act.wait_ge(transposed, units * p + u + 1)
                        if not first or u >= 4:
                            act.wait_ge(weighed, units // 2 * p + u // 2 - 1)
                        act.activation(probT[:, u % 4, 0:n], tr[:, u % 2, 0:n], ACT.Copy).then_inc(copied, 1)

                    def store(g):
                        act.wait_ge(weighed, units // 2 * p + 4 * (g + 1))
                        if not first or g:
                            act.wait_ge(parted, group * p + g)
                        act.activation(out[:, :], o[:, :], ACT.Copy).then_inc(stored, 1)

                    exps(0)
                    exps(1)
                    for u in range(units):
                        if u in fetch and not last_round:
                            if fetch[u] == 0:
                                act.wait_ge(q_ready, 2 * group * (p + 1))
                                act.wait_ge(k_ready, keys * (p + 1))
                            ahead.move(act, p + 1, fetch[u])
                            if fetch[u] < group + 1:
                                ahead.round_next(act, p + 1, fetch[u])
                        copies(u)
                        if u % 8 == 0 and u:
                            store(u // 8 - 1)
                        if u + 2 < units:
                            exps(u + 2)
                    store(group - 1)
                rounds3(act, pairs, body, q)

            @block.vector
            def _(dve):
                dve.memset(qz[:, :, :], 0.0).then_inc(zeroed, 1)
                dve.memset(vz[:, :, :, :], 0.0).then_inc(zeroed, 1)
                dve.memset(kk[:, :, :], 0.0).then_inc(zeroed, 1)
                dve.wait_ge(zeroed, 3)
                if forget is not None:
                    for h in range(2):
                        dve.memset(qz[64 - 64 * h:65 - 64 * h, h, :], 1.0).then_inc(zeroed, 1)
                    dve.wait_ge(zeroed, 5)
                q = InOrder(dve, chain)
                ahead.vector_start(dve)

                def store(pair):
                    dve.wait_ge(stored, pair + 1)
                    dve.tensor_copy(y.hi[:, pair, :], out[:, :]).then_inc(outed, 1)
                    dve.wait_ge(outed, pair + 1)
                    dve.tensor_tensor(y.lo[:, pair, :], out[:, :], y.value[:, pair, :], ALU.subtract).then_inc(parted, 1)

                def picks(p, first=False):
                    if not first:
                        dve.wait_ge(rows_made, 2 * p)
                    for h in range(2):
                        pick_row(dve, c, pick[:, h, :], 2 * p + h).then_inc(picked, 1)

                if forget is not None:
                    picks(0, True)

                def body(p, first, last_round):
                    if rope:
                        if not first:
                            dve.wait_ge(scored, units * p)
                        for m in range(group + 1):
                            dve.wait_ge(turned, (group + 1) * p + m + 1)
                            q(dve.tensor_tensor(rq[:, :], sc[:, 2 - m, :], c.tab("sin"), ALU.mult))
                            q(dve.tensor_tensor(box[:, m, :], box[:, m, :], c.tab("cos"), ALU.mult))
                            if m < group:
                                for half, n in zip(halves, (2 * m, 2 * m + 1)):
                                    last = dve.tensor_tensor(qz[half, n, :], box[half, m, :], rq[half, :], ALU.add)
                                    last.then_inc(q_ready, 1)
                                dve.wait_ge(q_ready, 2 * group * p + 2 * m + 2)
                            else:
                                dve.tensor_tensor(kk[:, 0, :], box[:, m, :], rq[:, :], ALU.add).then_inc(k_ready, 1)

                    def maxima(u):
                        g, i, h = unit(u)
                        n = len(spans[i]) * P
                        dve.wait_ge(scored, units * p + u + 1)
                        q(dve.tensor_reduce(top[:, u:u + 1], sc[:, u % 3, 0:n], AX_X, ALU.max))
                        if sinks is None:
                            dve.tensor_scalar(nmax[:, u:u + 1], top[:, u:u + 1], -scale, None, ALU.mult).then_inc(maxed, 1)
                        else:
                            q(dve.tensor_scalar(top[:, u:u + 1], top[:, u:u + 1], scale,
                                                sinks(2 * group * p + 2 * g + h), ALU.mult, ALU.max))
                            dve.tensor_scalar(nmax[:, u:u + 1], top[:, u:u + 1], -1.0, None, ALU.mult).then_inc(maxed, 1)

                    def normalise(u):
                        n = len(spans[unit(u)[1]]) * P
                        dve.wait_ge(exped, units * p + u + 1)
                        if sinks is not None:
                            q(dve.tensor_tensor(rsum[:, u:u + 1], rsum[:, u:u + 1], esink[:, u:u + 1], ALU.add))
                        q(dve.reciprocal(rinv[:, u:u + 1], rsum[:, u:u + 1]))
                        dve.tensor_scalar(prob[:, u % 2, 0:n], prob[:, u % 2, 0:n], rinv[:, u:u + 1], None,
                                          ALU.mult).then_inc(normed, 1)

                    maxima(0)
                    maxima(1)
                    if not first:
                        ahead.vector(dve, p, group + 1)
                    for u in range(units):
                        if u in fetch and fetch[u] < group + 1 and not last_round:
                            ahead.vector(dve, p + 1, fetch[u])
                        if u == 4 and forget is not None and not last_round:
                            picks(p + 1)
                        if u == 1 and not first:
                            store(group * p - 1)
                        if u % 8 == 2 and u > 8:
                            store(group * p + u // 8 - 1)
                        normalise(u)
                        if u + 2 < units:
                            maxima(u + 2)
                    if last_round:
                        store(group * p + group - 1)
                rounds3(dve, pairs, body, q)


def pick_row(dve, c, out, row):
    return dve.tensor_scalar(out, c.tab("ones"), c.table[:, bass.ds(row + TABLE_AT["ident"][0], 1)], None, ALU.mult)


def forget_rows(c, name, x, w_d, out, bias):
    nc = c.nc
    with Stage(nc, name) as st:
        feed = Feed(st, D, 1, 1)
        row, neg = st.sb("row", [P, S]), st.sb("neg", [P, S])
        acc = st.ps("acc", [P, S])
        achain, chain = st.sem("achain"), st.sem("chain")
        steps = Steps(st.sem("steps"), "biased least soft done")
        with nc.Block() as block:
            @block.sync
            def _(sp):
                feed.load(sp, 0, 0, True, w_d)

            @block.tensor
            def _(pe):
                feed.products(pe, 0, 0, acc[:, :], x, 0, DT)

            @block.scalar
            def _(act):
                q = InOrder(act, achain)
                feed.round(act, 0, 0, True, D)
                act.wait_ge(feed.used, 1)
                steps.done(act.activation(row[:, :], acc[:, :], ACT.Identity, bias=bias), "biased")
                steps.wait(act, "least")
                q(act.activation(row[:, :], row[:, :], ACT.Abs))
                q(act.activation(row[:, :], row[:, :], ACT.Exp, scale=-1.0))
                steps.done(act.activation(row[:, :], row[:, :], ACT.Ln, bias=1.0), "soft")

            @block.vector
            def _(dve):
                q = InOrder(dve, chain)
                feed.rest(dve, 0, 0, D)
                steps.wait(dve, "biased")
                steps.done(dve.tensor_scalar(neg[:, :], row[:, :], 0.0, None, ALU.min), "least")
                steps.wait(dve, "soft")
                q(dve.tensor_tensor(neg[:, :], neg[:, :], row[:, :], ALU.subtract))
                q(dve.tensor_scalar(neg[:, :], neg[:, :], -8.0, None, ALU.mult))
                q(dve.memset(row[:, :], 1.0))
                q(dve.memset(out[:, :], 0.0))
                steps.done(dve.tensor_tensor_scan(out[0:16, :], row[0:16, :], neg[0:16, :], 0.0, ALU.mult, ALU.add), "done")


def log_sigmoid_act(act, q, u, v):
    q(act.activation(u, v, ACT.Abs))
    q(act.activation(u, u, ACT.Exp, scale=-1.0))
    return act.activation(u, u, ACT.Ln, bias=1.0)


def linear_recurrence(c, name, x, w_d, heads, y, kind, norm_g, qb=None, fb=None, vb=None, ogb=None, lb=None,
                      small=None, fup_d=None):
    nc = c.nc
    gla = kind == "gla"
    with Stage(nc, name) as st:
        lower = st.sem("lower")
        box = st.sb("box", [P, 5, S])
        fup = st.sb("fup", [P, P])
        q_, f_, og, g, u, qd, kinv, kend, eg = (st.sb(n, [P, S]) for n in ("q", "f", "og", "g", "u", "qd", "kinv", "kend", "eg"))
        v = st.sb("v", [P, TT, P])
        a = st.sb("a", [P, TT, P])
        kt = st.sb("kt", [P, 2, TT, P])
        state = st.sb("state", [P, NC, P])
        lbc, olb = st.sb("lbc", [P, 8]), st.sb("olb", [P, 8])
        b = [st.ps(f"b{i}", [P, S]) for i in range(8)]
        zeroed, achain, chain, masked = st.sem("zeroed"), st.sem("achain"), st.sem("chain"), st.sem("masked")
        fup_landed, fup_used = st.sem("fup_landed"), st.sem("fup_used")
        steps = Steps(st.sem("steps"),
                      "activated gated logged summed decays folded scored kcopied updated "
                      "states mixed squared meaned rooted stored")
        bias = {} if gla else {0: qb, 1: fb, 2: vb, 3: ogb}
        ahead = Ahead(st, c, x, w_d, heads, [box[:, m, :] for m in range(4)], [b[6][:, :], b[7][:, :]], 2, bias)

        def low_rank(pe, r, first=False):
            if gla:
                pe.wait_ge(fup_landed, 16 * (r + 1))
                if not first:
                    steps.wait(pe, "kcopied", r - 1)
                pe.matmul(b[5][:, :], fup[:, :], small[:, :], start=True, stop=True).then_inc(fup_used, 1)

        with nc.Block() as block:
            @block.sync
            def _(sp):
                def body(h, first):
                    if gla:
                        if not first:
                            sp.wait_ge(fup_used, h)
                        sp.dma_start(fup[:, :], fup_d[h]).then_inc(fup_landed, 16)
                    ahead.sync(sp, h, first)
                rounds(sp, heads, body)
                ahead.sync_end(sp)

            @block.tensor
            def _(pe):
                ahead.tensor_start(pe)
                low_rank(pe, 0, True)

                def share(h, last_round, *which):
                    if not last_round:
                        for n in which:
                            ahead.tensor_share(pe, h + 1, n, 8)

                def body(h, first, last_round):
                    share(h, last_round, 0, 1, 2)
                    steps.wait(pe, "folded", h)
                    for t in range(TT):
                        pe.matmul(b[3][:, tile_cols(t)], kinv[:, tile_cols(t)], qd[:, tile_cols(t)], start=True, stop=True)
                    for t in range(TT):
                        pe.transpose(b[5][:, tile_cols(t)], box[:, 2, tile_cols(t)], c.tab("ident"))
                    for t in range(TT):
                        last = pe.transpose(b[4][:, tile_cols(t)], kend[:, tile_cols(t)], c.tab("ident"))
                    steps.done(last, "scored")
                    share(h, last_round, 3)
                    steps.wait(pe, "kcopied", h)
                    for n in range(NC - 1):
                        last = pe.matmul(b[n // 4][:, tile_cols(n % 4)], kt[:, n % 2, n // 2, :], v[:, n // 2, :],
                                         start=True, stop=True)
                    steps.done(last, "updated")
                    pe.wait_ge(masked, h + 1)
                    for t in range(TT):
                        pe.matmul(b[2][:, tile_cols(t)], v[:, t, :], a[:, t, :], start=t == 0, stop=False, skip_group_check=True)
                    share(h, last_round, 4)
                    steps.wait(pe, "states", h)
                    for n in range(1, NC):
                        cols = slice(n * CHUNK, (n + 1) * CHUNK)
                        last = pe.matmul(b[2][:, cols], state[:, n, :], qd[:, cols], start=False, stop=n == NC - 1,
                                         skip_group_check=True)
                    steps.done(last, "mixed")
                    share(h, last_round, 5, 6)
                    steps.wait(pe, "squared", h)
                    steps.done(pe.matmul(b[3][:, :], c.tab("ones"), u[:, :], start=True, stop=True), "meaned")
                    share(h, last_round, 7)
                    if not last_round:
                        low_rank(pe, h + 1)
                rounds3(pe, heads, body)

            @block.scalar
            def _(act):
                act.wait_ge(zeroed, 1)
                q = InOrder(act, achain)
                if not gla:
                    act.wait_ge(lower, 1)
                    act.activation(lbc[:, :], olb[:, :], ACT.Sigmoid).then_inc(lower, 1)
                ahead.scalar_start(act)

                def body(h, first, last_round):
                    ahead.landed(act, h)
                    if not first:
                        steps.wait(act, "stored", h - 1)
                    if gla:
                        act.wait_ge(fup_used, h + 1)
                        q(act.activation(box[:, 4, :], b[5][:, :], ACT.Identity, bias=fb(h)))
                    if gla:
                        q.free(act.activation(og[:, :], box[:, 3, :], ACT.Sigmoid))
                        act.preload_act_table_set("natural_log_exp_and_others")
                        steps.done(log_sigmoid_act(act, q, u[:, :], box[:, 4, :]), "activated")
                    else:
                        q(act.activation(og[:, :], box[:, 3, :], ACT.Sigmoid))
                        q(act.activation(q_[:, :], box[:, 0, :], ACT.Sigmoid))
                        steps.done(act.activation(f_[:, :], box[:, 1, :], ACT.Sigmoid), "activated")
                        act.preload_act_table_set("natural_log_exp_and_others")
                    steps.wait(act, "gated", h)
                    steps.done(act.activation(g[:, :], f_[:, :], ACT.Copy if gla else ACT.Ln), "logged")
                    steps.wait(act, "summed", h)
                    r = 1.0 / 16 if gla else 1.0
                    q(act.activation(u[:, :], g[:, :], ACT.Exp, scale=-r))
                    steps.done(act.activation(eg[:, :], g[:, :], ACT.Exp, scale=r), "decays")
                    if not last_round:
                        ahead.scalar(act, h + 1, 0)
                    steps.wait(act, "scored", h)
                    q(act.activation(v[:, :, :], b[5][:, :].rearrange("p (t f) -> p t f", t=TT), ACT.Copy))
                    for half in range(2):
                        rows = slice(64 * half, 64 * half + 64)
                        last = act.activation(kt[rows, half, :, :], b[4][rows, :].rearrange("p (t f) -> p t f", t=TT), ACT.Copy)
                        if half == 0:
                            q(last)
                    steps.done(last, "kcopied")
                    if not last_round:
                        ahead.scalar(act, h + 1, 1)
                    steps.wait(act, "mixed", h)
                    steps.done(act.activation(u[:, :], b[2][:, :], ACT.Square), "squared")
                    if not last_round:
                        ahead.scalar(act, h + 1, 2)
                    steps.wait(act, "meaned", h)
                    q(act.activation(g[:, :], b[3][:, :], ACT.Copy, scale=1.0 / P, bias=1e-6))
                    q(act.activation(g[:, :], g[:, :], ACT.Ln))
                    steps.done(act.activation(g[:, :], g[:, :], ACT.Exp, scale=-0.5), "rooted")
                    if not last_round:
                        ahead.scalar(act, h + 1, 3)
                rounds3(act, heads, body, q)

            @block.vector
            def _(dve):
                dve.memset(kt[:, :, :, :], 0.0).then_inc(zeroed, 1)
                q = InOrder(dve, chain)

                def lbc_at(h):
                    return lbc[:, bass.ds(h, 1)]

                def olb_at(h):
                    return olb[:, bass.ds(h, 1)]

                if not gla:
                    dve.tensor_tensor(olb[:, :], lb[:, 0:8], lb[:, 8:16], ALU.subtract).then_inc(lower, 1)
                    dve.wait_ge(lower, 2)
                    q(dve.tensor_scalar(olb[:, :], lbc[:, :], -1.0, 1.0, ALU.mult, ALU.add))
                ahead.vector_start(dve)

                def body(h, first, last_round):
                    steps.wait(dve, "activated", h)
                    if gla:
                        q(dve.scalar_tensor_tensor(f_[:, :], box[:, 4, :], 0.0, u[:, :], ALU.min, ALU.subtract))
                        q(dve.tensor_scalar(q_[:, :], box[:, 0, :], 0.125, None, ALU.mult))
                        q(dve.tensor_copy(kinv[:, :], box[:, 1, :]))
                        steps.done(dve.tensor_tensor(og[:, :], og[:, :], box[:, 3, :], ALU.mult), "gated")
                    else:
                        q(dve.tensor_scalar(f_[:, :], f_[:, :], olb_at(h), lbc_at(h), ALU.mult, ALU.add))
                        q(dve.tensor_scalar(kinv[:, :], f_[:, :], -1.0, 1.0, ALU.mult, ALU.add))
                        q(dve.tensor_tensor(q_[:, :], q_[:, :], box[:, 0, :], ALU.mult))
                        steps.done(dve.tensor_tensor(og[:, :], og[:, :], box[:, 3, :], ALU.mult), "gated")
                    steps.wait(dve, "logged", h)
                    steps.done(dve.tensor_tensor_scan(g[:, :], c.tab("restart"), g[:, :], 0.0, ALU.mult, ALU.add), "summed")
                    steps.wait(dve, "decays", h)
                    q(dve.tensor_tensor(qd[:, :], q_[:, :], eg[:, :], ALU.mult))
                    q(dve.tensor_tensor(kinv[:, :], kinv[:, :], u[:, :], ALU.mult))
                    chunked = "p (n t) -> p n t"
                    ends = eg[:, :].rearrange(chunked, n=NC)[:, :, CHUNK - 1:CHUNK].broadcast_to([P, NC, CHUNK])
                    steps.done(dve.tensor_tensor(kend[:, :].rearrange(chunked, n=NC), kinv[:, :].rearrange(chunked, n=NC),
                                                 ends, ALU.mult), "folded")
                    if not last_round:
                        ahead.vector(dve, h + 1, 0)
                    steps.wait(dve, "scored", h)
                    mask = c.tab("causal_chunk").rearrange("p (o t) -> p o t", o=1).broadcast_to([P, TT, P])
                    dve.tensor_tensor(a[:, :, :], b[3][:, :].rearrange("p (t f) -> p t f", t=TT), mask, ALU.mult).then_inc(masked, 1)
                    steps.wait(dve, "updated", h)
                    q(dve.tensor_copy(state[:, 1, :], b[0][:, 0:P]))
                    for n in range(1, NC - 1):
                        last = dve.scalar_tensor_tensor(state[:, n + 1, :], state[:, n, :], eg[:, (n + 1) * CHUNK - 1:(n + 1) * CHUNK],
                                                        b[n // 4][:, tile_cols(n % 4)], ALU.mult, ALU.add)
                        if n < NC - 2:
                            q(last)
                    steps.done(last, "states")
                    if not last_round:
                        ahead.vector(dve, h + 1, 1)
                        ahead.vector(dve, h + 1, 2)
                    steps.wait(dve, "rooted", h)
                    q(dve.scalar_tensor_tensor(g[:, :], g[:, :], norm_g, og[:, :], ALU.mult, ALU.mult))
                    q(dve.tensor_tensor(g[:, :], g[:, :], b[2][:, :], ALU.mult))
                    q(dve.tensor_copy(y.hi[:, h, :], g[:, :]))
                    steps.done(dve.tensor_tensor(y.lo[:, h, :], g[:, :], y.value[:, h, :], ALU.subtract), "stored")
                    if not last_round:
                        ahead.vector(dve, h + 1, 3)
                rounds3(dve, heads, body, q)


def causal_conv(dve, q, out, pad, taps, weight, bias, done=None):
    q(dve.tensor_scalar(out, pad[:, 0:S], weight(0), bias, ALU.mult, ALU.add))
    for i in range(1, taps):
        last = dve.scalar_tensor_tensor(out, pad[:, i:i + S], weight(i), out, ALU.mult, ALU.add)
        if done is None or i < taps - 1:
            q(last)
        else:
            last.then_inc(done, 1)


def mlstm(c, name, x, w_d, heads, y, small):
    nc = c.nc
    with Stage(nc, name) as st:
        box = st.sb("box", [P, 2, S])
        pick = st.sb("pick", [P, 2, P])
        pad, qk = st.sb("pad", [P, 2, S + 3]), st.sb("qk", [P, 2, S])
        v, og = st.sb("v", [P, TT, P]), st.sb("og", [P, S])
        li, lf, u, bsum, a, top, em, hh, one = (st.sb(n, [P, S]) for n in ("li", "lf", "u", "bsum", "a", "top", "em", "hh", "one"))
        diag, acol = st.sb("diag", [P, P]), st.sb("acol", [P, TT])
        e = st.sb("e", [P, TT, S])
        b = [st.ps(f"b{i}", [P, S]) for i in range(8)]
        zeroed, achain, chain, convolved, vturned, v_ready = (
            st.sem(n) for n in ("zeroed", "achain", "chain", "convolved", "vturned", "v_ready"))
        steps = Steps(st.sem("steps"), "picked rows taken gates exps scored weighted mixed absden divided "
                                       "squared meaned rooted stored")
        ahead = Ahead(st, c, x, w_d, heads, [pad[:, 0, 3:], pad[:, 1, 3:], box[:, 0, :], box[:, 1, :]],
                      [b[6][:, :], b[7][:, :]], 2)
        with nc.Block() as block:
            @block.sync
            def _(sp):
                rounds(sp, heads, lambda h, first: ahead.sync(sp, h, first))
                ahead.sync_end(sp)

            @block.tensor
            def _(pe):
                ahead.tensor_start(pe)

                def body(h, first, last_round):
                    steps.wait(pe, "picked", h)
                    for n in range(2):
                        last = pe.matmul(b[4 + n][:, :], pick[:, n, :], small[:, :], start=True, stop=True)
                    steps.done(last, "rows")
                    if not last_round:
                        ahead.tensor(pe, h + 1, 0)
                        ahead.tensor(pe, h + 1, 1)
                    steps.wait(pe, "exps", h)
                    for j in range(TT):
                        last = pe.matmul(b[j][:, 0:S - j * P], qk[:, 1, tile_cols(j)], qk[:, 0, j * P:S], start=True, stop=True)
                    steps.done(last, "scored")
                    for t in range(TT):
                        last = pe.transpose(b[4][:, tile_cols(t)], box[:, 0, tile_cols(t)], c.tab("ident"))
                    last.then_inc(vturned, 1)
                    if not last_round:
                        ahead.tensor(pe, h + 1, 2)
                    pe.wait_ge(v_ready, h + 1)
                    steps.wait(pe, "weighted", h)
                    for out, lhs in ((b[4], v), (b[5], None)):
                        for j in range(TT):
                            last = pe.matmul(out[:, j * P:S], c.tab("ones") if lhs is None else lhs[:, j, :],
                                             e[:, j, 0:S - j * P], start=j == 0, stop=j == TT - 1)
                    steps.done(last, "mixed")
                    if not last_round:
                        ahead.tensor(pe, h + 1, 3)
                    steps.wait(pe, "squared", h)
                    steps.done(pe.matmul(b[0][:, :], c.tab("ones"), u[:, :], start=True, stop=True), "meaned")
                rounds3(pe, heads, body)

            @block.scalar
            def _(act):
                act.wait_ge(zeroed, 2)
                q = InOrder(act, achain)
                ahead.scalar_start(act)

                def body(h, first, last_round):
                    ahead.landed(act, h)
                    if not first:
                        steps.wait(act, "stored", h - 1)
                    q.free(act.activation(og[:, :], box[:, 1, :], ACT.Sigmoid))
                    act.preload_act_table_set("natural_log_exp_and_others")
                    steps.wait(act, "rows", h)
                    q(act.activation(li[:, :], b[4][:, :], ACT.Identity, bias=c.col("ml_ib", h)))
                    q(act.activation(lf[:, :], b[5][:, :], ACT.Identity, bias=c.col("ml_fb", h)))
                    steps.done(log_sigmoid_act(act, q, u[:, :], lf[:, :]), "taken")
                    act.wait_ge(convolved, h + 1)
                    for n in range(2):
                        q.free(act.activation(qk[:, n, :], qk[:, n, :], ACT.Silu))
                    if not last_round:
                        ahead.scalar(act, h + 1, 0)
                        ahead.scalar(act, h + 1, 1)
                    act.preload_act_table_set("natural_log_exp_and_others")
                    steps.wait(act, "gates", h)
                    q(act.activation(em[:, :], em[:, :], ACT.Exp, scale=-1.0))
                    for j in range(TT):
                        last = act.activation(e[:, j, 0:S - j * P], e[:, j, 0:S - j * P], ACT.Exp, bias=acol[:, j:j + 1])
                        if j < TT - 1:
                            q(last)
                    steps.done(last, "exps")
                    act.wait_ge(vturned, h + 1)
                    act.activation(v[:, :, :], b[4][:, :].rearrange("p (t f) -> p t f", t=TT), ACT.Copy).then_inc(v_ready, 1)
                    if not last_round:
                        ahead.scalar(act, h + 1, 2)
                    steps.wait(act, "mixed", h)
                    steps.done(act.activation(u[:, :], b[5][:, :], ACT.Abs), "absden")
                    if not last_round:
                        ahead.scalar(act, h + 1, 3)
                    steps.wait(act, "divided", h)
                    steps.done(act.activation(u[:, :], hh[:, :], ACT.Square), "squared")
                    steps.wait(act, "meaned", h)
                    q(act.activation(u[:, :], b[0][:, :], ACT.Copy, scale=1.0 / P, bias=1e-6))
                    q(act.activation(u[:, :], u[:, :], ACT.Ln))
                    steps.done(act.activation(u[:, :], u[:, :], ACT.Exp, scale=-0.5), "rooted")
                rounds3(act, heads, body, q)

            @block.vector
            def _(dve):
                dve.memset(pad[:, :, 0:3], 0.0).then_inc(zeroed, 1)
                dve.memset(one[:, :], 1.0).then_inc(zeroed, 1)
                dve.wait_ge(zeroed, 2)
                q = InOrder(dve, chain)
                ahead.vector_start(dve)

                def body(h, first, last_round):
                    if not first:
                        steps.wait_round(dve, h)
                    q(pick_row(dve, c, pick[:, 0, :], h))
                    steps.done(pick_row(dve, c, pick[:, 1, :], h + 4), "picked")
                    ahead.landed(dve, h)
                    for n in range(2):
                        causal_conv(dve, q, qk[:, n, :], pad[:, n, :], 4, lambda i: c.col("ml_cw", h * 8 + n * 4 + i),
                                    c.col("ml_cb", h * 2 + n), convolved if n else None)
                    steps.wait(dve, "taken", h)
                    q(dve.tensor_scalar(lf[:, :], lf[:, :], 0.0, None, ALU.min))
                    q(dve.tensor_tensor(lf[:, :], lf[:, :], u[:, :], ALU.subtract))
                    q(dve.tensor_tensor_scan(bsum[:, :], one[:, :], lf[:, :], 0.0, ALU.mult, ALU.add))
                    q(dve.tensor_tensor(a[:, :], li[:, :], bsum[:, :], ALU.subtract))
                    q(dve.tensor_tensor_scan(top[:, :], one[:, :], a[:, :], 0.0, ALU.mult, ALU.max))
                    for j in range(TT):
                        q(dve.tensor_tensor_reduce(diag[:, :], a[:, tile_cols(j)], c.tab("ident"), 1.0, 0.0, ALU.mult,
                                                   ALU.add, acol[:, j:j + 1]))
                        q(dve.tensor_tensor(e[:, j, 0:S - j * P], c.tab("mask_after")[:, 0:S - j * P], top[:, j * P:S], ALU.subtract))
                    steps.done(dve.tensor_tensor(em[:, :], bsum[:, :], top[:, :], ALU.add), "gates")
                    if not last_round:
                        ahead.vector(dve, h + 1, 0)
                        ahead.vector(dve, h + 1, 1)
                    steps.wait(dve, "scored", h)
                    for j in range(TT):
                        ej = e[:, j, 0:S - j * P]
                        last = dve.scalar_tensor_tensor(ej, b[j][:, 0:S - j * P], 0.125, ej, ALU.mult, ALU.mult)
                        if j < TT - 1:
                            q(last)
                    steps.done(last, "weighted")
                    if not last_round:
                        ahead.vector(dve, h + 1, 2)
                    steps.wait(dve, "absden", h)
                    q(dve.tensor_tensor(hh[:, :], u[:, :], em[:, :], ALU.max))
                    q(dve.reciprocal(hh[:, :], hh[:, :]))
                    steps.done(dve.tensor_tensor(hh[:, :], hh[:, :], b[4][:, :], ALU.mult), "divided")
                    if not last_round:
                        ahead.vector(dve, h + 1, 3)
                    steps.wait(dve, "rooted", h)
                    q(dve.scalar_tensor_tensor(u[:, :], u[:, :], c.col("ml_ng", h), og[:, :], ALU.mult, ALU.mult))
                    q(dve.tensor_tensor(u[:, :], u[:, :], hh[:, :], ALU.mult))
                    q(dve.tensor_copy(y.hi[:, h, :], u[:, :]))
                    steps.done(dve.tensor_tensor(y.lo[:, h, :], u[:, :], y.value[:, h, :], ALU.subtract), "stored")
                rounds3(dve, heads, body, q)


def ssd(c, name, x, w_d, y, small):
    nc = c.nc
    with Stage(nc, name) as st:
        box = st.sb("box", [P, S])
        pick = st.sb("pick", [P, 2, P])
        pad, conv = st.sb("pad", [P, 3, S + 3]), st.sb("conv", [P, 3, S])
        z, one, la = st.sb("z", [P, S]), st.sb("one", [P, S]), st.sb("la", [P, 2, S])
        dt, u = st.sb("dt", [P, 2, S]), st.sb("u", [P, 2, S])
        rate, acol, dcol = st.sb("rate", [P, 2]), st.sb("acol", [P, 2, TT]), st.sb("dcol", [P, 2, TT])
        diag = st.sb("diag", [P, P])
        e = st.sb("e", [P, 2, TT, S])
        xz = st.sb("xz", [P, 2, TT, P])
        b = [st.ps(f"b{i}", [P, S]) for i in range(8)]
        zeroed, achain, chain, summed, expd = (st.sem(n) for n in ("zeroed", "achain", "chain", "summed", "expd"))
        steps = Steps(st.sem("steps"), "picked rows taken convolved activated turned weighted mixed stored")
        ahead = Ahead(st, c, x, w_d, 4, [pad[:, 0, 3:], box[:, :], pad[:, 1, 3:], pad[:, 2, 3:]],
                      [b[6][:, :], b[7][:, :]], 1)
        fetch = {(0, 3): 2, (1, 3): 3}
        with nc.Block() as block:
            @block.sync
            def _(sp):
                rounds(sp, 4, lambda i, first: ahead.sync(sp, i, first))
                ahead.sync_end(sp)

            @block.tensor
            def _(pe):
                ahead.tensor_start(pe)

                def body(i, first, last_round):
                    steps.wait(pe, "picked", i)
                    for h in range(2):
                        last = pe.matmul(b[4 + h][:, :], pick[:, h, :], small[:, :], start=True, stop=True)
                    steps.done(last, "rows")
                    if not last_round:
                        ahead.tensor(pe, i + 1, 0)
                        ahead.tensor(pe, i + 1, 1)
                    steps.wait(pe, "activated", i)
                    for t in range(TT):
                        pe.transpose(b[0][:, tile_cols(t)], conv[:, 0, tile_cols(t)], c.tab("ident"))
                    for j in range(TT):
                        last = pe.matmul(b[1 + j][:, 0:S - j * P], conv[:, 1, tile_cols(j)], conv[:, 2, j * P:S], start=True, stop=True)
                    steps.done(last, "turned")
                    if not last_round:
                        ahead.tensor(pe, i + 1, 2)
                        ahead.tensor(pe, i + 1, 3)
                    steps.wait(pe, "weighted", i)
                    for h in range(2):
                        for j in range(TT):
                            last = pe.matmul(b[5][:, j * P:S], xz[:, h, j, :], e[:, h, j, 0:S - j * P],
                                             start=h == 0 and j == 0, stop=h == 1 and j == TT - 1)
                    steps.done(last, "mixed")
                rounds3(pe, 4, body)

            @block.scalar
            def _(act):
                act.wait_ge(zeroed, 3)
                q = InOrder(act, achain)
                ahead.scalar_start(act)

                def body(i, first, last_round):
                    act.preload_act_table_set("natural_log_exp_and_others")
                    steps.wait(act, "rows", i)
                    for h in range(2):
                        q(act.activation(dt[:, h, :], b[4 + h][:, :], ACT.Identity, bias=c.col("sd_dtb", 2 * i + h)))
                        last = log_sigmoid_act(act, q, u[:, h, :], dt[:, h, :])
                        if h == 0:
                            q(last)
                    steps.done(last, "taken")
                    q(act.activation(rate[:, 0:1], c.col("sd_alog", 2 * i), ACT.Exp))
                    q(act.activation(rate[:, 1:2], c.col("sd_alog", 2 * i + 1), ACT.Exp))
                    if not last_round:
                        ahead.round_next(act, i + 1, 0)
                    ahead.landed(act, i)
                    q(act.activation(z[:, :], box[:, :], ACT.Silu))
                    steps.wait(act, "convolved", i)
                    steps.done(act.activation(conv[:, :, :], conv[:, :, :], ACT.Silu), "activated")
                    act.preload_act_table_set("natural_log_exp_and_others")
                    if not last_round:
                        ahead.move(act, i + 1, 0)
                        ahead.scalar(act, i + 1, 1)
                    for h in range(2):
                        for j in range(TT):
                            act.wait_ge(summed, 8 * i + 4 * h + j + 1)
                            act.activation(e[:, h, j, 0:S - j * P], e[:, h, j, 0:S - j * P], ACT.Exp,
                                           bias=acol[:, h, j:j + 1]).then_inc(expd, 1)
                            if (h, j) in fetch and not last_round:
                                ahead.scalar(act, i + 1, fetch[h, j])
                rounds3(act, 4, body, q)

            @block.vector
            def _(dve):
                dve.memset(pad[:, :, 0:3], 0.0).then_inc(zeroed, 1)
                dve.memset(one[:, :], 1.0).then_inc(zeroed, 1)
                dve.memset(xz[:, :, :, :], 0.0).then_inc(zeroed, 1)
                dve.wait_ge(zeroed, 3)
                q = InOrder(dve, chain)
                ahead.vector_start(dve)

                def body(i, first, last_round):
                    if not first:
                        steps.wait_round(dve, i)
                    q(pick_row(dve, c, pick[:, 0, :], 2 * i + 8))
                    steps.done(pick_row(dve, c, pick[:, 1, :], 2 * i + 9), "picked")
                    ahead.landed(dve, i)
                    causal_conv(dve, q, conv[:, 0, :], pad[:, 0, :], 4, lambda k: c.col("sd_cwx", i * 4 + k), c.col("sd_cbx", i))
                    for n in range(2):
                        causal_conv(dve, q, conv[:, 1 + n, :], pad[:, 1 + n, :], 4,
                                    lambda k: c.col("sd_cwbc", i * 8 + n * 4 + k), c.col("sd_cbbc", i * 2 + n))
                        if n == 0 and not last_round:
                            ahead.vector(dve, i + 1, 0)
                    steps.wait(dve, "taken", i)
                    q(dve.tensor_scalar(dt[:, :, :], dt[:, :, :], 0.0, None, ALU.max))
                    steps.done(dve.tensor_tensor(dt[:, :, :], dt[:, :, :], u[:, :, :], ALU.add), "convolved")
                    steps.wait(dve, "activated", i)
                    if not last_round:
                        ahead.vector(dve, i + 1, 1)
                    for h in range(2):
                        q(dve.tensor_scalar(la[:, h, :], dt[:, h, :], rate[:, h:h + 1], -1.0, ALU.mult, ALU.mult))
                        for j in range(TT):
                            ej = e[:, h, j, 0:S - j * P]
                            q(dve.tensor_tensor_scan(ej, one[:, 0:S - j * P], la[:, h, j * P:S], 0.0, ALU.mult, ALU.add))
                            q(dve.tensor_tensor_reduce(diag[:, :], ej[:, 0:P], c.tab("ident"), -1.0, 0.0, ALU.mult, ALU.add,
                                                       acol[:, h, j:j + 1]))
                            q(dve.tensor_tensor_reduce(diag[:, :], dt[:, h, tile_cols(j)], c.tab("ident"), 1.0, 0.0, ALU.mult,
                                                       ALU.add, dcol[:, h, j:j + 1]))
                            dve.tensor_tensor(ej[:, 0:P], ej[:, 0:P], c.tab("mask_after")[:, 0:P], ALU.add).then_inc(summed, 1)
                            if (h, j) in fetch and not last_round:
                                ahead.vector(dve, i + 1, fetch[h, j])
                    steps.wait(dve, "turned", i)
                    for h in range(2):
                        for j in range(TT):
                            ej = e[:, h, j, 0:S - j * P]
                            dve.wait_ge(expd, 8 * i + 4 * h + j + 1)
                            q(dve.tensor_tensor(ej, ej, b[1 + j][:, 0:S - j * P], ALU.mult))
                            last = dve.tensor_scalar(xz[:, h, j, 64 * h:64 * h + 64], b[0][:, j * P + 64 * h:j * P + 64 * h + 64],
                                                     dcol[:, h, j:j + 1], None, ALU.mult)
                            if (h, j) != (1, TT - 1):
                                q(last)
                    steps.done(last, "weighted")
                    steps.wait(dve, "mixed", i)
                    q(dve.scalar_tensor_tensor(conv[:, 0, :], conv[:, 0, :], c.col("sd_d", i), b[5][:, :], ALU.mult, ALU.add))
                    steps.done(dve.tensor_tensor(y[:, i, :], conv[:, 0, :], z[:, :], ALU.mult), "stored")
                rounds3(dve, 4, body, q)


class Events:

    def __init__(self, st, **per):
        self.per = per
        self.sems = {name: st.sem(name) for name in per}

    def done(self, ins, name):
        ins.then_inc(self.sems[name], 1)

    def wait(self, eng, name, r, i=None):
        i = self.per[name] - 1 if i is None else i
        eng.wait_ge(self.sems[name], r * self.per[name] + i + 1)


def rwkv(c, name, x, w_d, up_d, y, lora):
    nc = c.nc
    with Stage(nc, name) as st:
        up = st.sb("up", [P, 3, P])
        pad = st.sb("pad", [P, 3, S + 1])
        rkv = st.sb("rkv", [P, 3, S])
        ld, g, gp, aa, kn, tmp, gg, rhat, ahat, winv, wfull, bhat, khat = (
            st.sb(n, [P, S]) for n in ("ld", "g", "gp", "aa", "kn", "tmp", "gg", "rhat", "ahat", "winv", "wfull", "bhat", "khat"))
        bt, kt = st.sb("bt", [P, 2, TT, P]), st.sb("kt", [P, 2, TT, P])
        v, ta, tnv = (st.sb(n, [P, TT, P]) for n in ("v", "ta", "tnv"))
        mt, nt, rb, rk = (st.sb(n, [P, 2, TT, P]) for n in ("mt", "nt", "rb", "rk"))
        tri, inv, part, level = (st.sb(n, [P, 2, TT, P]) for n in ("tri", "inv", "part", "level"))
        state = st.sb("state", [P, NC, P])
        b = [st.ps(f"b{i}", [P, S]) for i in range(8)]
        landed, achain, chain, pre = (st.sem(n) for n in ("landed", "achain", "chain", "pre"))
        steps = LEVELS - 1
        ev = Events(st, lora_up=1, gates=1, kshifted=1, squared=1, normed=1, decays=1, exps=1, clamped=1, rooted=1, hats=1,
                    mt_made=2, turned=1, tcopied=1, bonus_made=1, bonused=1, inv0=2, tri_made=2, side_made=6, sided=6,
                    part0=steps, part1=steps, lpart0=steps, lpart1=steps, tp0=steps, tp1=steps, level0=steps, level1=steps,
                    updated0=steps + 1, updated1=steps + 1, nv_made=1, nv_here=1, ta_made=1, ta_here=1, g_made=1, gt_here=1,
                    h_made=1, r_made=1, rfolded=1, grown=NC - 2, state=NC - 1, mixed=1, gathered0=1, gathered1=1, meaned=1,
                    centred=1, csquared=1, varied=1, croot=1, scaled=1, affine=1, stored=1)
        ahead = Ahead(st, c, x, w_d, 4, [pad[:, n, 1:] for n in range(3)], [b[7][:, :]], 1)
        fetch = {1: 0, 3: 1}
        by_tile = "p (t f) -> p t f"
        heads = [slice(64 * h, 64 * h + 64) for h in range(2)]

        def bank(n):
            return b[n][:, :].rearrange(by_tile, t=TT)

        def growth(n):
            return mt[:, n // TT, n % TT, :], nt[:, n // TT, n % TT, :]

        with nc.Block() as block:
            @block.sync
            def _(sp):
                def body(p, first):
                    ahead.sync(sp, p, first)
                    if not first:
                        ev.wait(sp, "lora_up", p - 1)
                    sp.dma_start(up[:, :, :], up_d[p]).then_inc(landed, 16)
                rounds(sp, 4, body)
                ahead.sync_end(sp)

            @block.tensor
            def _(pe):
                ahead.tensor_start(pe)

                def body(p, first, last_round):
                    pe.wait_ge(landed, 16 * (p + 1))
                    if first:
                        pe.wait_ge(pre, 3)
                    for n, out in enumerate((0, 3, 6)):
                        last = pe.matmul(b[out][:, :], up[:, n, :], lora[:, 1 if n < 2 else 2, :], start=True, stop=True)
                    ev.done(last, "lora_up")
                    ev.wait(pe, "squared", p)
                    ev.done(pe.matmul(b[4][:, :], c.tab("head_ones"), tmp[:, :], start=True, stop=True), "normed")
                    ev.wait(pe, "hats", p)

                    def pair(out, l, r_, h):
                        for t in range(TT):
                            last = pe.matmul(b[out][:, tile_cols(t)], l[heads[h], tile_cols(t)], r_[heads[h], tile_cols(t)],
                                             start=True, stop=True)
                        return last
                    for h in range(2):
                        ev.done(pair(3 * h, bhat, ahat, h), "mt_made")
                    for out, src in ((1, bhat[:, :]), (2, khat[:, :]), (4, rkv[:, 2, :]), (5, ahat[:, :])):
                        for t in range(TT):
                            last = pe.transpose(b[out][:, tile_cols(t)], src[:, tile_cols(t)], c.tab("ident"))
                    ev.done(last, "turned")
                    ev.done(pe.matmul(b[6][:, :], c.tab("head_ones"), tmp[:, :], start=True, stop=True), "bonus_made")
                    for h in range(2):
                        ev.wait(pe, "inv0", p, h)
                        for t in range(TT):
                            last = pe.transpose(b[3 * h][:, tile_cols(t)], inv[:, h, t, :], c.tab("ident"))
                        ev.done(last, "tri_made")

                    sides = [(khat, ahat, 0), (khat, ahat, 1), (bhat, rhat, 0), (bhat, rhat, 1), (khat, rhat, 0), (khat, rhat, 1)]

                    def side(k):
                        if k == 0:
                            ev.wait(pe, "bonused", p)
                        else:
                            ev.wait(pe, "sided", p, k - 1)
                        ev.done(pair(6, *sides[k]), "side_made")

                    for i in range(steps):
                        for h in range(2):
                            ev.wait(pe, f"level{h}", p, i)
                            ev.wait(pe, f"updated{h}", p, i)
                            for t in range(TT):
                                last = pe.matmul(b[3 * h][:, tile_cols(t)], level[:, h, t, :], tri[:, h, t, :], start=True, stop=True)
                            ev.done(last, f"part{h}")
                        if i < 3:
                            side(2 * i)
                        if i == 3:
                            ev.wait(pe, "sided", p)
                            for h in range(2):
                                for t in range(TT):
                                    last = pe.matmul(bank(6)[:, t, heads[h]], nt[:, h, t, :], v[:, t, heads[h]], start=True, stop=True)
                            ev.done(last, "nv_made")
                        if not last_round:
                            ahead.tensor_share(pe, p + 1, i, steps + 1)
                        if i == 0:
                            ev.wait(pe, "tcopied", p)
                        for h in range(2):
                            ev.wait(pe, f"lpart{h}", p, i)
                            if i < steps - 1:
                                for t in range(TT):
                                    pe.matmul(b[3 * h + 1][:, tile_cols(t)], inv[:, h, t, :], part[:, h, t, :], start=True, stop=True)
                            for t in range(TT):
                                last = pe.matmul(b[3 * h + 2][:, tile_cols(t)], part[:, h, t, :], inv[:, h, t, :], start=True, stop=True)
                            ev.done(last, f"tp{h}")
                        if i < 3:
                            side(2 * i + 1)
                    ev.wait(pe, "nv_here", p)
                    for h in range(2):
                        ev.wait(pe, f"updated{h}", p)
                        for out, r_ in ((0, ta), (3, tnv)):
                            for t in range(TT):
                                last = pe.matmul(bank(out)[:, t, heads[h]], inv[:, h, t, :], r_[:, t, heads[h]], start=True, stop=True)
                    ev.done(last, "ta_made")
                    if not last_round:
                        ahead.tensor_share(pe, p + 1, steps, steps + 1)
                    ev.wait(pe, "ta_here", p)
                    for n in range(1, NC - 1):
                        out = bank(1 + n // TT)[:, n % TT, :]
                        pe.matmul(out, c.tab("ident"), c.tab("ident"), start=True, stop=False)
                        last = pe.matmul(out, ta[:, n // 2, :], bt[:, n % 2, n // 2, :], start=False, stop=True)
                    ev.done(last, "g_made")
                    for n in range(NC - 1):
                        out = bank(4 + n // TT)[:, n % TT, :]
                        pe.matmul(out, kt[:, n % 2, n // 2, :], v[:, n // 2, :], start=True, stop=False)
                        last = pe.matmul(out, bt[:, n % 2, n // 2, :], tnv[:, n // 2, :], start=False, stop=True)
                    ev.done(last, "h_made")
                    for h in range(2):
                        for t in range(TT):
                            last = pe.matmul(bank(3 * h)[:, t, :], ta[:, t, :], rb[:, h, t, :], start=True, stop=True)
                    ev.done(last, "r_made")
                    ev.wait(pe, "gt_here", p)
                    for n in range(1, NC - 1):
                        ev.wait(pe, "state", p, n - 1)
                        ev.done(pe.matmul(bank(6)[:, n % TT, :], growth(n)[0], state[:, n, :], start=True, stop=True), "grown")
                        if n <= TT:
                            t = n - 1
                            for h in range(2):
                                pe.matmul(bank(1 + h)[:, t, :], tnv[:, t, :], rb[:, h, t, :], start=t == 0, stop=False,
                                          skip_group_check=True)
                                pe.matmul(bank(1 + h)[:, t, :], v[:, t, :], rk[:, h, t, :], start=False, stop=False,
                                          skip_group_check=True)
                    ev.wait(pe, "rfolded", p)
                    for n in range(1, NC):
                        cols = slice(n * CHUNK, (n + 1) * CHUNK)
                        if n == NC - 1:
                            ev.wait(pe, "state", p)
                        for h in range(2):
                            last = pe.matmul(b[1 + h][:, cols], state[:, n, :], rhat[:, cols], start=False, stop=n == NC - 1,
                                             skip_group_check=True)
                    ev.done(last, "mixed")
                    ev.wait(pe, "gathered0", p)
                    ev.wait(pe, "gathered1", p)
                    ev.done(pe.matmul(b[4][:, :], c.tab("head_ones"), kn[:, :], start=True, stop=True), "meaned")
                    ev.wait(pe, "csquared", p)
                    ev.done(pe.matmul(b[5][:, :], c.tab("head_ones"), tmp[:, :], start=True, stop=True), "varied")
                rounds3(pe, 4, body)

            @block.scalar
            def _(act):
                q = InOrder(act, achain)
                act.wait_ge(pre, 1)
                act.activation(lora[0:64, 1, :], lora[0:64, 1, :], ACT.Tanh).then_inc(pre, 1)
                act.activation(lora[:, 2, :], lora[:, 2, :], ACT.Sigmoid).then_inc(pre, 1)
                ahead.scalar_start(act)

                def body(p, first, last_round):
                    if not first:
                        ev.wait(act, "stored", p - 1)
                    ev.wait(act, "lora_up", p)
                    q.free(act.activation(ld[:, :], b[0][:, :], ACT.Sigmoid, bias=c.col("w0", p)))
                    q.free(act.activation(aa[:, :], b[3][:, :], ACT.Sigmoid, bias=c.col("a0", p)))
                    ev.done(act.activation(gg[:, :], b[6][:, :], ACT.Copy), "gates")
                    act.preload_act_table_set("natural_log_exp_and_others")
                    ev.wait(act, "kshifted", p)
                    q(act.activation(kn[:, :], rkv[:, 1, :], ACT.Copy, scale=c.col("k_k", p)))
                    ev.done(act.activation(tmp[:, :], kn[:, :], ACT.Square), "squared")
                    ev.wait(act, "decays", p)
                    q.free(act.activation(wfull[:, :], g[:, :], ACT.Exp))
                    q.free(act.activation(winv[:, :], g[:, :], ACT.Exp, scale=-1.0))
                    ev.done(act.activation(gp[:, :], gp[:, :], ACT.Exp), "exps")
                    ev.wait(act, "clamped", p)
                    q(act.activation(tmp[:, :], tmp[:, :], ACT.Ln))
                    ev.done(act.activation(tmp[:, :], tmp[:, :], ACT.Exp, scale=-0.5), "rooted")
                    ev.wait(act, "turned", p)
                    for dst, n in ((bt, 1), (kt, 2)):
                        for half in range(2):
                            rows = heads[half]
                            q.free(act.activation(dst[rows, half, :, :], b[n][rows, :].rearrange(by_tile, t=TT), ACT.Copy))
                    q.free(act.activation(v[:, :, :], bank(4), ACT.Copy))
                    ev.done(act.activation(ta[:, :, :], bank(5), ACT.Copy), "tcopied")
                    for i in range(steps):
                        for h in range(2):
                            ev.wait(act, f"part{h}", p, i)
                            ev.done(act.activation(part[:, h, :, :], bank(3 * h), ACT.Copy), f"lpart{h}")
                        if i == 3:
                            ev.wait(act, "nv_made", p)
                            ev.done(act.activation(tnv[:, :, :], bank(6), ACT.Copy), "nv_here")
                        if i in fetch and not last_round:
                            ahead.scalar(act, p + 1, fetch[i])
                    ev.wait(act, "ta_made", p)
                    q.free(act.activation(ta[:, :, :], bank(0), ACT.Copy, scale=-1.0))
                    ev.done(act.activation(tnv[:, :, :], bank(3), ACT.Copy, scale=-1.0), "ta_here")
                    if not last_round:
                        ahead.scalar(act, p + 1, 2)
                    ev.wait(act, "mixed", p)
                    ev.done(act.activation(kn[heads[1], :], b[2][heads[1], :], ACT.Copy), "gathered1")
                    ev.wait(act, "centred", p)
                    ev.done(act.activation(tmp[:, :], kn[:, :], ACT.Square), "csquared")
                    ev.wait(act, "varied", p)
                    q(act.activation(g[:, :], b[5][:, :], ACT.Copy, scale=1.0 / 64, bias=64e-5))
                    q(act.activation(g[:, :], g[:, :], ACT.Ln))
                    ev.done(act.activation(g[:, :], g[:, :], ACT.Exp, scale=-0.5), "croot")
                    ev.wait(act, "scaled", p)
                    ev.done(act.activation(kn[:, :], kn[:, :], ACT.Identity, scale=c.col("gn_g", p), bias=c.col("gn_b", p)), "affine")
                rounds3(act, 4, body, q)

            @block.vector
            def _(dve):
                q = InOrder(dve, chain)
                q(dve.memset(pad[:, :, 0:1], 0.0))
                for n in (1, 2):
                    q(dve.tensor_tensor(tmp[:, 1:S], lora[:, n, 0:S - 1], lora[:, n, 1:S], ALU.subtract))
                    q(dve.tensor_scalar(tmp[:, 0:1], lora[:, n, 0:1], -1.0, None, ALU.mult))
                    q(dve.scalar_tensor_tensor(lora[:, n, :], tmp[:, :], c.col("lora_mu", n - 1), lora[:, n, :], ALU.mult, ALU.add))
                q(dve.memset(bt[:, :, :, :], 0.0))
                dve.memset(kt[:, :, :, :], 0.0).then_inc(pre, 1)
                ahead.vector_start(dve)

                def wide(name_):
                    return c.tab(name_).rearrange("p (o t) -> p o t", o=1).broadcast_to([P, TT, P])

                def body(p, first, last_round):
                    def shift(n, mu, done=None):
                        q(dve.tensor_tensor(rkv[:, n, :], pad[:, n, 0:S], pad[:, n, 1:S + 1], ALU.subtract))
                        last = dve.scalar_tensor_tensor(rkv[:, n, :], rkv[:, n, :], c.col(mu, p), pad[:, n, 1:S + 1], ALU.mult, ALU.add)
                        if done:
                            ev.done(last, done)
                        else:
                            q.free(last)
                    ahead.landed(dve, p)
                    shift(1, "k_mu", "kshifted")
                    ev.wait(dve, "gates", p)
                    q(dve.tensor_scalar(ld[:, :], ld[:, :], -DECAY_SCALE, None, ALU.mult))
                    q(dve.tensor_tensor_scan(g[:, :], c.tab("restart"), ld[:, :], 0.0, ALU.mult, ALU.add))
                    ev.done(dve.tensor_tensor(gp[:, :], g[:, :], ld[:, :], ALU.subtract), "decays")
                    shift(0, "r_mu")
                    ev.wait(dve, "normed", p)
                    ev.done(dve.tensor_scalar(tmp[:, :], b[4][:, :], 1e-24, None, ALU.max), "clamped")
                    shift(2, "v_mu")
                    ev.wait(dve, "decays", p)
                    q(dve.tensor_scalar(ld[:, :], aa[:, :], 1.0, c.col("k_a", p), ALU.subtract, ALU.mult))
                    q(dve.scalar_tensor_tensor(rkv[:, 1, :], ld[:, :], 1.0, rkv[:, 1, :], ALU.add, ALU.mult))
                    ev.wait(dve, "exps", p)
                    q.free(dve.tensor_tensor(rhat[:, :], rkv[:, 0, :], wfull[:, :], ALU.mult))
                    q.free(dve.tensor_tensor(khat[:, :], rkv[:, 1, :], winv[:, :], ALU.mult))
                    ev.wait(dve, "rooted", p)
                    q(dve.tensor_tensor(kn[:, :], kn[:, :], tmp[:, :], ALU.mult))
                    q.free(dve.tensor_tensor(ahat[:, :], kn[:, :], gp[:, :], ALU.mult))
                    q(dve.tensor_tensor(bhat[:, :], aa[:, :], winv[:, :], ALU.mult))
                    q.free(dve.tensor_tensor(bhat[:, :], bhat[:, :], kn[:, :], ALU.mult))
                    ev.done(dve.scalar_tensor_tensor(tmp[:, :], rkv[:, 0, :], c.col("r_k", p), rkv[:, 1, :], ALU.mult, ALU.mult), "hats")
                    for h in range(2):
                        ev.wait(dve, "mt_made", p, h)
                        q(dve.tensor_tensor(mt[:, h, :, :], bank(3 * h), wide("strict_chunk"), ALU.mult))
                        q(dve.tensor_tensor(level[:, h, :, :], mt[:, h, :, :], wide("level0"), ALU.mult))
                        ev.done(dve.tensor_tensor(inv[:, h, :, :], wide("ident"), level[:, h, :, :], ALU.subtract), "inv0")
                    ev.wait(dve, "inv0", p)
                    for h in range(2):
                        ev.done(dve.tensor_tensor(level[:, h, :, :], mt[:, h, :, :], wide("level1"), ALU.mult), f"level{h}")
                    for h in range(2):
                        ev.wait(dve, "tri_made", p, h)
                        ev.done(dve.tensor_copy(tri[:, h, :, :], bank(3 * h)), f"updated{h}")
                    ev.wait(dve, "bonus_made", p)
                    ev.done(dve.tensor_tensor(aa[:, :], rkv[:, 2, :], b[6][:, :], ALU.mult), "bonused")

                    sides = [(nt, 0, "strict_chunk"), (nt, 1, "strict_chunk"), (rb, 0, "causal_chunk"), (rb, 1, "causal_chunk"),
                             (rk, 0, "causal_chunk"), (rk, 1, "causal_chunk")]

                    def side(k):
                        dst, h, mask = sides[k]
                        ev.wait(dve, "side_made", p, k)
                        ev.done(dve.tensor_tensor(dst[:, h, :, :], bank(6), wide(mask), ALU.mult), "sided")

                    for i in range(steps):
                        if i < steps - 1:
                            for h in range(2):
                                ev.wait(dve, f"part{h}", p, i)
                                ev.done(dve.tensor_tensor(level[:, h, :, :], mt[:, h, :, :], wide(f"level{i + 2}"), ALU.mult), f"level{h}")
                        if i < 3:
                            side(2 * i)
                        for h in range(2):
                            ev.wait(dve, f"tp{h}", p, i)
                            ev.wait(dve, f"updated{h}", p, i)
                            if i < steps - 1:
                                q.free(dve.tensor_tensor(tri[:, h, :, :], tri[:, h, :, :], bank(3 * h + 1), ALU.subtract))
                            ev.done(dve.tensor_tensor(inv[:, h, :, :], inv[:, h, :, :], bank(3 * h + 2), ALU.subtract), f"updated{h}")
                        if i < 3:
                            side(2 * i + 1)
                        if i in fetch and not last_round:
                            ahead.vector(dve, p + 1, fetch[i])
                    ev.wait(dve, "g_made", p)
                    mask = c.tab("head_ones").rearrange("p (o t) -> p o t", o=1).broadcast_to([P, TT - 1, P])
                    q.free(dve.tensor_tensor(mt[:, 0, 1:TT, :], bank(1)[:, 1:TT, :], mask, ALU.mult))
                    ev.done(dve.tensor_tensor(mt[:, 1, 0:TT - 1, :], bank(2)[:, 0:TT - 1, :], mask, ALU.mult), "gt_here")
                    ev.wait(dve, "h_made", p)

                    def end(n):
                        return wfull[:, (n + 1) * CHUNK - 1:(n + 1) * CHUNK]
                    for n in range(NC - 1):
                        dst = state[:, 1, :] if n == 0 else growth(n)[1]
                        h_n = dve.scalar_tensor_tensor(dst, bank(4 + n // TT)[:, n % TT, :], end(n), c.tab("head_ones"), ALU.mult, ALU.mult)
                        if n == 0:
                            ev.done(h_n, "state")
                            continue
                        q(h_n)
                        ev.wait(dve, "grown", p, n - 1)
                        ev.done(dve.scalar_tensor_tensor(state[:, n + 1, :], bank(6)[:, n % TT, :], end(n), dst, ALU.mult, ALU.add), "state")
                        if n == 2:
                            ev.wait(dve, "r_made", p)
                            q.free(dve.tensor_tensor(rhat[heads[0], :], rhat[heads[0], :], b[0][heads[0], :], ALU.add))
                            ev.done(dve.tensor_tensor(rhat[heads[1], :], rhat[heads[1], :], b[3][heads[1], :], ALU.add), "rfolded")
                    if not last_round:
                        ahead.vector(dve, p + 1, 2)
                    ev.wait(dve, "mixed", p)
                    ev.done(dve.tensor_copy(kn[heads[0], :], b[1][heads[0], :]), "gathered0")
                    ev.wait(dve, "meaned", p)
                    ev.done(dve.scalar_tensor_tensor(kn[:, :], b[4][:, :], -1.0 / 64, kn[:, :], ALU.mult, ALU.add), "centred")
                    ev.wait(dve, "croot", p)
                    ev.done(dve.tensor_tensor(kn[:, :], kn[:, :], g[:, :], ALU.mult), "scaled")
                    ev.wait(dve, "affine", p)
                    q(dve.tensor_tensor(kn[:, :], kn[:, :], aa[:, :], ALU.add))
                    q(dve.tensor_tensor(kn[:, :], kn[:, :], gg[:, :], ALU.mult))
                    q(dve.tensor_copy(y.hi[:, p, :], kn[:, :]))
                    ev.done(dve.tensor_tensor(y.lo[:, p, :], kn[:, :], y.value[:, p, :], ALU.subtract), "stored")
                rounds3(dve, 4, body, q)


def gelu_values(c, name, x, w_d, v, sums):
    nc = c.nc
    chunks, halves, kc = 4, 2, DT // 2
    with Stage(nc, name) as st:
        feed = Feed(st, kc * S, halves, 2)
        acc = st.ps("acc", [P, 2, TT, S])
        made, done = st.sem("made"), st.sem("done")
        with nc.Block() as block:
            @block.sync
            def _(sp):
                def body(r, first):
                    for m in range(halves):
                        feed.load(sp, r, m, first, w_d[r, :, m, :])
                rounds(sp, chunks, body)

            @block.tensor
            def _(pe):
                for r in range(chunks):
                    for m in range(halves):
                        s, slot = feed.at(r, m)
                        pe.wait_ge(feed.parted, s + 1)
                        for t in range(TT):
                            if m == 0 and r >= 2:
                                pe.wait_ge(done, TT * (r - 2) + t + 1)
                            for k in range(kc):
                                for n, (a_, w_) in enumerate(((x.hi, feed.hi), (x.lo, feed.hi), (x.hi, feed.lo))):
                                    last = pe.matmul(acc[:, r % 2, t, :], a_[:, m * kc + k, tile_cols(t)],
                                                     w_[:, slot, k * S:(k + 1) * S], start=m == 0 and k == 0 and n == 0,
                                                     stop=m == halves - 1 and k == kc - 1 and n == 2)
                            if m == halves - 1 and t < TT - 1:
                                last.then_inc(made, 1)
                        last.then_inc(feed.used, 1)

            @block.scalar
            def _(act):
                for m in range(2):
                    feed.round(act, 0, m, True, kc * S)
                for r in range(chunks):
                    for m in range(halves):
                        if r < chunks - 1:
                            feed.round(act, r + 1, m, False, kc * S)
                    for t in range(TT):
                        if t < TT - 1:
                            act.wait_ge(made, (TT - 1) * r + t + 1)
                        else:
                            act.wait_ge(feed.used, halves * (r + 1))
                        act.activation(v[:, t, r * S:(r + 1) * S], acc[:, r % 2, t, :], ACT.Gelu_apprx_tanh,
                                       accum_out=sums[:, t, r:r + 1]).then_inc(done, 1)

            @block.vector
            def _(dve):
                def body(r, first):
                    for m in range(halves):
                        feed.rest(dve, r, m, kc * S)
                rounds(dve, chunks, body)


def spatial_gate(c, name, v, sums, u, bs_d, ws_d, pair):
    nc = c.nc
    width = v.shape[2]
    groups, per = 8, 2
    with Stage(nc, name) as st:
        ws, bs = st.sb("ws", [P, groups, P]), st.sb("bs", [P, groups, P])
        wsum = st.sb("wsum", [P, groups, P])
        total, var, mean, negmean, rstd = (st.sb(n, [P, TT]) for n in ("total", "var", "mean", "negmean", "rstd"))
        acc, mixed, shift = st.ps("acc", [P, 2, S]), st.sb("mixed_s", [P, 3, S]), st.sb("shift", [P, 2, P])
        sq, rows = st.ps("sq", [P, width]), st.ps("rows", [P, 2, S])
        landed, chain, centred, rooted, achain, ready, masked, summed, made, gated, rounded, parted = (
            st.sem(n) for n in ("landed", "chain", "centred", "rooted", "achain", "ready", "masked", "summed",
                                "made", "gated", "rounded", "parted"))
        with nc.Block() as block:
            @block.sync
            def _(sp):
                sp.dma_start(bs[:, :, :], bs_d).then_inc(landed, 16)
                sp.dma_start(ws[:, :, :], ws_d).then_inc(landed, 16)

            @block.scalar
            def _(act):
                act.preload_act_table_set("natural_log_exp_and_others")
                q = InOrder(act, achain)
                act.wait_ge(centred, 1)
                for t in range(TT):
                    q(act.activation(sq[:, :], v[:, t, :], ACT.Square, bias=negmean[:, t:t + 1], accum_out=var[:, t:t + 1]))
                q(act.activation(rstd[:, :], var[:, :], ACT.Copy, scale=1.0 / width, bias=1e-5))
                q(act.activation(rstd[:, :], rstd[:, :], ACT.Ln))
                act.activation(rstd[:, :], rstd[:, :], ACT.Exp, scale=-0.5).then_inc(rooted, 1)
                for m in range(groups * per):
                    act.wait_ge(gated, m + 1)
                    act.activation(pair.hi[:, m, :], mixed[:, m % 3, :], ACT.Copy).then_inc(rounded, 1)

            @block.vector
            def _(dve):
                q = InOrder(dve, chain)
                q(dve.tensor_reduce(total[:, :], sums[:, :, :], AX_X, ALU.add))
                q(dve.tensor_scalar(mean[:, :], total[:, :], 1.0 / width, None, ALU.mult))
                dve.tensor_scalar(negmean[:, :], mean[:, :], -1.0, None, ALU.mult).then_inc(centred, 1)
                dve.wait_ge(landed, 32)
                mask = c.tab("causal").rearrange("p (o t) -> p o t", o=1).broadcast_to([P, groups, P])
                dve.tensor_tensor(ws[:, :, :], ws[:, :, :], mask, ALU.mult).then_inc(masked, 1)
                dve.wait_ge(summed, 1)
                q(dve.tensor_copy(wsum[:, :, :], rows[:, :, :].rearrange("p a (g t) -> p (a g) t", t=P)))
                dve.wait_ge(rooted, 1)
                for t in range(TT):
                    dve.tensor_scalar(v[:, t, :], v[:, t, :], mean[:, t:t + 1], rstd[:, t:t + 1], ALU.subtract,
                                      ALU.mult).then_inc(ready, 1)

                def rest(m):
                    dve.wait_ge(rounded, m + 1)
                    dve.tensor_tensor(pair.lo[:, m, :], mixed[:, m % 3, :], pair.value[:, m, :], ALU.subtract).then_inc(parted, 1)

                for m in range(groups * per):
                    q(dve.scalar_tensor_tensor(shift[:, m % 2, :], wsum[:, m // per, :], c.col("gm_b", m), bs[:, m // per, :],
                                               ALU.mult, ALU.add))
                    dve.wait_ge(made, m + 1)
                    if m >= 3:
                        dve.wait_ge(parted, m - 2)
                    bias = shift[:, m % 2, :].rearrange("p (o t) -> p o t", o=1).broadcast_to([P, TT, P])
                    q(dve.scalar_tensor_tensor(mixed[:, m % 3, :].rearrange("p (t f) -> p t f", t=TT),
                                               acc[:, m % 2, :].rearrange("p (t f) -> p t f", t=TT), c.col("gm_g", m), bias,
                                               ALU.mult, ALU.add))
                    dve.tensor_tensor(mixed[:, m % 3, :], u[:, m, :], mixed[:, m % 3, :], ALU.mult).then_inc(gated, 1)
                    if m:
                        rest(m - 1)
                rest(groups * per - 1)

            @block.tensor
            def _(pe):
                pe.wait_ge(masked, 1)
                for g in range(groups):
                    last = pe.matmul(rows[:, g // TT, tile_cols(g % TT)], c.tab("ones"), ws[:, g, :], start=True, stop=True)
                last.then_inc(summed, 1)
                for m in range(groups * per):
                    if m >= 2:
                        pe.wait_ge(gated, m - 1)
                    for t in range(TT):
                        if m == 0:
                            pe.wait_ge(ready, t + 1)
                        last = pe.matmul(acc[:, m % 2, tile_cols(t)], v[:, t, tile_cols(m)], ws[:, m // per, :], start=True, stop=True)
                    last.then_inc(made, 1)


def build(nc, a, out_d):
    with ExitStack() as keep:
        def sb(name, shape, stack=keep):
            return stack.enter_context(nc.sbuf_tensor(name, shape, F32))

        def pair(name, tiles_, stack):
            return Pair(lambda n, shape, dtype: stack.enter_context(nc.sbuf_tensor(n, shape, dtype)), name, [P, tiles_, S])

        table, column = sb("table", [P, TABLE_WIDTH]), sb("column", [P, COLUMN_WIDTH])
        x = sb("x", [P, DT, S])
        c = Ctx(nc, table, column)
        load_constants(c, a["table"], a["column"], a["x"], x)

        with ExitStack() as blocks:
            xn = pair("xn", DT, blocks)
            split_all(c, "sx", x, DT, xn)
            with ExitStack() as s:
                hidden = pair("hidden1", FT, s)
                swiglu_up(c, "f1u", a["f1_up"], xn, hidden, FT)
                project(c, "f1d", a["f1_down"], hidden, FT, DT, x, residual=x, res_scale=ALPHA, scale=0.5)
            norm(c, "ln1", x, x, DT, True, 1e-5, lambda k: c.col("ln1_g", k), lambda k: c.col("ln1_b", k), xn)
            with ExitStack() as s:
                y_a = pair("y_attn", DT, s)
                attention(c, "att", xn, a["att_w"], y_a, [[0], [0, 1], [1, 2], [2, 3]], 2,
                          qb=lambda p: c.col("att_qb", p), kb=lambda r: c.col("att_kb", r), vb=lambda r: c.col("att_vb", r),
                          sinks=lambda h, n=1: c.col("sinks", h, n), rope=True)
                y_h = pair("y_hgrn", DT, s)
                linear_recurrence(c, "hg", xn, a["hg_w"], 8, y_h, "hgrn", c.col("hg_ng"), qb=lambda h: c.col("hg_qb", h),
                                  fb=lambda h: c.col("hg_fb", h), vb=lambda h: c.col("hg_vb", h), ogb=lambda h: c.col("hg_ogb", h),
                                  lb=c.col("hg_lb", 0, 16))
                merged = pair("merged1", DT, s)
                merge(c, "mg1", xn, a["mg1_w"], [y_a, y_h], DT, pair=merged, gate_b=lambda b, m: c.col("gate_b", b * DT + m))
                project(c, "wo1", a["wo1"], merged, DT, DT, x, residual=x, res_scale=ALPHA)
            norm(c, "ln2", x, x, DT, True, 1e-5, lambda k: c.col("ln2_g", k), lambda k: c.col("ln2_b", k), xn)
            with ExitStack() as s:
                hidden = pair("hidden2", FT, s)
                swiglu_up(c, "f2u", a["f2_up"], xn, hidden, FT)
                project(c, "f2d", a["f2_down"], hidden, FT, DT, x, residual=x, res_scale=ALPHA, scale=0.5)
            norm(c, "ln3", x, x, DT, True, 1e-5, lambda k: c.col("ln3_g", k), lambda k: c.col("ln3_b", k))

            norm(c, "rn1", x, None, DT, False, 1e-6, lambda k: c.col("mix2_g", k), pair=xn)
            with ExitStack() as s:
                low = sb("low", [P, 4, S], s)
                project(c, "low", a["low_w"], xn, DT, 4, low)
                y_0 = pair("y_0", 4, s)
                rwkv(c, "rw", xn, a["rw_w"], a["rw_up"], y_0, low)
                y_1, part = pair("y_1", 4, s), sb("part", [P, DT, S], s)
                linear_recurrence(c, "gla", xn, a["gla_w"], 4, y_1, "gla", c.col("gla_ng"), fb=lambda h: c.col("gla_fb", h),
                                  small=low[:, 0, :], fup_d=a["gla_fup"])
                merge(c, "mg2", xn, a["mg2_w"][:, 0:2], [y_0, y_1], 4, out=part)
                mlstm(c, "ml", xn, a["ml_w"], 4, y_0, low[:, 0, :])
                with ExitStack() as s2:
                    y_s = sb("y_ssd", [P, 4, S], s2)
                    ssd(c, "sd", xn, a["sd_w"], y_s, low[:, 0, :])
                    norm(c, "sdn", y_s, None, 4, False, 1e-6, lambda k: c.col("sd_ng", k), pair=y_1)
                merged = pair("merged2", DT, s)
                merge(c, "mg3", xn, a["mg2_w"][:, 2:4], [y_0, y_1], 4, so_far=part, pair=merged)
                project(c, "wo2", a["wo2"], merged, DT, DT, x, residual=x)
            norm(c, "rn2", x, None, DT, False, 1e-6, lambda k: c.col("ffn2_g", k), pair=xn)
            with ExitStack() as s:
                hidden = pair("hidden3", FT, s)
                conv_glu_up(c, "f3u", a["f3_up"], xn, hidden, FT,
                            lambda i, t: c.col("ffn2_cw", i * 2 * FT + t), lambda t: c.col("ffn2_cb", t),
                            lambda i, t: c.col("ffn2_cw", i * 2 * FT + FT + t), lambda t: c.col("ffn2_cb", FT + t))
                project(c, "f3d", a["f3_down"], hidden, FT, DT, x, residual=x)
            norm(c, "rn3", x, x, DT, False, 1e-6, lambda k: c.col("fin2_g", k))

        with ExitStack() as s:
            u, v, sums = sb("u", [P, 16, S], s), sb("v", [P, TT, 16 * P], s), sb("sums", [P, TT, 4], s)
            with ExitStack() as s2:
                xn = pair("xm", DT, s2)
                norm(c, "m0", x, None, DT, False, 1e-6, lambda k: c.col("mix3_g", k), pair=xn)
                project(c, "gmu", a["gm_u"], xn, DT, 16, u, func=ACT.Gelu_apprx_tanh)
                gelu_values(c, "gmv", xn, a["gm_v"], v, sums)
            mixed = pair("mixed", 16, s)
            spatial_gate(c, "gms", v, sums, u, a["gm_bs"], a["gm_ws"], mixed)
            project(c, "gmo", a["gm_out"], mixed, 16, DT, x, residual=x)
        with ExitStack() as blocks:
            xn = pair("xo", DT, blocks)
            for layer in range(2):
                if layer:
                    norm(c, "m1", x, None, DT, False, 1e-6, lambda k: c.col("mix3_g", DT + k), pair=xn)
                    with ExitStack() as s:
                        y, rows = pair("y_fox", DT, s), sb("rows", [P, S], s)
                        forget_rows(c, "fr", xn, a["fox_f"], rows, c.col("fox_fb"))
                        attention(c, "fox", xn, a["fox_w"], y, [list(range(i + 1)) for i in range(TT)], 1, forget=rows)
                        project(c, "foxo", a["fox_o"], y, DT, DT, x, residual=x)
                norm(c, f"n{layer}", x, None, DT, False, 1e-6, lambda k: c.col("ffn3_g", layer * DT + k), pair=xn)
                with ExitStack() as s:
                    hidden = pair(f"hidden4{layer}", 16, s)
                    conv_glu_up(c, f"g{layer}u", a[f"g{layer}_up"], xn, hidden, 16,
                                lambda i, t: c.col("ffn3_cw", layer * 48 + i * 16 + t), lambda t: c.col("ffn3_cb", layer * 16 + t))
                    project(c, f"g{layer}d", a[f"g{layer}_down"], hidden, 16, DT, x, residual=x)
        norm(c, "fin", x, x, DT, False, 1e-6, lambda k: c.col("fin3_g", k), sink_d=out_d)


def lay_out(i):
    i = {k: np.asarray(v) for k, v in i.items()}
    a = {}

    def tiles(w):
        k, m = w.shape
        return w.reshape(k // P, P, m // P, P).transpose(2, 1, 0, 3).reshape(m // P, P, k)

    def stack(*ws):
        return np.stack([tiles(w) for w in ws], 2)

    def columns(v):
        return v.reshape(-1, P).T

    def padded_heads(w, heads):
        out = np.zeros((w.shape[0], heads, P), w.dtype)
        out[:, :, 0:64] = w.reshape(w.shape[0], heads, 64)
        return out.reshape(w.shape[0], heads * P)

    def doubled(w):
        w = w.reshape(w.shape[0], 4, 64)
        return np.stack([w] * 2, 2).reshape(w.shape[0], 8 * 64)

    col = {}
    a["table"] = np.concatenate(list(TABLES.values()), 1)
    a["x"] = i["x"][0].T.reshape(DT, P, S).transpose(1, 0, 2)

    for n in ("ln1_g", "ln1_b", "ln2_g", "ln2_b", "ln3_g", "ln3_b"):
        col[n] = columns(i[n][0])
    for n in (1, 2):
        a[f"f{n}_up"] = stack(i[f"ffn{n}_w1"][0], i[f"ffn{n}_w3"][0])
        a[f"f{n}_down"] = tiles(i[f"ffn{n}_w2"][0])
    cuts = np.cumsum([1024, 256, 256, 1024, 1024, 1024, 1024, 1024])
    q, k, v, f, qh, ih, og, ga, gh = np.split(i["w_in"][0], cuts, 1)
    bq, bk, bv, bf, bqh, bih, bog, bga, bgh = np.split(i["b_in"], cuts, 1)
    q = tiles(q)
    a["att_w"] = np.stack([q[0::2], q[1::2], tiles(doubled(k)), tiles(doubled(v))], 2)
    col["att_vb"] = columns(doubled(bv)[0])
    col["att_qb"], col["att_kb"] = columns(bq[0]), columns(doubled(bk)[0])
    col["sinks"] = np.broadcast_to(i["attn_sinks"][0], (P, 16))
    a["hg_w"] = stack(qh, f, ih, og)
    col["hg_vb"] = columns(bih[0])
    col["hg_qb"], col["hg_fb"], col["hg_ogb"] = columns(bqh[0]), columns(bf[0]), columns(bog[0])
    col["hg_lb"] = columns(i["hgrn_lb_logits"].reshape(-1))
    col["hg_ng"] = columns(i["hgrn_norm_g"][0])
    col["gate_b"] = np.concatenate([columns(bga[0]), columns(bgh[0])], 1)
    gates = [tiles(ga), tiles(gh)]
    outs = [tiles(i["w_proj_attn"][0]), tiles(i["w_proj_hgrn"][0])]
    a["mg1_w"] = np.stack([np.concatenate([g, o], 2) for g, o in zip(gates, outs)], 1)
    a["wo1"] = tiles(i["w_out"][0])

    w = i["w_in_2"][0]
    r2, k2, v2, wlo, alo, glo, gq, gk, gv, gf, go, mqk, mv, mi, mf, mo, sz, sx, sb_, sc, sdt, fg = np.split(w, np.cumsum(
        [512, 512, 512, 64, 64, 128, 256, 256, 512, 16, 512, 512, 512, 4, 4, 512, 512, 512, 256, 256, 8]), 1)
    zero = np.zeros((D, 96), w.dtype)
    small = np.concatenate([mi, mf, sdt, gf, zero], 1)
    a["low_w"] = tiles(np.concatenate([small, wlo, alo, glo, np.zeros((D, P), w.dtype)], 1))
    col["mix2_g"] = columns(i["mix_norm_g_2"][0])
    mu = i["rwkv_mu_2"][0]
    col["r_mu"], col["k_mu"], col["v_mu"], col["lora_mu"] = (columns(m) for m in np.split(mu, [512, 1024, 1536]))
    for n, key in (("w0", "rwkv_w0_2"), ("a0", "rwkv_a0_2"), ("k_k", "rwkv_k_k_2"), ("k_a", "rwkv_k_a_2"),
                   ("r_k", "rwkv_r_k_2"), ("gn_g", "rwkv_gn_g_2"), ("gn_b", "rwkv_gn_b_2")):
        col[n] = columns(i[key][0].reshape(-1))
    a["rw_w"] = stack(r2, k2, v2)
    lows = np.zeros((4, P, 3, P), w.dtype)
    lows[:, 0:64, 0, :] = i["rwkv_w_up_2"][0].reshape(64, 4, P).transpose(1, 0, 2)
    lows[:, 64:128, 1, :] = i["rwkv_a_up_2"][0].reshape(64, 4, P).transpose(1, 0, 2)
    lows[:, :, 2, :] = i["rwkv_g_up_2"][0].reshape(P, 4, P).transpose(1, 0, 2)
    a["rw_up"] = lows
    a["gla_w"] = stack(padded_heads(gq, 4), padded_heads(gk, 4), gv, go)
    fup = np.zeros((4, P, P), w.dtype)
    fup[:, 16:32, 0:64] = i["gla_f_up_2"][0].reshape(16, 4, 64).transpose(1, 0, 2)
    a["gla_fup"] = fup
    col["gla_fb"] = columns(padded_heads(i["gla_f_bias_2"], 4)[0])
    col["gla_ng"] = columns(i["gla_norm_g_2"][0])
    a["ml_w"] = stack(padded_heads(mqk[:, 0:256], 4), padded_heads(mqk[:, 256:512], 4), mv, mo)
    cw = i["mlstm_conv_w_2"][0]
    taps = np.stack([padded_heads(cw[:, 0:256], 4).reshape(4, 4, P), padded_heads(cw[:, 256:], 4).reshape(4, 4, P)], 0)
    col["ml_cw"] = taps.transpose(3, 2, 0, 1).reshape(P, 32)
    cb = i["mlstm_conv_b_2"]
    col["ml_cb"] = np.stack([padded_heads(cb[:, 0:256], 4).reshape(4, P), padded_heads(cb[:, 256:], 4).reshape(4, P)], 1) \
        .reshape(8, P).T
    col["ml_ib"] = np.broadcast_to(i["mlstm_i_bias_2"][0], (P, 4))
    col["ml_fb"] = np.broadcast_to(i["mlstm_f_bias_2"][0], (P, 4))
    col["ml_ng"] = columns(i["mlstm_norm_g_2"][0])
    twice = lambda m: np.repeat(m.reshape(m.shape[0], 2, P), 2, 1).reshape(m.shape[0], 4 * P)
    a["sd_w"] = stack(sx, sz, twice(sb_), twice(sc))
    cw, cb = i["ssd_conv_w_2"][0], i["ssd_conv_b_2"]
    col["sd_cwx"] = cw[:, 0:512].reshape(4, 4, P).transpose(2, 1, 0).reshape(P, 16)
    col["sd_cbx"] = columns(cb[0, 0:512])
    bc = np.stack([twice(cw[:, 512:768]).reshape(4, 4, P), twice(cw[:, 768:]).reshape(4, 4, P)], 0)
    col["sd_cwbc"] = bc.transpose(3, 2, 0, 1).reshape(P, 32)
    bc = np.stack([twice(cb[:, 512:768]).reshape(4, P), twice(cb[:, 768:]).reshape(4, P)], 0)
    col["sd_cbbc"] = bc.transpose(2, 1, 0).reshape(P, 8)
    col["sd_dtb"] = np.broadcast_to(i["ssd_dt_bias_2"][0], (P, 8))
    col["sd_alog"] = np.broadcast_to(i["ssd_a_log_2"][0], (P, 8))
    col["sd_d"] = columns(np.repeat(i["ssd_d_2"][0], 64))
    col["sd_ng"] = columns(i["ssd_norm_g_2"][0])
    proj = i["branch_proj_2"][0]
    a["mg2_w"] = np.stack([np.concatenate([tiles(fg[:, n * D:(n + 1) * D]), tiles(proj[n])], 2) for n in range(4)], 1)
    a["wo2"] = tiles(i["w_out_2"][0])
    up = i["ffn_up_2"][0]
    a["f3_up"], a["f3_down"] = stack(up[:, 0:D_FF], up[:, D_FF:]), tiles(i["ffn_down_2"][0])
    col["ffn2_g"], col["fin2_g"] = columns(i["ffn_norm_g_2"][0]), columns(i["final_norm_g_2"])
    col["ffn2_cw"] = columns(i["ffn_conv_w_2"][0].reshape(-1))
    col["ffn2_cb"] = columns(i["ffn_conv_b_2"][0])

    col["mix3_g"], col["ffn3_g"] = columns(i["mix_norm_g_3"].reshape(-1)), columns(i["ffn_norm_g_3"].reshape(-1))
    col["ffn3_cw"] = columns(i["ffn_conv_w_3"].reshape(-1))
    col["ffn3_cb"] = columns(i["ffn_conv_b_3"].reshape(-1))
    col["fin3_g"] = columns(i["final_norm_g_3"])
    w = i["gm_w_in_3"][0]
    a["gm_u"] = tiles(w[:, 0:2048])
    a["gm_v"] = w[:, 2048:].reshape(2, DT // 2, P, 4, S).transpose(3, 2, 0, 1, 4).reshape(4, P, 2, DT // 2 * S)
    col["gm_g"], col["gm_b"] = columns(i["gm_ln_g_3"][0]), columns(i["gm_ln_b_3"][0])
    a["gm_bs"] = np.broadcast_to(i["gm_b_s_3"][0], (P, 8, P))
    a["gm_ws"] = i["gm_w_s_3"][0].transpose(2, 0, 1)
    a["gm_out"] = tiles(i["gm_w_out_3"][0])
    q, k, v, f = np.split(i["fox_w_qkvf_3"][0], [D, 2 * D, 3 * D], 1)
    a["fox_w"] = stack(q, k, v)
    wide = np.zeros((D, P), f.dtype)
    wide[:, 0:16] = f
    a["fox_f"] = tiles(wide)[0]
    fb = np.zeros((P, 1), f.dtype)
    fb[0:16, 0] = i["fox_b_f_3"][0]
    col["fox_fb"] = fb
    a["fox_o"] = tiles(i["fox_w_o_3"][0])
    for n in range(2):
        a[f"g{n}_up"] = stack(i["ffn_w_gate_3"][n], i["ffn_w_up_3"][n])
        a[f"g{n}_down"] = tiles(i["ffn_w_down_3"][n])
    for n, width in COLUMNS:
        assert col[n].shape == (P, width), (n, col[n].shape)
    a["column"] = np.concatenate([col[n] for n, _ in COLUMNS], 1)
    return {k: np.ascontiguousarray(v) for k, v in a.items()}


def kernel(**inputs):
    import concourse.bacc as _bacc
    from concourse.bass_utils import run_bass_kernel_spmd as _run

    nc = _bacc.Bacc("TRN2", target_bir_lowering=False, num_devices=1)
    arrays = {f"in_{name}": array for name, array in lay_out(inputs).items()}
    args = {name[3:]: nc.dram_tensor(name, array.shape, F32, kind="ExternalInput").ap() for name, array in arrays.items()}
    out = nc.dram_tensor("out", (P, DT, S), F32, kind="ExternalOutput").ap()
    build(nc, args, out)
    r = _run(nc, [arrays], core_ids=[0])
    return np.asarray(r.results[0]["out"]).transpose(2, 1, 0).reshape(1, S, D)
```
